# Optimizing a Trainium2 kernel written in Bass

```python
import math
import jax
import jax.numpy as jnp
from jax import lax
import numpy as np

D_MODEL = 2048
BATCH = 1
SEQ = 256
DEPTH = 2
DEC_BATCH = 8
DEC_SEQ = 4
PAST_LEN = 2048
PAGE_SIZE = 128

SSM_WIDTH = D_MODEL // 2
ATTN_WIDTH = D_MODEL - SSM_WIDTH
SSM_CH = 16
SSM_GROUPS = SSM_WIDTH // SSM_CH
SSM_STATE = 64
DT_MIN = 1e-3
DT_MAX = 1e-1
HEAD_DIM = 128
N_HEADS = ATTN_WIDTH // HEAD_DIM
N_KV_HEADS = 2
GQA = N_HEADS // N_KV_HEADS
KV_WIDTH = N_KV_HEADS * HEAD_DIM
N_BRANCH = 3
CMP_LEN = 32
CMP_STRIDE = 16
CMP_HIDDEN = HEAD_DIM
SEL_LEN = 64
N_SEL = 16
WINDOW = 512
WIN_QBLK = 128
SEL_QBLK = 64
FORCED_SCORE = 1e4
D_FF = -(-8 * D_MODEL // (3 * 256)) * 256
NORM_EPS = 1e-6
IN_SPLITS = (SSM_WIDTH,) + tuple(SSM_WIDTH + ATTN_WIDTH + i * KV_WIDTH for i in range(7))
IN_WIDTH = SSM_WIDTH + ATTN_WIDTH + 6 * KV_WIDTH + N_HEADS * N_BRANCH

kernel_name = 'hymba_s5_nsa_decode_step'

def rmsnorm(x, g):
    xf = x.astype(jnp.float32)
    y = xf * lax.rsqrt(jnp.mean(xf * xf, axis=-1, keepdims=True) + NORM_EPS)
    return (y * g.astype(jnp.float32)).astype(x.dtype)

def alibi_slopes():
    h = jnp.arange(1, N_HEADS + 1, dtype=jnp.float32)
    return (2.0 ** (-8.0 * h / N_HEADS)).reshape(N_KV_HEADS, GQA)

def masked_softmax(s, valid):
    s = jnp.where(valid, s.astype(jnp.float32), -jnp.inf)
    m = jnp.max(s, axis=-1, keepdims=True)
    m = jnp.where(jnp.isfinite(m), m, 0.0)
    e = jnp.exp(s - m)
    den = jnp.sum(e, axis=-1, keepdims=True)
    return e / jnp.maximum(den, jnp.finfo(jnp.float32).tiny)

def dense_gqa(q, k, v, dist, valid):
    s = jnp.einsum('...tkgd,...skd->...kgts', q, k).astype(jnp.float32) * HEAD_DIM ** -0.5
    s = s - alibi_slopes()[:, :, None, None] * dist[..., None, None, :, :]
    p = masked_softmax(s, valid[..., None, None, :, :])
    o = jnp.einsum('...kgts,...skd->...tkgd', p.astype(v.dtype), v)
    return o, p

def _linear_combine(e1, e2):
    a1, b1 = e1
    a2, b2 = e2
    return a2 * a1, a2 * b1 + b2

def s5_mixer(u, h0, p):
    bsz, t_len, _ = u.shape
    uf = u.astype(jnp.float32).reshape(bsz, t_len, SSM_GROUPS, SSM_CH)
    lam = lax.complex(p['ssm_a_re'].astype(jnp.float32), p['ssm_a_im'].astype(jnp.float32))
    dt = jnp.exp(p['ssm_log_dt'].astype(jnp.float32))[:, None]
    lam_bar = jnp.exp(lam * dt)
    b = lax.complex(p['ssm_b_re'].astype(jnp.float32), p['ssm_b_im'].astype(jnp.float32))
    b_bar = ((lam_bar - 1.0) / lam)[..., None] * b
    bu = lax.complex(jnp.einsum('btgp,gnp->btgn', uf, b_bar.real),
                     jnp.einsum('btgp,gnp->btgn', uf, b_bar.imag))
    a = jnp.broadcast_to(lam_bar, bu.shape)
    a_cum, h = lax.associative_scan(_linear_combine, (a, bu), axis=1)
    h = h + a_cum * lax.complex(h0[..., 0].astype(jnp.float32), h0[..., 1].astype(jnp.float32))[:, None]
    y = (jnp.einsum('gpn,btgn->btgp', p['ssm_c_re'].astype(jnp.float32), h.real)
         - jnp.einsum('gpn,btgn->btgp', p['ssm_c_im'].astype(jnp.float32), h.imag))
    y = (y + p['ssm_d'].astype(jnp.float32) * uf).reshape(bsz, t_len, SSM_WIDTH)
    z = jax.nn.gelu(y)
    z = z * jax.nn.sigmoid(z @ p['ssm_w_glu'].astype(jnp.float32))
    h_last = jnp.stack([h[:, -1].real, h[:, -1].imag], axis=-1)
    return z.astype(u.dtype), h_last.astype(h0.dtype)

def project(xn, p):
    bsz, t_len, _ = xn.shape
    u, q, kc, vc, ks, vs, kw, vw, g = jnp.split(xn @ p['w_in'], IN_SPLITS, axis=-1)
    q = rmsnorm(q.reshape(bsz, t_len, N_KV_HEADS, GQA, HEAD_DIM), p['q_norm'])

    def heads(t):
        return t.reshape(bsz, t_len, N_KV_HEADS, HEAD_DIM)

    kv_cmp = jnp.stack([heads(kc), heads(vc)], axis=3)
    kv_slc = jnp.stack([rmsnorm(heads(ks), p['k_norm_slc']), heads(vs)], axis=3)
    kv_win = jnp.stack([rmsnorm(heads(kw), p['k_norm_win']), heads(vw)], axis=3)
    gates = jax.nn.sigmoid(g.astype(jnp.float32)).reshape(bsz, t_len, N_KV_HEADS, GQA, N_BRANCH)
    return u, q, kv_cmp, kv_slc, kv_win, gates

def compress(rows, w1, b1, w2):
    bsz, length = rows.shape[:2]
    n_chunk = length // CMP_STRIDE
    c = rows[:, :n_chunk * CMP_STRIDE].reshape(bsz, n_chunk, CMP_STRIDE, N_KV_HEADS, HEAD_DIM)
    c = c.transpose(0, 1, 3, 2, 4).reshape(bsz, n_chunk, N_KV_HEADS, CMP_STRIDE * HEAD_DIM)
    half = CMP_STRIDE * HEAD_DIM
    h = c[:, :-1] @ w1[:half] + c[:, 1:] @ w1[half:] + b1
    return jax.nn.gelu(h) @ w2

def compressed_kv(kv_rows, p):
    ck = rmsnorm(compress(kv_rows[..., 0, :], p['cmp_w1_k'], p['cmp_b1_k'], p['cmp_w2_k']), p['k_norm_cmp'])
    cv = compress(kv_rows[..., 1, :], p['cmp_w1_v'], p['cmp_b1_v'], p['cmp_w2_v'])
    return ck, cv

def cmp_attend(q, ck, cv, q_pos):
    nc = ck.shape[1]
    start = jnp.arange(nc) * CMP_STRIDE
    valid = (start + CMP_LEN - 1)[None, :] <= q_pos[:, None]
    dist = (q_pos[:, None] - start[None, :]).astype(jnp.float32) - (CMP_LEN - 1) / 2
    o, prob = dense_gqa(q, ck, cv, dist, valid)
    return o, prob.sum(axis=2)

def select_blocks(p_cmp, q_pos, n_blocks):
    nc = p_cmp.shape[-1]
    per = SEL_LEN // CMP_STRIDE
    ci = jnp.arange(nc)
    j = jnp.arange(n_blocks)
    overlap = ((ci // per)[None, :] == j[:, None]).astype(jnp.float32) + \
        (((ci + 1) // per)[None, :] == j[:, None]).astype(jnp.float32)
    score = jnp.einsum('bktc,jc->bktj', p_cmp, overlap)
    qb = q_pos // SEL_LEN
    forced = (j[None, :] == 0) | (j[None, :] == qb[:, None]) | (j[None, :] == qb[:, None] - 1)
    causal = j[None, :] * SEL_LEN <= q_pos[:, None]
    score = jnp.where(forced, FORCED_SCORE, jnp.where(causal, score, -1.0))
    _, idx = lax.top_k(score, min(N_SEL, n_blocks))
    return idx

def sel_attend(q, g, idx, q_pos):
    bsz, _, t_len, nsel = idx.shape
    nk = nsel * SEL_LEN
    g = g.reshape(bsz, N_KV_HEADS, t_len, nk, 2, HEAD_DIM)
    kpos = (idx[..., None] * SEL_LEN + jnp.arange(SEL_LEN)).reshape(bsz, N_KV_HEADS, t_len, nk)
    dist = q_pos[:, None] - kpos
    s = jnp.einsum('btkgd,bktsd->bkgts', q, g[..., 0, :]).astype(jnp.float32) * HEAD_DIM ** -0.5
    s = s - alibi_slopes()[None, :, :, None, None] * dist.astype(jnp.float32)[:, :, None]
    p = masked_softmax(s, (dist >= 0)[:, :, None])
    return jnp.einsum('bkgts,bktsd->btkgd', p.astype(g.dtype), g[..., 1, :])

def sel_prompt(q, kv_slc, idx):
    bsz, s_len = q.shape[:2]
    nq = s_len // SEL_QBLK
    kvb = kv_slc.reshape(bsz, s_len // SEL_LEN, SEL_LEN, N_KV_HEADS, 2, HEAD_DIM).transpose(0, 3, 1, 2, 4, 5)
    bi = jnp.arange(bsz)[:, None, None, None]
    ki = jnp.arange(N_KV_HEADS)[None, :, None, None]
    qc = q.reshape(bsz, nq, SEL_QBLK, N_KV_HEADS, GQA, HEAD_DIM).swapaxes(0, 1)
    ic = idx.reshape(bsz, N_KV_HEADS, nq, SEL_QBLK, -1).transpose(2, 0, 1, 3, 4)
    pc = jnp.arange(s_len).reshape(nq, SEL_QBLK)

    def block(args):
        qb, ib, pb = args
        return sel_attend(qb, kvb[bi, ki, ib], ib, pb)

    out = lax.map(block, (qc, ic, pc))
    return out.swapaxes(0, 1).reshape(bsz, s_len, N_KV_HEADS, GQA, HEAD_DIM)

def gather_selected_sample(cache_slc_kv, layer, page_table, new_kv, idx):
    bsz, _, t_len, _ = idx.shape
    past_blocks = PAST_LEN // SEL_LEN
    per_page = PAGE_SIZE // SEL_LEN
    bi = jnp.arange(bsz)[:, None, None, None]
    ki = jnp.arange(N_KV_HEADS)[None, :, None, None]
    jp = jnp.minimum(idx, past_blocks - 1)
    phys = page_table[bi, jp // per_page]
    rows = (jp % per_page)[..., None] * SEL_LEN + jnp.arange(SEL_LEN)
    g_past = cache_slc_kv[layer, phys[..., None], rows, ki[..., None]]
    nb_new = -(-t_len // SEL_LEN)
    newb = jnp.pad(new_kv, ((0, 0), (0, nb_new * SEL_LEN - t_len), (0, 0), (0, 0), (0, 0)))
    newb = newb.reshape(bsz, nb_new, SEL_LEN, N_KV_HEADS, 2, HEAD_DIM)
    jn = jnp.clip(idx - past_blocks, 0, nb_new - 1)
    g_new = newb[bi[..., None], jn[..., None], jnp.arange(SEL_LEN), ki[..., None]]
    return jnp.where((idx < past_blocks)[..., None, None, None], g_past, g_new.astype(g_past.dtype))

def win_prompt(q, kv_win):
    bsz, s_len = q.shape[:2]
    nb = s_len // WIN_QBLK
    wb = WINDOW // WIN_QBLK
    kvp = jnp.pad(kv_win, ((0, 0), (WINDOW, 0), (0, 0), (0, 0), (0, 0)))
    kvp = kvp.reshape(bsz, nb + wb, WIN_QBLK, N_KV_HEADS, 2, HEAD_DIM)
    band = jnp.concatenate([kvp[:, i:i + nb] for i in range(wb + 1)], axis=2)
    qpos = jnp.arange(s_len).reshape(nb, WIN_QBLK)
    kpos = (jnp.arange(nb) * WIN_QBLK - WINDOW)[:, None] + jnp.arange((wb + 1) * WIN_QBLK)
    d = qpos[:, :, None] - kpos[:, None, :]
    valid = (d >= 0) & (d < WINDOW) & (kpos[:, None, :] >= 0)
    qb = q.reshape(bsz, nb, WIN_QBLK, N_KV_HEADS, GQA, HEAD_DIM)
    o, _ = dense_gqa(qb, band[..., 0, :], band[..., 1, :], d.astype(jnp.float32), valid)
    return o.reshape(bsz, s_len, N_KV_HEADS, GQA, HEAD_DIM)

def mix_output(ssm_y, gates, o_cmp, o_slc, o_win, p):
    bsz, t_len = ssm_y.shape[:2]
    attn = gates[..., 0:1] * o_cmp + gates[..., 1:2] * o_slc + gates[..., 2:3] * o_win
    attn = attn.reshape(bsz, t_len, ATTN_WIDTH).astype(ssm_y.dtype)
    h = jnp.concatenate([rmsnorm(ssm_y, p['norm_ssm_out']), rmsnorm(attn, p['norm_attn_out'])], axis=-1)
    return h @ p['w_out']

def swiglu_ffn(x, p):
    h = rmsnorm(x, p['norm_ffn'])
    return (jax.nn.silu(h @ p['w_ffn_gate']) * (h @ p['w_ffn_up'])) @ p['w_ffn_down']

def prompt_mixer(x, p):
    bsz, s_len, _ = x.shape
    u, q, kv_cmp, kv_slc, kv_win, gates = project(rmsnorm(x, p['norm_mix']), p)
    h0 = jnp.zeros((bsz, SSM_GROUPS, SSM_STATE, 2), jnp.float32)
    ssm_y, h_last = s5_mixer(u, h0, p)
    pos = jnp.arange(s_len)
    ck, cv = compressed_kv(kv_cmp, p)
    o_cmp, p_cmp = cmp_attend(q, ck, cv, pos)
    idx = select_blocks(p_cmp, pos, s_len // SEL_LEN)
    o_slc = sel_prompt(q, kv_slc, idx)
    o_win = win_prompt(q, kv_win)
    y = mix_output(ssm_y, gates, o_cmp, o_slc, o_win, p)
    wbuf = min(WINDOW, PAST_LEN)
    win_state = jnp.pad(kv_win, ((0, 0), (max(wbuf - s_len, 0), 0), (0, 0), (0, 0), (0, 0)))[:, -wbuf:]
    return y, kv_cmp, kv_slc, win_state, h_last

def sample_mixer(x, p, cache_cmp_kv, cache_slc_kv, layer, page_table, win_buf, h0):
    bsz, t_len, _ = x.shape
    u, q, kv_cmp, kv_slc, kv_win, gates = project(rmsnorm(x, p['norm_mix']), p)
    ssm_y, h_last = s5_mixer(u, h0, p)
    pos = PAST_LEN + jnp.arange(t_len)
    past_cmp = cache_cmp_kv[layer, page_table].reshape(bsz, PAST_LEN, N_KV_HEADS, 2, HEAD_DIM)
    ck, cv = compressed_kv(jnp.concatenate([past_cmp, kv_cmp.astype(past_cmp.dtype)], axis=1), p)
    o_cmp, p_cmp = cmp_attend(q, ck, cv, pos)
    idx = select_blocks(p_cmp, pos, -(-(PAST_LEN + t_len) // SEL_LEN))
    o_slc = sel_attend(q, gather_selected_sample(cache_slc_kv, layer, page_table, kv_slc, idx), idx, pos)
    wbuf = win_buf.shape[1]
    kv_all = jnp.concatenate([win_buf, kv_win.astype(win_buf.dtype)], axis=1)
    kpos = PAST_LEN - wbuf + jnp.arange(wbuf + t_len)
    d = pos[:, None] - kpos[None, :]
    o_win, _ = dense_gqa(q, kv_all[..., 0, :], kv_all[..., 1, :], d.astype(jnp.float32), (d >= 0) & (d < WINDOW))
    y = mix_output(ssm_y, gates, o_cmp, o_slc, o_win, p)
    return y, kv_cmp, kv_slc, kv_all[:, -wbuf:], h_last

def setup_inputs(seed: int = 0) -> dict:
    key = jax.random.key(seed)
    ks = iter(jax.random.split(key, 48))

    def nrm(shape, scale=1.0):
        return jax.random.normal(next(ks), shape, jnp.float32) * scale

    def gain(n):
        return 1.0 + 0.02 * nrm((DEPTH, n))

    n_pages = PAST_LEN // PAGE_SIZE
    n_used = DEC_BATCH * n_pages
    n_pool = n_used + n_used // 4
    wbuf = min(WINDOW, PAST_LEN)
    n_idx = jnp.arange(SSM_STATE, dtype=jnp.float32)
    cache_shape = (DEPTH, n_pool, PAGE_SIZE, N_KV_HEADS, 2, HEAD_DIM)
    return {
        'x_prompt': nrm((BATCH, SEQ, D_MODEL)),
        'x_sample': nrm((DEC_BATCH, DEC_SEQ, D_MODEL)),
        'cache_cmp_kv': nrm(cache_shape),
        'cache_slc_kv': nrm(cache_shape),
        'state_win_kv': nrm((DEPTH, DEC_BATCH, wbuf, N_KV_HEADS, 2, HEAD_DIM)),
        'state_ssm': nrm((DEPTH, DEC_BATCH, SSM_GROUPS, SSM_STATE, 2), 0.1),
        'page_table': jax.random.permutation(next(ks), n_pool)[:n_used].reshape(DEC_BATCH, n_pages).astype(jnp.int32),
        'norm_mix': gain(D_MODEL),
        'w_in': nrm((DEPTH, D_MODEL, IN_WIDTH), D_MODEL ** -0.5),
        'ssm_a_re': -0.5 + 0.01 * nrm((DEPTH, SSM_GROUPS, SSM_STATE)),
        'ssm_a_im': math.pi * n_idx + 0.01 * nrm((DEPTH, SSM_GROUPS, SSM_STATE)),
        'ssm_log_dt': jax.random.uniform(next(ks), (DEPTH, SSM_GROUPS), jnp.float32, math.log(DT_MIN), math.log(DT_MAX)),
        'ssm_b_re': nrm((DEPTH, SSM_GROUPS, SSM_STATE, SSM_CH), (2 * SSM_CH) ** -0.5),
        'ssm_b_im': nrm((DEPTH, SSM_GROUPS, SSM_STATE, SSM_CH), (2 * SSM_CH) ** -0.5),
        'ssm_c_re': nrm((DEPTH, SSM_GROUPS, SSM_CH, SSM_STATE), SSM_STATE ** -0.5),
        'ssm_c_im': nrm((DEPTH, SSM_GROUPS, SSM_CH, SSM_STATE), SSM_STATE ** -0.5),
        'ssm_d': nrm((DEPTH, SSM_GROUPS, SSM_CH)),
        'ssm_w_glu': nrm((DEPTH, SSM_WIDTH, SSM_WIDTH), SSM_WIDTH ** -0.5),
        'q_norm': gain(HEAD_DIM),
        'k_norm_cmp': gain(HEAD_DIM),
        'k_norm_slc': gain(HEAD_DIM),
        'k_norm_win': gain(HEAD_DIM),
        'cmp_w1_k': nrm((DEPTH, CMP_LEN * HEAD_DIM, CMP_HIDDEN), (CMP_LEN * HEAD_DIM) ** -0.5),
        'cmp_b1_k': nrm((DEPTH, CMP_HIDDEN), 0.02),
        'cmp_w2_k': nrm((DEPTH, CMP_HIDDEN, HEAD_DIM), CMP_HIDDEN ** -0.5),
        'cmp_w1_v': nrm((DEPTH, CMP_LEN * HEAD_DIM, CMP_HIDDEN), (CMP_LEN * HEAD_DIM) ** -0.5),
        'cmp_b1_v': nrm((DEPTH, CMP_HIDDEN), 0.02),
        'cmp_w2_v': nrm((DEPTH, CMP_HIDDEN, HEAD_DIM), CMP_HIDDEN ** -0.5),
        'norm_ssm_out': gain(SSM_WIDTH),
        'norm_attn_out': gain(ATTN_WIDTH),
        'w_out': nrm((DEPTH, D_MODEL, D_MODEL), D_MODEL ** -0.5),
        'norm_ffn': gain(D_MODEL),
        'w_ffn_gate': nrm((DEPTH, D_MODEL, D_FF), D_MODEL ** -0.5),
        'w_ffn_up': nrm((DEPTH, D_MODEL, D_FF), D_MODEL ** -0.5),
        'w_ffn_down': nrm((DEPTH, D_FF, D_MODEL), D_FF ** -0.5),
    }

def reference(x_prompt, x_sample, cache_cmp_kv, cache_slc_kv, state_win_kv, state_ssm, page_table,
              norm_mix, w_in, ssm_a_re, ssm_a_im, ssm_log_dt, ssm_b_re, ssm_b_im, ssm_c_re, ssm_c_im,
              ssm_d, ssm_w_glu, q_norm, k_norm_cmp, k_norm_slc, k_norm_win,
              cmp_w1_k, cmp_b1_k, cmp_w2_k, cmp_w1_v, cmp_b1_v, cmp_w2_v,
              norm_ssm_out, norm_attn_out, w_out, norm_ffn, w_ffn_gate, w_ffn_up, w_ffn_down):
    y_prompt, y_sample = x_prompt, x_sample
    cmp_p, slc_p, win_p, ssm_p = [], [], [], []
    cmp_s, slc_s, win_s, ssm_s = [], [], [], []
    for l in range(DEPTH):
        p = {
            'norm_mix': norm_mix[l], 'w_in': w_in[l],
            'ssm_a_re': ssm_a_re[l], 'ssm_a_im': ssm_a_im[l], 'ssm_log_dt': ssm_log_dt[l],
            'ssm_b_re': ssm_b_re[l], 'ssm_b_im': ssm_b_im[l], 'ssm_c_re': ssm_c_re[l], 'ssm_c_im': ssm_c_im[l],
            'ssm_d': ssm_d[l], 'ssm_w_glu': ssm_w_glu[l],
            'q_norm': q_norm[l], 'k_norm_cmp': k_norm_cmp[l], 'k_norm_slc': k_norm_slc[l], 'k_norm_win': k_norm_win[l],
            'cmp_w1_k': cmp_w1_k[l], 'cmp_b1_k': cmp_b1_k[l], 'cmp_w2_k': cmp_w2_k[l],
            'cmp_w1_v': cmp_w1_v[l], 'cmp_b1_v': cmp_b1_v[l], 'cmp_w2_v': cmp_w2_v[l],
            'norm_ssm_out': norm_ssm_out[l], 'norm_attn_out': norm_attn_out[l], 'w_out': w_out[l],
            'norm_ffn': norm_ffn[l], 'w_ffn_gate': w_ffn_gate[l], 'w_ffn_up': w_ffn_up[l], 'w_ffn_down': w_ffn_down[l],
        }
        m, kc, ksl, kw, hs = prompt_mixer(y_prompt, p)
        y_prompt = y_prompt + m
        y_prompt = y_prompt + swiglu_ffn(y_prompt, p)
        cmp_p.append(kc)
        slc_p.append(ksl)
        win_p.append(kw)
        ssm_p.append(hs)
        m, kc, ksl, kw, hs = sample_mixer(y_sample, p, cache_cmp_kv, cache_slc_kv, l, page_table,
                                          state_win_kv[l], state_ssm[l])
        y_sample = y_sample + m
        y_sample = y_sample + swiglu_ffn(y_sample, p)
        cmp_s.append(kc)
        slc_s.append(ksl)
        win_s.append(kw)
        ssm_s.append(hs)
    new_cmp_kv_prompt = jnp.stack(cmp_p)
    new_slc_kv_prompt = jnp.stack(slc_p)
    new_win_kv_prompt = jnp.stack(win_p)
    new_ssm_prompt = jnp.stack(ssm_p)
    new_cmp_kv_sample = jnp.stack(cmp_s)
    new_slc_kv_sample = jnp.stack(slc_s)
    new_win_kv_sample = jnp.stack(win_s)
    new_ssm_sample = jnp.stack(ssm_s)
    return (y_prompt, y_sample, new_cmp_kv_prompt, new_slc_kv_prompt, new_win_kv_prompt, new_ssm_prompt,
            new_cmp_kv_sample, new_slc_kv_sample, new_win_kv_sample, new_ssm_sample)


_drawn_inputs = setup_inputs


def setup_inputs(seed=0):
    import zlib

    import numpy as np

    out = dict(_drawn_inputs(seed))
    spreads = {}
    factors = {'ssm_a_re': 3.994,
     'q_norm': 7.546,
     'k_norm_cmp': 8.0,
     'k_norm_slc': 3.993,
     'k_norm_win': 4.013,
     'cmp_b1_k': 8.0,
     'cmp_b1_v': 4.465,
     'norm_ssm_out': 3.702,
     'norm_attn_out': 4.012,
     'norm_ffn': 3.76}
    for name, (base, spread) in spreads.items():
        noise = np.random.default_rng([zlib.crc32(name.encode()), seed]).standard_normal(out[name].shape)
        drawn = base * np.exp(spread * noise) if base else spread * noise
        out[name] = jnp.asarray(drawn.astype(out[name].dtype))
    for name, factor in factors.items():
        out[name] = (out[name] * factor).astype(out[name].dtype)
    return out
```

```python
from contextlib import ExitStack

import numpy as np

import concourse.bass as bass
from concourse import mybir

F32 = mybir.dt.float32
I32 = mybir.dt.int32
ALU = mybir.AluOpType
ACT = mybir.ActivationFunctionType
AXX = mybir.AxisListType.X

P = 128
L = 2
D_MODEL, SEQ, NB, NT = 2048, 256, 8, 4
SMP = NB * NT
TOK = SEQ + SMP
PAST, PAGE, NPG, WIN = 2048, 128, 16, 512
KC = D_MODEL // P
D_FF = 5632
MF = D_FF // 256
NQ, NKV, GQA, HD = 8, 2, 4, 128
SC = 8
NCMP, NCMP_P = 127, 15
NBLK, NSEL, SEL = 33, 16, 64
CH = 16
NPAIR, QP = 32, 8
EPS = 1e-6
SCALE = HD ** -0.5
TINY = 1.1754943508222875e-38
MASKED = -1e30
FORCED = 1e4
STEP = 2 * TOK

T_Q, T_KC, T_VC, T_KS, T_VS, T_KW, T_VW, NTILE = 8, 16, 18, 20, 22, 24, 26, 28
C_MIX, C_FFN, C_NSSM, C_NATT, C_D, C_QN, C_KS, C_KW, C_KC, C_B1, NPAR = 0, 16, 32, 40, 48, 56, 57, 58, 59, 60, 62
K_ID, K_ONE, K_DS, K_DW, K_DC, K_DCP, K_D1, K_SLR, K_SLH, K_G, K_FRC = range(11)


def constant_table():
    r = np.arange(P)
    t, s = r[:, None], np.arange(SMP)[None, :]
    b, step, g = (r % 32) // NT, r % NT, r // 32
    big = -MASKED
    fresh = np.where((s // NT == b[:, None]) & (s % NT <= step[:, None]), step[:, None] - s % NT, big)
    past = PAST + step[:, None] - np.arange(PAST)[None, :]
    j = np.arange(WIN)[None, :]
    win = np.where(j > step[:, None], WIN + step[:, None] - j, big)
    c = np.arange(NCMP)[None, :]
    cmp_s = PAST + step[:, None] - 16 * c - 15.5
    cp = np.arange(NCMP_P)[None, :]
    cmp_p = [np.where(16 * cp + 31 <= t + 128 * n, t + 128 * n - 16 * cp - 15.5, big) for n in range(2)]
    causal = np.where(P + t - np.arange(SEQ)[None, :] >= 0, P + t - np.arange(SEQ)[None, :], big)
    slope = -(2.0 ** -np.arange(1, NQ + 1))
    rows = np.stack([slope[g], slope[4 + g]], 1)
    blk = np.arange(NBLK)
    force = np.where((blk == 0) | (blk >= 31), FORCED, 0.0)
    parts = [np.eye(P), np.ones((P, P)), np.concatenate([past, fresh], 1), np.concatenate([win, fresh], 1),
             cmp_s, np.concatenate(cmp_p, 1), causal, rows, np.tile(slope, (P, 1)),
             (r[:, None] % 32 == np.arange(32)[None, :]) * 1.0, np.tile(force, (P, 1))]
    at = np.cumsum([0] + [x.shape[1] for x in parts])
    return np.concatenate(parts, 1).astype(np.float32), [int(a) for a in at]


def tie_table():
    i = np.arange(NBLK)
    return np.tile((i[None, :] < i[:, None]).reshape(1, -1), (64, 1)).astype(np.float32)



SEMS = """consts_in x_in pages_in zero_set zero_out
params_in ssm_in gate_w_in w2_in slot0_full slot1_full slot0_used slot1_used
mix_sq mix_stat mix_var mix_root mix_normed
lam_dt lam_xr lam_mag lam_half lam_sin bbar_ready bbar_turned bbar_evac c_slot bu_done bu_evac scan_done
state_kept y_done y_evac z_ready proj_evac gates_done gates_sig states_out
gated_step glu_done glu_sig glu_evac
qk_sq qk_stat qk_var qk_root qk_normed kv_out vt_done vr_ready qgain
cache0_full cache1_full cache0_used cache1_used conv_done conv_evac hid_pre hid_ready w2_done ck_evac
ckn_sq ckn_stat ckn_var ckn_root ck_normed
q_copied ps_done ps_evac ps_max p_exp p_ready pt_done pt_evac po_done po_evac
qpad_ready cs_done cs_ready c_max c_exp c_prob gsum_done tie_in ranked gates_rows
kring0_full kring1_full kring2_full kring3_full kring_free kgroup_done kgroup_evac fresh_done fresh_evac
sw_max sw_exp sw_ready st_done st_evac
vring0_full vring1_full vring2_full vring3_full vwin_full vring_free so_done so_evac
sn_sq sn_stat sn_var sn_root sn_normed an_sq an_stat an_var an_root an_normed
out_step out_evac fn_sq fn_stat fn_var fn_root fn_normed
gu_done silu_ready gu_evac down_done down_evac win_copied x_out y_out""".split()


def build(nc, T):
    _, at = constant_table()
    stack = ExitStack()
    handles = [nc.alloc_semaphore(n) for n in SEMS]
    assert [h.num for h in handles] == list(range(handles[0].num, handles[0].num + len(SEMS)))
    S = dict(zip(SEMS, handles))

    def sb(name, shape, dt=F32):
        return stack.enter_context(nc.sbuf_tensor(name, shape, dt))

    CT = sb("consts", [P, at[-1]])

    def const(i):
        return CT[:, at[i]:at[i + 1]]
    ident, ones = const(K_ID), const(K_ONE)
    XT = sb("residual", [P, KC, TOK])
    WR = sb("weight_slots", [P, 2, 16, 256])
    PJ = sb("projected", [P, NTILE, TOK])
    HC = sb("normed", [P, KC, TOK])
    ZB = sb("ssm_out", [P, SC, TOK])
    PR = sb("params", [P, NPAR])
    W2 = sb("cmp_w2", [P, 2, HD])
    SQ = sb("squares", [P, 2, TOK])
    NV = sb("norm_var", [P, 2, TOK])
    NR = sb("norm_rstd", [P, 2, TOK])
    GT = sb("gates_t", [24, TOK])
    GR = sb("gates_rows", [P, 3, 24])
    GS = sb("gates_sample", [P, NKV, 3])
    PG = sb("page_numbers", [1, NB * NPG], I32)
    SM = sb("smalls", [P, 32])
    VRF = sb("v_rows", [P, 3 * 2 * 2 * HD])
    VR = VRF[:, :].rearrange("p (t b h d) -> p t b h d", t=3, b=2, h=2)
    WG = VRF[:, 0:KC * 24].rearrange("p (k x) -> p k x", k=KC)
    ARENA = 17800
    AR = sb("arena", [P, ARENA])
    PS = [stack.enter_context(nc.psum_tensor(f"banks{i}", [P, 2, 512], F32)) for i in range(4)]

    def bank(i):
        return PS[i // 2][:, i % 2, :]

    def carve(sizes):
        out, o = [], 0
        for n in sizes:
            out.append(AR[:, o:o + n])
            o += n
        assert o <= ARENA, o
        return out

    s_hs, s_bn, s_cb, s_bbn, s_bbs, s_cbs, s_t1, s_t2, s_pwr, s_pwi, s_h0, s_hl, s_ca, s_c1, s_c2, s_lam = carve(
        [QP * 2 * TOK, 2048, 2048, 512, 512, 512, 1920, 1920, 512, 512, 512, 576, 256, 256, 256, 26 * 32])
    HS = s_hs.rearrange("p (j r t) -> p j r t", j=QP, r=2)
    BN = s_bn.rearrange("p (r j x) -> p r j x", r=2, j=NPAIR)
    CB = s_cb.rearrange("p (j r x) -> p j r x", j=NPAIR, r=2)
    BBN = s_bbn.rearrange("p (r j x) -> p r j x", r=2, j=QP)
    BBS = s_bbs.rearrange("p (r t x) -> p r t x", r=2, t=2)
    CBS = s_cbs.rearrange("p (j r x) -> p j r x", j=QP, r=2)
    PWR = s_pwr.rearrange("p (j i) -> p j i", j=NPAIR)
    PWI = s_pwi.rearrange("p (j i) -> p j i", j=NPAIR)
    H0 = s_h0.rearrange("p (j r b) -> p j r b", j=NPAIR, r=2)
    HL = s_hl.rearrange("p (j r b) -> p j r b", j=NPAIR, r=2)
    CA = s_ca.rearrange("p (j r c) -> p j r c", j=QP, r=2)

    def lam(i, n=1):
        return s_lam[:, 32 * i:32 * (i + n)]
    c_t0, c_t1, c_hid, c_hb = carve([8192, 8192, 508, 256])
    CTB = [x.rearrange("p (g h k i c) -> p g h k i c", g=NPG, h=2, k=2, i=16) for x in (c_t0, c_t1)]
    HID = [c_hid[:, 254 * i:254 * i + 254] for i in range(2)]
    ubuf = PJ[:, 0:8, :].rearrange("p a b -> p (a b)")
    zbuf = ZB[:, :, :].rearrange("p a b -> p (a b)")
    CK = ubuf[:, 0:NB * 2 * NCMP].rearrange("p (b h c) -> p b h c", b=NB, h=2)
    CKP = ubuf[:, 2032:2062].rearrange("p (h c) -> p h c", h=2)
    CV = zbuf[:, 0:2048].rearrange("p (b h d) -> p b h d", b=NB, h=2)
    CVP = zbuf[:, 2048:2304].rearrange("p (h d) -> p h d", h=2)
    p_s, p_pt, p_qs = carve([2 * 3 * 256, 2 * 5 * 128, 256])
    SPR = p_s.rearrange("p (t b s) -> p t b s", t=2, b=3)
    PTP = p_pt.rearrange("p (t n s) -> p t n s", t=2, n=5)
    QS = p_qs.rearrange("p (t s) -> p t s", t=2)
    NS, NW = PAST + SMP, WIN + SMP
    a_s, a_w, a_c, a_ring, a_qp, a_qa, a_pt = carve([2 * NS, 2 * NW, 2 * NCMP, 4096, 2048, 256, 2 * 23 * 128])
    SS = a_s.rearrange("p (k s) -> p k s", k=2)
    SW = a_w.rearrange("p (k s) -> p k s", k=2)
    SCM = a_c.rearrange("p (k s) -> p k s", k=2)
    KR = [a_ring[:, 1024 * n:1024 * n + 1024].rearrange("p (h s) -> p h s", h=2) for n in range(4)]
    VG = [a_ring[:, 1024 * n:1024 * n + 1024].rearrange("p (g h d) -> p g h d", g=4, h=2) for n in range(4)]
    VW = a_qp[:, 0:1024].rearrange("p (g h d) -> p g h d", g=4, h=2)
    QPF = a_qp
    QPD = a_qp.rearrange("p (k b r) -> p k b r", k=2, b=NB)
    QA = a_qa.rearrange("p (k r) -> p k r", k=2)
    PTS = a_pt.rearrange("p (n k r) -> p n k r", n=23, k=2)
    SEL3 = a_pt[0:64, 0:3267].rearrange("p (n a) -> p n a", n=3)
    PPD = a_pt[0:64, 3267:3399]
    SCR = a_pt[0:64, 3400:3433]
    SUM2 = a_pt[0:64, 3440:3504]
    RNK = a_pt[0:64, 3510:3543]
    MB = a_pt[:, 3550:3614].rearrange("p (k j) -> p k j", k=2)
    HT = AR[:, 0:2 * MF * TOK].rearrange("p (m t) -> p m t", m=2 * MF)

    J_IN, J_GLU, J_W1, J_OUT, J_GU, J_DN = 0, 14, 18, 20, 28, 72
    full = [S["slot0_full"], S["slot1_full"]]
    used = [S["slot0_used"], S["slot1_used"]]

    with nc.Block() as block:
        @block.sync
        def _(sp):
            sp.dma_start(CT[:, :], T["consts"]).then_inc(S["consts_in"], 16)
            sp.dma_start(XT[:, :, :], T["x"]).then_inc(S["x_in"], 16)
            sp.dma_start(PG[:, :], T["pages"]).then_inc(S["pages_in"], 16)
            sp.wait_ge(S["zero_set"], 1)
            for i in range(L):
                sp.dma_start(T["win_zeros"][i], AR[:, 0:1024]).then_inc(S["zero_out"], 16)
            sp.wait_ge(S["consts_in"], 16)
            sp.wait_ge(S["x_in"], 16)
            sp.wait_ge(S["pages_in"], 16)
            sp.wait_ge(S["zero_out"], 16 * L)

        @block.vector
        def _(dve):
            dve.memset(AR[:, 0:1024], 0.0).then_inc(S["zero_set"], 1)
    nc.all_engine_barrier(sems_to_clear=range(handles[0].num, handles[-1].num + 1))

    with nc.Fori(0, L) as lay:
        with nc.Block() as block:
            @block.sync
            def _(sp):
                def slot_load(n, later, dst, src):
                    if n >= 2 or not isinstance(later, int):
                        sp.wait_ge(used[n % 2], n // 2 + later)
                    sp.dma_start(dst, src).then_inc(full[n % 2], 16)

                def slot(n, k=16):
                    return WR[:, n % 2, 0:k, :].rearrange("p k x -> p (k x)")

                def row(name, i):
                    return T[name][bass.ds(i, 1)].rearrange("a p x -> p (a x)")

                def stream(name, first, count, k=16, peel=0):
                    for i in range(peel):
                        slot_load(first + i, 0, slot(i, k), row(name, lay * count + i))
                    with sp.Fori(peel // 2, count // 2) as i:
                        for s in range(2):
                            sp.wait_ge(used[s], first // 2 + i)
                            sp.dma_start(slot(s, k), row(name, lay * count + 2 * i + s)).then_inc(full[s], 16)

                stream("w_in", J_IN, 14, peel=2)
                sp.dma_start(T["win_kept"][bass.ds(lay, 1)].rearrange("a b r x -> (a b) r x"),
                             T["win_rows"][bass.ds(lay, 1)].rearrange("a b r x -> (a b) r x")[:, NT:WIN, :])\
                    .then_inc(S["win_copied"], 16)
                stream("w_glu", J_GLU, 4, k=8)
                for k in range(2):
                    slot_load(J_W1 + k, 0, slot(k), row("cmp_w1", lay * 2 + k))
                stream("w_out", J_OUT, 8)
                stream("w_gu", J_GU, 44)
                stream("w_down", J_DN, 32, k=11)
                sp.wait_ge(S["win_copied"], 16)

            @block.gpsimd
            def _(pool):
                def row(name, i):
                    return T[name][bass.ds(i, 1)].rearrange("a p x -> p (a x)")
                pool.dma_start(PR[:, :], row("params", lay)).then_inc(S["params_in"], 16)
                pool.dma_start(lam(0, 3), row("lam", lay)).then_inc(S["ssm_in"], 16)
                pool.dma_start(s_bn, row("ssm_b", lay)).then_inc(S["ssm_in"], 16)
                pool.dma_start(s_cb, row("ssm_c", lay)).then_inc(S["ssm_in"], 16)
                pool.dma_start(s_h0, row("ssm_h0", lay)).then_inc(S["ssm_in"], 16)
                pool.dma_start(VRF[:, 0:KC * 24], row("w_gates", lay)).then_inc(S["gate_w_in"], 16)
                pool.dma_start(W2[:, :, :].rearrange("p k d -> p (k d)"), row("cmp_w2", lay)).then_inc(S["w2_in"], 16)
                with pool.Fori(0, 4) as q:
                    pool.wait_ge(S["scan_done"], q + 1)
                    pool.tensor_copy(HL[:, bass.ds(q * QP, QP), :, 0:1], HS[:, :, :, SEQ - 1:SEQ])
                    pool.tensor_copy(HL[:, bass.ds(q * QP, QP), :, 1:9], HS[:, :, :, SEQ + NT - 1:TOK:NT])\
                        .then_inc(S["state_kept"], 2)
                pool.wait_ge(S["state_kept"], 8)
                pool.dma_start(row("ssm_last", lay), s_hl).then_inc(S["states_out"], 16)
                pool.wait_ge(S["qk_normed"], 6)
                pool.wait_ge(S["proj_evac"], 16)
                pool.dma_start(row("kv_new", lay), PJ[:, T_KC:NTILE, :].rearrange("p m t -> p (m t)"))\
                    .then_inc(S["kv_out"], 16)
                pool.wait_ge(S["states_out"], 16)
                pool.wait_ge(S["y_evac"], 5)
                pool.wait_ge(S["scan_done"], 4)
                with pool.Fori(0, NB // 2) as b2:
                    for h in range(2):
                        with pool.Fori(0, NPG) as g:
                            pool.wait_ge(S[f"cache{h}_used"], b2 + 1)
                            page = pool.value_load(PG[0:1, bass.ds(b2 * 2 * NPG + h * NPG + g, 1)], min_val=0, max_val=159)
                            pool.dma_start(AR[:, bass.ds(8192 * h + g * 512, 512)], row("cache_cmp", lay * 160 + page))\
                                .then_inc(S[f"cache{h}_full"], 16)
                pool.wait_ge(S["cache0_used"], 5)
                pool.wait_ge(S["cache1_used"], 5)
                pool.wait_ge(S["ck_evac"], 18)
                pool.dma_start(SEL3[:, 2, :], T["ties"]).then_inc(S["tie_in"], 16)
                with pool.Fori(0, 4) as g4:
                    for b in range(NB):
                        n = b % 4
                        with pool.Fori(0, 4) as g:
                            pool.wait_ge(S["kring_free"], g4 * 8 + b + 1)
                            page = pool.value_load(PG[0:1, bass.ds(g4 * 4 + b * NPG + g, 1)], min_val=0, max_val=159)
                            dst = KR[n].rearrange("p h (g s) -> p h g s", g=4)[:, :, bass.ds(g, 1), :].rearrange("p h g s -> p h (g s)")
                            src = T["cache_slc_k"][bass.ds(lay * 160 + page, 1)].rearrange("a p (h s) -> p (a h) s", h=2)
                            pool.dma_start(dst, src).then_inc(S[f"kring{n}_full"], 16)
                for b in range(NB):
                    pool.wait_ge(S["kring_free"], 33 + b)
                    pool.dma_start(a_ring[:, 1024 * (b % 4):1024 * (b % 4) + 1024],
                                   row("win_k", lay * NB + b)).then_inc(S[f"kring{b % 4}_full"], 16)
                pool.wait_ge(S["kring_free"], 44)
                pool.wait_ge(S["fresh_done"], 1)
                with pool.Fori(0, NB) as b:
                    for n in range(4):
                        with pool.Fori(0, 4) as g:
                            pool.wait_ge(S["vring_free"], b * 5 + n + 1)
                            page = pool.value_load(PG[0:1, bass.ds(b * NPG + n * 4 + g, 1)], min_val=0, max_val=159)
                            pool.dma_start(a_ring[:, bass.ds(1024 * n + g * 256, 256)], row("cache_slc_v", lay * 160 + page))\
                                .then_inc(S[f"vring{n}_full"], 16)
                    pool.wait_ge(S["vring_free"], b * 5 + 5)
                    pool.dma_start(a_qp[:, 0:1024], row("win_v", lay * NB + b)).then_inc(S["vwin_full"], 16)
                for n, v in [("params_in", 16), ("ssm_in", 64), ("gate_w_in", 16), ("w2_in", 16), ("states_out", 16),
                             ("kv_out", 16), ("tie_in", 16), ("cache0_full", 1024), ("cache1_full", 1024),
                             ("vwin_full", 128)] + [(f"kring{i}_full", 544) for i in range(4)] \
                        + [(f"vring{i}_full", 512) for i in range(4)]:
                    pool.wait_ge(S[n], v)
                pool.dma_reset(range(handles[0].num, handles[-1].num + 1))

            def norm_squares(act, n, src, count, before=None):
                for c in range(count):
                    if c >= 2:
                        act.wait_ge(S[n + "_stat"], c - 1)
                    act.activation(SQ[:, c % 2, :], src(c), ACT.Square).then_inc(S[n + "_sq"], 1)

            def norm_sum(pe, n, count, dst):
                for c in range(count):
                    pe.wait_ge(S[n + "_sq"], c + 1)
                    pe.matmul(dst, ones, SQ[:, c % 2, :], start=c == 0, stop=c == count - 1).then_inc(S[n + "_stat"], 1)

            def norm_root(act, n, k, v, r):
                act.wait_ge(S[n + "_var"], k)
                act.activation(r, v, ACT.Sqrt).then_inc(S[n + "_root"], 1)

            def norm_var(dve, n, k, stat, v, width):
                dve.wait_ge(S[n + "_stat"], k)
                dve.tensor_scalar(v, stat, 1.0 / width, EPS, ALU.mult, ALU.add).then_inc(S[n + "_var"], 1)

            def norm_recip(dve, n, k, v, r, t):
                dve.wait_ge(S[n + "_root"], k)
                dve.reciprocal(r, r)
                dve.drain()
                dve.tensor_tensor(t, r, r, ALU.mult)
                dve.drain()
                dve.scalar_tensor_tensor(out=t, in0=t, scalar=-0.5, in1=v, op0=ALU.mult, op1=ALU.mult)
                dve.drain()
                dve.scalar_tensor_tensor(out=r, in0=t, scalar=1.5, in1=r, op0=ALU.add, op1=ALU.mult)
                dve.drain()

            def norm_all(dve, n, src, dst, gain, count, stat=4):
                norm_var(dve, n, count, bank(stat)[:, 0:TOK], NV[:, 0, :], count * P)
                norm_recip(dve, n, 1, NV[:, 0, :], NR[:, 0, :], NV[:, 1, :])
                for c in range(count):
                    dve.scalar_tensor_tensor(out=dst(c), in0=src(c), scalar=PR[:, gain + c:gain + c + 1],
                                             in1=NR[:, 0, :], op0=ALU.mult, op1=ALU.mult).then_inc(S[n + "_normed"], 1)

            QK = [T_Q, T_Q + 2, T_Q + 4, T_Q + 6, T_KS, T_KW]
            QKG = [C_QN] * 4 + [C_KS, C_KW]

            @block.tensor
            def _(pe):
                for n in ("cache0_used", "cache1_used", "ps_done", "pt_done"):
                    pe.drain().then_inc(S[n], 1)
                norm_sum(pe, "mix", KC, bank(4)[:, 0:TOK])

                def products(s, wait, rhs, banks_, k=16, start=True, stop=True, first=0):
                    pe.wait_ge(full[s], wait)
                    for m in range(2):
                        for c in range(k):
                            mm = pe.matmul(banks_[:, m, 0:TOK], WR[:, s, c, 128 * m:128 * m + 128], rhs(first + c),
                                           start=start and c == 0, stop=stop and c == k - 1)
                    mm.then_inc(used[s], 1)

                def hc(c):
                    return HC[:, c, :]

                pe.wait_ge(S["mix_normed"], KC)
                with pe.Fori(0, 2) as i:
                    for s in range(2):
                        pe.wait_ge(S["proj_evac"], 2 * i + s + 1)
                        products(s, 16 + 16 * i, hc, PS[s])

                def turn_b(n):
                    pe.wait_ge(S["bbar_ready"], n)
                    for r in range(2):
                        for t in range(2):
                            mm = pe.transpose(bank(4)[:, 256 * r + 128 * t:256 * r + 128 * t + 128],
                                              BBN[:, r, 4 * t:4 * t + 4, :].rearrange("p j x -> p (j x)"), ident)
                    mm.then_inc(S["bbar_turned"], 1)

                def bu(q, n):
                    pe.wait_ge(S["bbar_evac"], n)
                    for j in range(QP):
                        o = 32 * (j % 4)
                        for r in range(2):
                            k = 2 * j + r
                            pe.wait_ge(S["bu_evac"], q * 16 + k + 1)
                            pe.matmul(bank(6 + k % 2)[:, 0:TOK], BBS[o:o + 32, r, j // 4, :],
                                      NV[o:o + 32, j // 4, :],
                                      start=True, stop=True).then_inc(S["bu_done"], 1)

                def y_out(n, b_read):
                    pe.wait_ge(S["scan_done"], n)
                    pe.wait_ge(S["c_slot"], n)
                    pe.wait_ge(S["bbar_evac"], b_read)
                    for j in range(QP):
                        o = 32 * (j % 4)
                        for r in range(2):
                            mm = pe.matmul(PS[2][o:o + 32, j // 4, 0:TOK], CBS[:, j, r, :], HS[:, j, r, :],
                                           start=r == 0, stop=r == 1, tile_position=(0, o))
                    mm.then_inc(S["y_done"], 1)

                pe.wait_ge(S["proj_evac"], 6)
                turn_b(1)
                bu(0, 1)
                with pe.Fori(0, 3) as q:
                    pe.wait_ge(S["y_evac"], q + 1)
                    turn_b(q + 2)
                    for s in range(2):
                        pe.wait_ge(S["proj_evac"], 2 * q + s + 5)
                        products(s, 48 + 16 * q, hc, PS[s])
                    y_out(q + 1, q + 2)
                    bu(q + 1, q + 2)
                with pe.Fori(0, 2) as i:
                    for s in range(2):
                        pe.wait_ge(S["proj_evac"], 2 * i + s + 11)
                        products(s, 96 + 16 * i, hc, PS[s])
                pe.wait_ge(S["gate_w_in"], 16)
                pe.wait_ge(S["proj_evac"], 16)
                for c in range(KC):
                    mm = pe.matmul(bank(0)[0:24, 0:TOK], WG[:, c, :], HC[:, c, :], start=c == 0, stop=c == KC - 1)
                mm.then_inc(S["gates_done"], 1)
                y_out(4, 4)
                pe.wait_ge(S["y_evac"], 5)
                for n in range(6):
                    pe.wait_ge(S["qk_sq"], n + 1)
                    if n:
                        pe.wait_ge(S["qk_var"], n)
                    for m in range(2):
                        mm = pe.matmul(PS[2][:, m, 0:TOK], ones, SQ[:, m, :], start=True, stop=True)
                    mm.then_inc(S["qk_stat"], 1)
                pe.wait_ge(S["gates_sig"], 1)
                pe.wait_ge(S["bu_evac"], 66)
                for t in range(3):
                    n = P if t < 2 else SMP
                    b_ = bank([1, 6, 7][t])
                    for i, tile in enumerate([T_VS, T_VS + 1, T_VW, T_VW + 1]):
                        pe.transpose(b_[0:n, 128 * i:128 * i + 128], PJ[:, tile, P * t:P * t + n], ident)
                    pe.transpose(bank(0)[0:n, 32 * t:32 * t + 24], GT[0:24, P * t:P * t + n], ident[0:24, 0:24])\
                        .then_inc(S["vt_done"], 1)
                pe.wait_ge(S["z_ready"], 1)
                pe.wait_ge(S["vr_ready"], 3)
                with pe.Fori(0, 2) as i:
                    for s in range(2):
                        pe.wait_ge(S["glu_evac"], 2 * i + s + 1)
                        products(s, 128 + 16 * i, lambda c: ZB[:, c, :], PS[s], k=8)
                pe.wait_ge(S["glu_evac"], 6)
                pe.wait_ge(S["w2_in"], 16)
                for k in range(2):
                    pe.wait_ge(full[k], 16 * (J_W1 // 2 + 1))
                W1 = [WR[:, k, :, :].rearrange("p a b -> p (a b)").rearrange("p (l h) -> p l h", h=HD) for k in range(2)]
                for k in range(2):
                    for l in range(32):
                        mm = pe.matmul(bank(k)[:, 0:2 * NCMP_P], W1[k][:, l, :],
                                       PJ[:, T_KC + 2 * k:T_KC + 2 * k + 2, l:l + 16 * (NCMP_P - 1) + 1:16],
                                       start=l == 0, stop=l == 31)
                    mm.then_inc(S["conv_done"], 1)

                def second(k, n, cols):
                    pe.wait_ge(S["hid_ready"], n)
                    if k == 0:
                        mm = pe.matmul(bank(2)[:, 0:2 * cols], W2[:, 0, :], HID[0][:, 0:2 * cols], start=True, stop=True)
                    else:
                        for h in range(2):
                            mm = pe.matmul(bank(3)[0:cols, 128 * h:128 * h + 128], HID[1][:, cols * h:cols * h + cols],
                                           W2[:, 1, :], start=True, stop=True)
                    mm.then_inc(S["w2_done"], 1)

                second(0, 1, NCMP_P)
                second(1, 2, NCMP_P)
                with pe.Fori(0, NB // 2) as b2:
                    for hb in range(2):
                        n0 = b2 * 4 + 2 * hb + 2
                        pe.wait_ge(S[f"cache{hb}_full"], b2 * 256 + 256)
                        for k in range(2):
                            pe.wait_ge(S["conv_evac"], n0 + k - 1)
                            for half in range(2):
                                for i in range(16):
                                    mm = pe.matmul(bank(k)[:, 256 * half:256 * half + 256]
                                                   .rearrange("p (h g c) -> p h g c", h=2, g=NPG),
                                                   W1[k][:, 16 * half + i, :],
                                                   CTB[hb][:, :, :, k, i, :].rearrange("p g h c -> p h g c"),
                                                   start=i == 0, stop=i == 15)
                            mm.then_inc(S["conv_done"], 1)
                        mm = pe.drain()
                        mm.then_inc(S[f"cache{hb}_used"], 1)
                        for k in range(2):
                            pe.wait_ge(S["ck_evac"], n0 + k - 1)
                            second(k, n0 + k + 1, NCMP)
                for s in range(2):
                    pe.drain().then_inc(used[s], 1)
                pe.drain().then_inc(S["kring_free"], 4)
                pe.drain().then_inc(S["vring_free"], 5)
                for n in range(5):
                    w = 508 if n < 4 else 2 * NCMP_P
                    pe.wait_ge(S["ckn_sq"], n + 1)
                    if n:
                        pe.wait_ge(S["ckn_var"], n)
                    pe.matmul(bank(4)[:, 0:w], ones, SQ[:, :, :].rearrange("p a b -> p (a b)")[:, 0:w],
                              start=True, stop=True).then_inc(S["ckn_stat"], 1)
                pe.wait_ge(S["ck_normed"], 5)
                for k in range(NKV):
                    with pe.Fori(0, GQA) as g:
                        n = g + GQA * k
                        pe.wait_ge(S["q_copied"], n + 1)
                        for t in range(2):
                            w = P * (t + 1)
                            pe.wait_ge(S["ps_evac"], n + 1)
                            sc = PS[t]
                            pe.matmul(sc[:, 0, 0:w], QS[:, t, :], PJ[:, T_KS + k, 0:w], start=True, stop=True)
                            pe.matmul(sc[:, 0, 256:256 + w], QS[:, t, :], PJ[:, T_KW + k, 0:w], start=True, stop=True)
                            pe.matmul(sc[:, 1, 0:NCMP_P], QS[:, t, :], CKP[:, k, :], start=True, stop=True)\
                                .then_inc(S["ps_done"], 1)
                        for t in range(2):
                            pe.wait_ge(S["p_ready"], 2 * n + t + 1)
                            pe.wait_ge(S["pt_evac"], 2 * n + t + 1)
                            at_ = 0
                            for br in range(2):
                                for x in range(t + 1):
                                    pe.transpose(PS[2][:, 0, 128 * at_:128 * at_ + 128], SPR[:, t, br, P * x:P * x + P], ident)
                                    at_ += 1
                            pe.transpose(PS[2][0:NCMP_P, 1, 0:P], SPR[:, t, 2, 0:NCMP_P], ident).then_inc(S["pt_done"], 1)
                        for t in range(2):
                            pe.wait_ge(S["pt_evac"], 2 * n + t + 2)
                            pe.wait_ge(S["po_evac"], 2 * n + t + 1)
                            at_ = 0
                            for br in range(2):
                                for x in range(t + 1):
                                    pe.matmul(bank(6)[:, 0:P], VR[:, x, br, k, :], PTP[:, t, at_, :], start=at_ == 0, stop=False)
                                    at_ += 1
                            pe.matmul(bank(6)[:, 0:P], CVP[0:NCMP_P, k, :], PTP[0:NCMP_P, t, 4, :], start=False, stop=True)\
                                .then_inc(S["po_done"], 1)
                pe.wait_ge(S["qpad_ready"], 1)
                pe.wait_ge(S["po_evac"], 17)
                for k in range(NKV):
                    for b in range(NB):
                        mm = pe.matmul(bank(k)[:, 0:NCMP], QPD[:, k, b, :], CK[:, b, k, :], start=b == 0, stop=b == NB - 1)
                mm.then_inc(S["cs_done"], 1)
                for k in range(NKV):
                    pe.matmul(bank(7)[:, 64 * k:64 * k + 32], QA[:, k, :], PJ[:, T_KS + k, SEQ:TOK], start=True, stop=True)
                    mm = pe.matmul(bank(7)[:, 64 * k + 32:64 * k + 64], QA[:, k, :], PJ[:, T_KW + k, SEQ:TOK],
                                   start=True, stop=True)
                mm.then_inc(S["fresh_done"], 1)
                pe.wait_ge(S["c_prob"], 1)
                for k in range(NKV):
                    mm = pe.matmul(bank(6)[32 * k:32 * k + 32, 0:NCMP], const(K_G), SCM[:, k, :], start=True, stop=True,
                                   tile_position=(0, 32 * k))
                mm.then_inc(S["gsum_done"], 1)

                def key_group(n, wait):
                    pe.wait_ge(S["kgroup_evac"], n + 1)
                    for b in range(NB):
                        pe.wait_ge(S[f"kring{b % 4}_full"], wait(b))
                        for k in range(NKV):
                            mm = pe.matmul(PS[1][:, k, :], QPD[:, k, b, :], KR[b % 4][:, k, :], start=b == 0, stop=b == NB - 1)
                        mm.then_inc(S["kring_free"], 1)
                    pe.drain().then_inc(S["kgroup_done"], 1)

                with pe.Fori(0, 4) as g4:
                    key_group(g4, lambda b: g4 * 128 + 64 * (b // 4) + 64)
                key_group(4, lambda b: 512 + 16 * (b // 4 + 1))
                banks_ = [0, 1, 4, 5, 6, 7]
                pe.wait_ge(S["ranked"], 1)
                pe.wait_ge(S["fresh_evac"], 1)
                pe.wait_ge(S["sw_ready"], 3)
                blocks = [(SS, x, P) for x in range(16)] + [(SS, 16, SMP)] + [(SW, x, P) for x in range(4)] \
                    + [(SW, 4, SMP)] + [(SCM, 0, NCMP)]
                for n in range(12):
                    if n >= 6:
                        pe.wait_ge(S["st_evac"], n - 5)
                    for m, (src, x, w) in enumerate(blocks[2 * n:2 * n + 2]):
                        for k in range(NKV):
                            mm = pe.transpose(bank(banks_[n % 6])[0:w, 256 * m + 128 * k:256 * m + 128 * k + 128],
                                              src[:, k, P * x:P * x + w], ident)
                    mm.then_inc(S["st_done"], 1)
                pe.wait_ge(S["st_evac"], 12)
                for k in range(NKV):
                    o = PS[1][:, k, 0:P]
                    pe.matmul(o, VR[0:SMP, 2, 0, k, :], PTS[0:SMP, 16, k, :], start=True, stop=False, skip_group_check=True)
                    pe.matmul(o, VR[0:SMP, 2, 1, k, :], PTS[0:SMP, 21, k, :], start=False, stop=False, skip_group_check=True)
                    for b in range(NB):
                        pe.matmul(o.rearrange("p (g r) -> p g r", g=GQA)[:, :, NT * b:NT * b + NT], CV[0:NCMP, b, k, :],
                                  PTS[0:NCMP, 22, k, :].rearrange("p (g r) -> p g r", g=GQA)[:, :, NT * b:NT * b + NT],
                                  start=False, stop=False, skip_group_check=True)
                with pe.Fori(0, NB) as b:
                    for n in range(5):
                        if n < 4:
                            pe.wait_ge(S[f"vring{n}_full"], b * 64 + 64)
                        else:
                            pe.wait_ge(S["vwin_full"], b * 16 + 16)
                        src = VG[n] if n < 4 else VW
                        for g in range(4):
                            blk = 4 * n + g if n < 4 else 17 + g
                            for k in range(NKV):
                                mm = pe.matmul(PS[1][:, k, 0:P].rearrange("p (g r) -> p g r", g=GQA)[:, :, bass.ds(b * NT, NT)],
                                               src[:, g, k, :],
                                               PTS[:, blk, k, :].rearrange("p (g r) -> p g r", g=GQA)[:, :, bass.ds(b * NT, NT)],
                                               start=False, stop=False, skip_group_check=True)
                        mm.then_inc(S["vring_free"], 1)
                pe.drain().then_inc(S["so_done"], 1)
                norm_sum(pe, "sn", SC, bank(4)[:, 0:TOK])
                norm_sum(pe, "an", SC, bank(5)[:, 0:TOK])
                pe.wait_ge(S["sn_normed"], SC)
                pe.wait_ge(S["an_normed"], SC)
                with pe.Fori(0, 4) as i:
                    for s in range(2):
                        pe.wait_ge(S["out_evac"], 2 * i + s + 1)
                        products(s, 16 * (J_OUT // 2 + 1) + 16 * i, hc, PS[s])
                norm_sum(pe, "fn", KC, bank(4)[:, 0:TOK])
                pe.wait_ge(S["fn_normed"], KC)
                with pe.Fori(0, MF // 2) as i:
                    for m in range(2):
                        pe.wait_ge(S["gu_evac"], 2 * i + m + 1)
                        for s in range(2):
                            products(s, 16 * (J_GU // 2 + 1) + 32 * i + 16 * m, hc, PS[2 * m + s])
                        pe.drain().then_inc(S["gu_done"], 1)
                pe.wait_ge(S["gu_evac"], MF + 2)
                with pe.Fori(0, 4) as i:
                    for m in range(2):
                        pe.wait_ge(S["down_evac"], 2 * i + m + 1)
                        for qd in range(4):
                            products(qd % 2, 16 * (J_DN // 2 + 1) + 64 * i + 32 * m + 16 * (qd // 2), lambda c: HT[:, c, :],
                                     PS[m], k=11, start=qd == 0, stop=qd == 3, first=11 * qd)
                        pe.drain().then_inc(S["down_done"], 1)

            @block.scalar
            def _(act):
                def evac(dst, src, sem, by=1):
                    act.activation(dst, src, ACT.Copy).then_inc(S[sem], by)

                act.wait_ge(S["params_in"], 16)
                act.drain().then_inc(S["proj_evac"], 2)
                act.drain().then_inc(S["bu_evac"], 2)
                act.drain().then_inc(S["pt_evac"], 1)
                norm_squares(act, "mix", lambda c: XT[:, c, :], KC)
                norm_root(act, "mix", 1, NV[:, 0, :], NR[:, 0, :])
                act.wait_ge(S["ssm_in"], 64)
                act.activation(lam(3), lam(2), ACT.Exp).then_inc(S["lam_dt"], 1)
                act.wait_ge(S["lam_xr"], 1)
                act.activation(lam(6), lam(4), ACT.Exp).then_inc(S["lam_mag"], 1)
                act.activation(lam(9), lam(7), ACT.Sin)
                act.activation(lam(10), lam(8), ACT.Sin).then_inc(S["lam_sin"], 1)
                with act.Fori(0, 2) as i:
                    for s in range(2):
                        act.wait_ge(used[s], i + 1)
                        evac(PJ[:, bass.ds(4 * i + 2 * s, 2), :], PS[s][:, :, 0:TOK], "proj_evac")

                def b_slot(q):
                    act.wait_ge(S["proj_evac"], 6)
                    act.wait_ge(S["bbar_turned"], q + 1)
                    act.activation(NV[:, :, :], PJ[:, bass.ds(2 * q, 2), :], ACT.Copy)
                    act.activation(s_bbs, bank(4), ACT.Copy)
                    act.drain().then_inc(S["bbar_evac"], 1)

                def c_slot(q):
                    act.activation(CBS[:, :, 0, :], CB[:, bass.ds(q * QP, QP), 0, :], ACT.Copy)
                    act.mul(CBS[:, :, 1, :], CB[:, bass.ds(q * QP, QP), 1, :], -1.0)
                    act.drain().then_inc(S["c_slot"], 1)

                def states(q):
                    for k in range(16):
                        act.wait_ge(S["bu_done"], q * 16 + k + 1)
                        evac(HS[:, k // 2, k % 2, :], bank(6 + k % 2)[:, 0:TOK], "bu_evac")

                b_slot(0)
                c_slot(0)
                states(0)
                with act.Fori(0, 3) as q:
                    b_slot(q + 1)
                    for s in range(2):
                        act.wait_ge(used[s], q + 3)
                        evac(PJ[:, bass.ds(4 * q + 8 + 2 * s, 2), :], PS[s][:, :, 0:TOK], "proj_evac")
                    act.wait_ge(S["y_done"], q + 1)
                    c_slot(q + 1)
                    act.wait_ge(S["state_kept"], 2 * q + 2)
                    states(q + 1)
                with act.Fori(0, 2) as i:
                    for s in range(2):
                        act.wait_ge(used[s], i + 6)
                        evac(PJ[:, bass.ds(4 * i + 20 + 2 * s, 2), :], PS[s][:, :, 0:TOK], "proj_evac")
                act.wait_ge(S["gates_done"], 1)
                act.activation(GT[:, :], bank(0)[0:24, 0:TOK], ACT.Sigmoid).then_inc(S["gates_sig"], 1)
                act.wait_ge(S["y_evac"], 5)
                act.activation(ZB[:, :, :], ZB[:, :, :], ACT.Gelu_apprx_tanh).then_inc(S["z_ready"], 1)
                for n, tile in enumerate(QK):
                    if n:
                        act.wait_ge(S["qk_normed"], n)
                    act.activation(SQ[:, :, :], PJ[:, tile:tile + 2, :], ACT.Square).then_inc(S["qk_sq"], 1)
                    norm_root(act, "qk", n + 1, NV[:, :, :], NR[:, :, :])
                act.wait_ge(S["qk_normed"], 6)
                with act.Fori(0, 2) as i:
                    for s in range(2):
                        act.wait_ge(used[s], i + 8)
                        act.wait_ge(S["glu_evac"], 2 * i + s + 1)
                        act.activation((NV, NR)[s][:, :, :], PS[s][:, :, 0:TOK], ACT.Sigmoid).then_inc(S["glu_sig"], 1)

                def hidden(k, n, w):
                    act.wait_ge(S["hid_pre"], n)
                    act.activation(HID[k][:, 0:w], HID[k][:, 0:w], ACT.Gelu_apprx_tanh,
                                   bias=PR[:, C_B1 + k:C_B1 + k + 1]).then_inc(S["hid_ready"], 1)

                for k in range(2):
                    hidden(k, k + 1, 2 * NCMP_P)
                with act.Fori(0, NB) as b:
                    for k in range(2):
                        hidden(k, b * 2 + k + 3, 2 * NCMP)
                act.wait_ge(S["ck_evac"], 18)
                sq = SQ[:, :, :].rearrange("p a b -> p (a b)")
                for n in range(5):
                    w = 508 if n < 4 else 2 * NCMP_P
                    if n:
                        act.wait_ge(S["ck_normed"], n)
                    act.activation(sq[:, 0:w], ubuf[:, 508 * n:508 * n + w], ACT.Square).then_inc(S["ckn_sq"], 1)
                    norm_root(act, "ckn", n + 1, NV[:, :, :].rearrange("p a b -> p (a b)")[:, 0:w],
                              NR[:, :, :].rearrange("p a b -> p (a b)")[:, 0:w])
                with act.Fori(0, NQ) as n:
                    for t in range(2):
                        w = P * (t + 1)
                        act.wait_ge(S["ps_max"], 2 * n + t + 1)
                        for br in range(3):
                            v = SPR[:, t, br, 0:(w if br < 2 else NCMP_P)]
                            e = act.activation(v, v, ACT.Exp, bias=SM[:, 3 * t + br:3 * t + br + 1],
                                               accum_out=SM[:, 6 + 3 * t + br:7 + 3 * t + br])
                        act.drain().then_inc(S["p_exp"], 1)
                    for t in range(2):
                        act.wait_ge(S["pt_done"], 2 * n + t + 2)
                        act.wait_ge(S["po_evac"], 2 * n + 1)
                        act.activation(PTP[:, t, 0:2 * (t + 1), :].rearrange("p n s -> p (n s)"),
                                       PS[2][:, 0, 0:256 * (t + 1)], ACT.Copy)
                        act.activation(PTP[0:NCMP_P, t, 4, :], PS[2][0:NCMP_P, 1, 0:P], ACT.Copy)
                        act.drain().then_inc(S["pt_evac"], 1)
                act.wait_ge(S["c_max"], 1)
                for k in range(NKV):
                    act.activation(SCM[:, k, :], SCM[:, k, :], ACT.Exp, bias=SM[:, k:k + 1], accum_out=SM[:, 2 + k:3 + k])
                act.drain().then_inc(S["c_exp"], 1)
                act.wait_ge(S["sw_max"], 1)
                for k in range(NKV):
                    for i, v in enumerate((SS, SW)):
                        act.activation(v[:, k, :], v[:, k, :], ACT.Exp, bias=SM[:, 6 + 2 * i + k:7 + 2 * i + k],
                                       accum_out=SM[:, 10 + 2 * i + k:11 + 2 * i + k])
                act.drain().then_inc(S["sw_exp"], 1)
                widths = [P] * 16 + [SMP] + [P] * 4 + [SMP] + [NCMP]
                for n in range(12):
                    act.wait_ge(S["st_done"], n + 1)
                    w = widths[2 * n:2 * n + 2]
                    src = bank([0, 1, 4, 5, 6, 7][n % 6])
                    if len(set(w)) == 1:
                        act.activation(PTS[0:w[0], 2 * n:2 * n + len(w), :, :].rearrange("p n k r -> p (n k r)"),
                                       src[0:w[0], 0:256 * len(w)], ACT.Copy)
                    else:
                        for m in range(2):
                            act.activation(PTS[0:w[m], 2 * n + m, :, :].rearrange("p k r -> p (k r)"),
                                           src[0:w[m], 256 * m:256 * m + 256], ACT.Copy)
                    act.drain().then_inc(S["st_evac"], 1)
                norm_squares(act, "sn", lambda c: HC[:, c, :], SC)
                norm_root(act, "sn", 1, NV[:, 0, :], NR[:, 0, :])
                act.wait_ge(S["sn_stat"], SC)
                act.wait_ge(S["so_evac"], 2)
                norm_squares(act, "an", lambda c: HC[:, SC + c, :], SC)
                norm_root(act, "an", 1, NV[:, 0, :], NR[:, 0, :])
                act.wait_ge(S["an_stat"], SC)
                act.wait_ge(S["out_evac"], 10)
                norm_squares(act, "fn", lambda c: XT[:, c, :], KC)
                norm_root(act, "fn", 1, NV[:, 0, :], NR[:, 0, :])
                act.wait_ge(S["fn_normed"], KC)
                with act.Fori(0, MF // 2) as i:
                    for m in range(2):
                        act.wait_ge(S["gu_done"], 2 * i + m + 1)
                        act.wait_ge(S["gu_evac"], 2 * i + m + 1)
                        act.activation((NV, NR)[m][:, :, :], PS[2 * m][:, :, 0:TOK], ACT.Silu).then_inc(S["silu_ready"], 1)

            @block.vector
            def _(dve):
                def tt(out, a, b, op):
                    return dve.tensor_tensor(out, a, b, op)

                for n, v in (("glu_evac", 2), ("out_evac", 2), ("gu_evac", 2), ("down_evac", 2),
                             ("y_evac", 1), ("ps_evac", 1), ("po_evac", 1), ("kgroup_evac", 1)):
                    dve.drain().then_inc(S[n], v)
                dve.wait_ge(S["params_in"], 16)
                norm_all(dve, "mix", lambda c: XT[:, c, :], lambda c: HC[:, c, :], C_MIX, KC)
                dve.tensor_scalar(PR[:, C_QN:C_QN + 1], PR[:, C_QN:C_QN + 1], SCALE, None, ALU.mult).then_inc(S["qgain"], 1)
                dve.wait_ge(S["lam_dt"], 1)
                LRE, LIM, DT, XR, XI, MAG, RA, RH, SN, SH, AR_, AI_, T1, T2 = (lam(i) for i in (0, 1, 3, 4, 5, 6, 7, 8, 9, 10, 11, 12, 13, 14))
                CR, CI, NR_, DEN, AIN = lam(15), lam(16), lam(17), lam(18), lam(19)
                tt(XR, LRE, DT, ALU.mult)
                tt(XI, LIM, DT, ALU.mult)
                dve.drain()
                magic = 12582912.0
                dve.tensor_scalar(T1, XI, float(1 / (2 * np.pi)), magic, ALU.mult, ALU.add)
                dve.drain()
                dve.tensor_scalar(T1, T1, -magic, None, ALU.add)
                dve.drain()
                c1 = 6.28125
                c2 = float(np.float32(2 * np.pi - c1))
                c3 = float(2 * np.pi - c1 - c2)
                dve.scalar_tensor_tensor(out=RA, in0=T1, scalar=-c1, in1=XI, op0=ALU.mult, op1=ALU.add)
                dve.drain()
                dve.scalar_tensor_tensor(out=RA, in0=T1, scalar=-c2, in1=RA, op0=ALU.mult, op1=ALU.add)
                dve.drain()
                dve.scalar_tensor_tensor(out=RA, in0=T1, scalar=-c3, in1=RA, op0=ALU.mult, op1=ALU.add)
                dve.drain()
                dve.tensor_scalar(RA, RA, 3.1415925, -3.1415925, ALU.min, ALU.max)
                dve.drain()
                dve.tensor_scalar(RH, RA, 0.5, None, ALU.mult)
                dve.drain().then_inc(S["lam_xr"], 1)
                dve.wait_ge(S["lam_sin"], 1)
                tt(T1, SH, SH, ALU.mult)
                tt(AI_, MAG, SN, ALU.mult)
                dve.drain()
                dve.tensor_scalar(T1, T1, -2.0, 1.0, ALU.mult, ALU.add)
                dve.drain()
                tt(AR_, MAG, T1, ALU.mult)
                dve.drain()
                tt(T1, LRE, LRE, ALU.mult)
                tt(T2, LIM, LIM, ALU.mult)
                dve.drain()
                tt(DEN, T1, T2, ALU.add)
                dve.tensor_scalar(NR_, AR_, -1.0, None, ALU.add)
                dve.tensor_scalar(AIN, AI_, -1.0, None, ALU.mult)
                dve.drain()
                dve.reciprocal(DEN, DEN)
                tt(T1, NR_, LRE, ALU.mult)
                tt(T2, AI_, LIM, ALU.mult)
                dve.drain()
                tt(CR, T1, T2, ALU.add)
                dve.drain()
                tt(CR, CR, DEN, ALU.mult)
                dve.drain()
                tt(T1, AI_, LRE, ALU.mult)
                tt(T2, NR_, LIM, ALU.mult)
                dve.drain()
                tt(CI, T1, T2, ALU.subtract)
                dve.drain()
                tt(CI, CI, DEN, ALU.mult)

                def cmul(outr, outi, ar, ai, br, bi, t1, t2):
                    tt(t1, ar, br, ALU.mult)
                    tt(t2, ai, bi, ALU.mult)
                    dve.drain()
                    tt(outr, t1, t2, ALU.subtract)
                    dve.drain()
                    tt(t1, ar, bi, ALU.mult)
                    tt(t2, ai, br, ALU.mult)
                    dve.drain()
                    tt(outi, t1, t2, ALU.add)
                    dve.drain()

                dve.tensor_copy(PWR[:, :, 0], AR_)
                dve.tensor_copy(PWI[:, :, 0], AI_)
                dve.drain()
                for k in (1, 2, 4, 8):
                    tr = s_t1[:, 0:32 * k].rearrange("p (j i) -> p j i", i=k)
                    ti = s_t2[:, 0:32 * k].rearrange("p (j i) -> p j i", i=k)
                    cmul(PWR[:, :, k:2 * k], PWI[:, :, k:2 * k], PWR[:, :, 0:k], PWI[:, :, 0:k],
                         PWR[:, :, k - 1:k].to_broadcast([P, NPAIR, k]), PWI[:, :, k - 1:k].to_broadcast([P, NPAIR, k]), tr, ti)
                AP_ = [(PWR[:, :, 15], PWI[:, :, 15])] + [(lam(20 + 2 * i), lam(21 + 2 * i)) for i in range(3)]
                for i in range(3):
                    cmul(*AP_[i + 1], *AP_[i], *AP_[i], T1, T2)

                def bbar(q, n):
                    if n is not None:
                        dve.wait_ge(S["bbar_turned"], n)
                    sl = bass.ds(q * QP, QP)
                    b_ = [BN[:, r, sl, :] for r in range(2)]
                    cr, ci = (v[:, sl].unsqueeze(2).to_broadcast([P, QP, 32]) for v in (CR, CI))
                    t1, t2 = (v.rearrange("p (j x) -> p j x", j=QP) for v in (s_c1, s_c2))
                    cmul(BBN[:, 0], BBN[:, 1], cr, ci, b_[0], b_[1], t1, t2)
                    dve.drain().then_inc(S["bbar_ready"], 1)

                def swapped(v):
                    a = [list(x) for x in v.ap]
                    step, n = a[2]
                    return bass.AP(v.tensor, v.offset + step, [a[0], a[1], [-step, n]] + a[3:])

                ARQ, AIQ = s_lam[:, 0:8], s_lam[:, 8:24].rearrange("p (j r) -> p j r", r=2)

                def scan(q):
                    sl = bass.ds(q * QP, QP)

                    def coef(pr, pi):
                        dve.tensor_copy(ARQ, pr[:, sl])
                        dve.tensor_copy(AIQ[:, :, 1], pi[:, sl])
                        dve.tensor_scalar(AIQ[:, :, 0], pi[:, sl], -1.0, None, ALU.mult)
                        dve.drain()

                    def advance(prev, cur, n):
                        t1 = s_c1[:, 0:QP * 2 * n].rearrange("p (j r c) -> p j r c", j=QP, r=2)
                        t2 = s_c2[:, 0:QP * 2 * n].rearrange("p (j r c) -> p j r c", j=QP, r=2)
                        tt(t1, prev, ARQ.unsqueeze(2).unsqueeze(3).to_broadcast([P, QP, 2, n]), ALU.mult)
                        tt(t2, swapped(prev), AIQ.unsqueeze(3).to_broadcast([P, QP, 2, n]), ALU.mult)
                        dve.drain()
                        tt(cur, cur, t1, ALU.add)
                        dve.drain()
                        tt(cur, cur, t2, ALU.add)
                        dve.drain()

                    coef(PWR[:, :, 0], PWI[:, :, 0])
                    dve.tensor_copy(CA[:, :, :, 0:NB], H0[:, sl, :, :])
                    dve.drain()
                    advance(CA[:, :, :, 0:NB], HS[:, :, :, SEQ:TOK:NT], NB)
                    for i in range(1, NT):
                        advance(HS[:, :, :, SEQ + i - 1:TOK:NT], HS[:, :, :, SEQ + i:TOK:NT], NB)
                    for i in range(1, CH):
                        advance(HS[:, :, :, i - 1:SEQ:CH], HS[:, :, :, i:SEQ:CH], CH)
                    dve.tensor_copy(CA, HS[:, :, :, CH - 1:SEQ:CH])
                    for i, d in enumerate((1, 2, 4, 8)):
                        coef(*AP_[i])
                        advance(CA[:, :, :, 0:CH - d], CA[:, :, :, d:CH], CH - d)
                    for r in range(2):
                        t1, t2 = (v.rearrange("p (j c i) -> p j c i", j=QP, c=CH - 1) for v in (s_t1, s_t2))
                        pr, pi = (v[:, sl, :].unsqueeze(2).to_broadcast([P, QP, CH - 1, CH]) for v in (PWR, PWI))
                        own = CA[:, :, r, 0:CH - 1].unsqueeze(3).to_broadcast([P, QP, CH - 1, CH])
                        other = CA[:, :, 1 - r, 0:CH - 1].unsqueeze(3).to_broadcast([P, QP, CH - 1, CH])
                        tt(t1, pr, own, ALU.mult)
                        tt(t2, pi, other, ALU.mult)
                        dve.drain()
                        tt(t1, t1, t2, ALU.add if r else ALU.subtract)
                        dve.drain()
                        h = HS[:, :, r, CH:SEQ].rearrange("p j (c i) -> p j c i", i=CH)
                        tt(h, h, t1, ALU.add)
                        dve.drain()
                    dve.drain().then_inc(S["scan_done"], 1)

                def y_evac(q, n):
                    dve.wait_ge(S["y_done"], n)
                    for t in range(2):
                        dve.scalar_tensor_tensor(out=ZB[:, bass.ds(2 * q + t, 1), :].rearrange("p a t -> p (a t)"),
                                                 in0=PJ[:, bass.ds(2 * q + t, 1), :].rearrange("p a t -> p (a t)"),
                                                 scalar=PR[:, bass.ds(C_D + 2 * q + t, 1)],
                                                 in1=PS[2][:, t, 0:TOK], op0=ALU.mult, op1=ALU.add)
                    dve.drain().then_inc(S["y_evac"], 1)

                bbar(0, None)
                with dve.Fori(0, 3) as q:
                    bbar(q + 1, q + 1)
                    dve.wait_ge(S["bu_evac"], 16 * q + 18)
                    scan(q)
                    y_evac(q, q + 1)
                dve.wait_ge(S["bu_evac"], 66)
                scan(3)
                dve.wait_ge(S["proj_evac"], 16)
                y_evac(3, 4)
                for n, tile in enumerate(QK):
                    norm_var(dve, "qk", n + 1, PS[2][:, :, 0:TOK], NV[:, :, :], HD)
                    norm_recip(dve, "qk", n + 1, NV[:, :, :], NR[:, :, :], SQ[:, :, :])
                    dve.scalar_tensor_tensor(out=PJ[:, tile:tile + 2, :], in0=PJ[:, tile:tile + 2, :],
                                             scalar=PR[:, QKG[n]:QKG[n] + 1], in1=NR[:, :, :],
                                             op0=ALU.mult, op1=ALU.mult)
                    dve.drain().then_inc(S["qk_normed"], 1)
                for t in range(3):
                    n = P if t < 2 else SMP
                    if t == 0:
                        dve.wait_ge(S["vt_done"], 3)
                    dve.tensor_copy(VRF[0:n, 512 * t:512 * t + 512], bank([1, 6, 7][t])[0:n, :])
                    dve.tensor_copy(GR[0:n, t, :], bank(0)[0:n, 32 * t:32 * t + 24])
                    dve.drain().then_inc(S["vr_ready"], 1)
                for g in range(GQA):
                    for k in range(NKV):
                        at_ = 3 * (GQA * k + g)
                        dve.tensor_copy(GS[32 * g:32 * g + 32, k, :], GR[0:SMP, 2, at_:at_ + 3])
                with dve.Fori(0, 2) as i:
                    for s in range(2):
                        dve.wait_ge(S["glu_sig"], 2 * i + s + 1)
                        tt(HC[:, bass.ds(4 * i + 2 * s, 2), :], ZB[:, bass.ds(4 * i + 2 * s, 2), :], (NV, NR)[s][:, :, :], ALU.mult)\
                            .then_inc(S["glu_evac"], 1)
                def pre(k, n, w, first):
                    dve.wait_ge(S["conv_done"], n)
                    if first:
                        dve.tensor_copy(HID[k][:, 0:w], bank(k)[:, 0:w])
                    else:
                        dve.wait_ge(S["w2_done"], n - 2)
                        dve.tensor_copy(c_hb, bank(k)[:, 256:512])
                        dve.drain()
                        tt(HID[k].rearrange("p (h c) -> p h c", h=2),
                           bank(k)[:, 0:256].rearrange("p (h c) -> p h c", h=2)[:, :, 0:NCMP],
                           c_hb.rearrange("p (h c) -> p h c", h=2)[:, :, 1:128], ALU.add)
                    dve.drain().then_inc(S["hid_pre"], 1)
                    dve.drain().then_inc(S["conv_evac"], 1)

                dve.wait_ge(S["glu_evac"], 6)
                for k in range(2):
                    pre(k, k + 1, 2 * NCMP_P, True)
                dve.wait_ge(S["w2_done"], 1)
                dve.tensor_copy(CKP, bank(2)[:, 0:2 * NCMP_P].rearrange("p (h c) -> p h c", h=2)).then_inc(S["ck_evac"], 1)
                dve.wait_ge(S["w2_done"], 2)
                dve.tensor_copy(CVP[0:NCMP_P], bank(3)[0:NCMP_P, 0:256].rearrange("p (h d) -> p h d", h=2))\
                    .then_inc(S["ck_evac"], 1)
                with dve.Fori(0, NB) as b:
                    for k in range(2):
                        pre(k, b * 2 + k + 3, 2 * NCMP, False)
                    dve.wait_ge(S["w2_done"], b * 2 + 3)
                    dve.tensor_copy(ubuf[:, bass.ds(b * 254, 254)], bank(2)[:, 0:254]).then_inc(S["ck_evac"], 1)
                    dve.wait_ge(S["w2_done"], b * 2 + 4)
                    dve.tensor_copy(zbuf[0:NCMP, bass.ds(b * 256, 256)], bank(3)[0:NCMP, 0:256]).then_inc(S["ck_evac"], 1)
                flat = [v[:, :, :].rearrange("p a b -> p (a b)") for v in (NV, NR, SQ)]
                for n in range(5):
                    w = 508 if n < 4 else 2 * NCMP_P
                    v, r, t = (x[:, 0:w] for x in flat)
                    norm_var(dve, "ckn", n + 1, bank(4)[:, 0:w], v, HD)
                    norm_recip(dve, "ckn", n + 1, v, r, t)
                    c = ubuf[:, 508 * n:508 * n + w]
                    dve.scalar_tensor_tensor(out=c, in0=c, scalar=PR[:, C_KC:C_KC + 1], in1=r, op0=ALU.mult, op1=ALU.mult)
                    dve.drain().then_inc(S["ck_normed"], 1)
                d1, dcp, slh = const(K_D1), const(K_DCP), const(K_SLH)
                with dve.Fori(0, NQ) as n:
                    dve.wait_ge(S["ps_done"], 2 * n + 1)
                    dve.tensor_copy(QS, PJ[:, bass.ds(n + T_Q, 1), 0:SEQ].rearrange("p a (t s) -> p (a t) s", t=2))\
                        .then_inc(S["q_copied"], 1)
                    slope = slh[:, bass.ds(n, 1)]
                    for t in range(2):
                        w = P * (t + 1)
                        dve.wait_ge(S["ps_done"], 2 * n + t + 2)
                        dve.wait_ge(S["pt_done"], 2 * n + 1)
                        dist = d1[:, SEQ - w:SEQ].unsqueeze(1).to_broadcast([P, 2, w])
                        dve.scalar_tensor_tensor(out=SPR[:, t, 0:2, 0:w], in0=dist, scalar=slope,
                                                 in1=PS[t][:, 0, :].rearrange("p (b s) -> p b s", b=2)[:, :, 0:w],
                                                 op0=ALU.mult, op1=ALU.add)
                        dve.scalar_tensor_tensor(out=SPR[:, t, 2, 0:NCMP_P], in0=dcp[:, NCMP_P * t:NCMP_P * t + NCMP_P],
                                                 scalar=slope, in1=PS[t][:, 1, 0:NCMP_P], op0=ALU.mult, op1=ALU.add)
                        dve.drain()
                        dve.tensor_reduce(SM[:, 3 * t:3 * t + 2], SPR[:, t, 0:2, 0:w], AXX, ALU.max)
                        dve.tensor_reduce(SM[:, 3 * t + 2:3 * t + 3], SPR[:, t, 2, 0:NCMP_P], AXX, ALU.max)
                        dve.drain()
                        dve.tensor_scalar(SM[:, 3 * t:3 * t + 3], SM[:, 3 * t:3 * t + 3], -1e20, -1.0, ALU.max, ALU.mult)\
                            .then_inc(S["ps_max"], 1)
                    dve.drain().then_inc(S["ps_evac"], 1)
                    for t in range(2):
                        w = P * (t + 1)
                        dve.wait_ge(S["p_exp"], 2 * n + t + 1)
                        f = SM[:, 6 + 3 * t:9 + 3 * t]
                        dve.tensor_scalar(f, f, TINY, None, ALU.max)
                        dve.drain()
                        dve.reciprocal(f, f)
                        dve.drain()
                        tt(f[:, 0:2], f[:, 0:2], GR[:, t, bass.ds(3 * n + 1, 2)], ALU.mult)
                        tt(f[:, 2:3], f[:, 2:3], GR[:, t, bass.ds(3 * n, 1)], ALU.mult)
                        dve.drain()
                        for br in range(3):
                            v = SPR[:, t, br, 0:(w if br < 2 else NCMP_P)]
                            dve.tensor_scalar(v, v, f[:, br:br + 1], None, ALU.mult)
                        dve.drain().then_inc(S["p_ready"], 1)
                    for t in range(2):
                        dve.wait_ge(S["po_done"], 2 * n + t + 1)
                        dve.tensor_copy(HC[:, bass.ds(n + SC, 1), P * t:P * t + P].rearrange("p a s -> p (a s)"), bank(6)[:, 0:P])\
                            .then_inc(S["po_evac"], 1)
                dve.memset(QPF, 0.0)
                dve.drain()
                for k in range(NKV):
                    for g in range(GQA):
                        base = QPD[:, k, 0, 32 * g:32 * g + NT]
                        dst = bass.AP(base.tensor, base.offset, [list(base.ap[0]), [P + NT, NB], [1, NT]])
                        dve.tensor_copy(dst, PJ[:, T_Q + GQA * k + g, SEQ:TOK].rearrange("p (b t) -> p b t", b=NB))
                    dve.tensor_copy(QA[:, k, :].rearrange("p (g r) -> p g r", g=GQA), PJ[:, T_Q + GQA * k:T_Q + GQA * k + GQA, SEQ:TOK])
                dve.drain().then_inc(S["qpad_ready"], 1)
                ds_, dw, dc, slr = const(K_DS), const(K_DW), const(K_DC), const(K_SLR)

                def biased(out, dist, k, scores):
                    dve.scalar_tensor_tensor(out=out, in0=dist, scalar=slr[:, k:k + 1], in1=scores, op0=ALU.mult, op1=ALU.add)

                dve.wait_ge(S["cs_done"], 1)
                for k in range(NKV):
                    biased(SCM[:, k, :], dc, k, bank(k)[:, 0:NCMP])
                dve.drain()
                dve.tensor_reduce(SM[:, 0:2], SCM, AXX, ALU.max)
                dve.drain()
                dve.tensor_scalar(SM[:, 0:2], SM[:, 0:2], -1.0, None, ALU.mult).then_inc(S["c_max"], 1)
                dve.wait_ge(S["fresh_done"], 1)
                for k in range(NKV):
                    biased(SS[:, k, PAST:NS], ds_[:, PAST:NS], k, bank(7)[:, 64 * k:64 * k + 32])
                    biased(SW[:, k, WIN:NW], dw[:, WIN:NW], k, bank(7)[:, 64 * k + 32:64 * k + 64])
                dve.drain().then_inc(S["fresh_evac"], 1)
                dve.wait_ge(S["c_exp"], 1)
                dve.tensor_scalar(SM[:, 2:4], SM[:, 2:4], TINY, None, ALU.max)
                dve.drain()
                dve.reciprocal(SM[:, 2:4], SM[:, 2:4])
                dve.drain()
                for k in range(NKV):
                    dve.tensor_scalar(SCM[:, k, :], SCM[:, k, :], SM[:, 2 + k:3 + k], None, ALU.mult)
                dve.drain()
                dve.scalar_tensor_tensor(out=SCM, in0=SCM, scalar=TINY, in1=SCM, op0=ALU.is_ge, op1=ALU.mult)
                dve.drain().then_inc(S["c_prob"], 1)
                dve.memset(PPD, 0.0)
                dve.memset(SCR, 0.0)
                dve.drain()
                dve.wait_ge(S["gsum_done"], 1)
                dve.tensor_copy(PPD[:, 1:128], bank(6)[0:64, 0:NCMP])
                dve.drain()
                dve.tensor_reduce(SUM2[:, 0:32], PPD[:, 1:129].rearrange("p (j c) -> p j c", c=4), AXX, ALU.add)
                dve.tensor_reduce(SUM2[:, 32:64], PPD[:, 0:128].rearrange("p (j c) -> p j c", c=4), AXX, ALU.add)
                dve.drain()
                tt(SCR[:, 0:32], SUM2[:, 0:32], SUM2[:, 32:64], ALU.add)
                dve.drain()
                tt(SCR, SCR, const(K_FRC)[0:64, :], ALU.max)
                dve.drain()
                other = SCR.unsqueeze(1).to_broadcast([64, NBLK, NBLK])
                own = SCR.unsqueeze(2).to_broadcast([64, NBLK, NBLK])
                sel = [SEL3[:, n, :].rearrange("p (j i) -> p j i", j=NBLK) for n in range(3)]
                tt(sel[0], other, own, ALU.is_gt)
                tt(sel[1], other, own, ALU.is_equal)
                dve.drain()
                dve.wait_ge(S["tie_in"], 16)
                tt(sel[1], sel[1], sel[2], ALU.mult)
                dve.drain()
                tt(sel[0], sel[0], sel[1], ALU.add)
                dve.drain()
                dve.tensor_reduce(RNK, sel[0], AXX, ALU.add)
                dve.drain()
                dve.tensor_scalar(RNK, RNK, float(NSEL), MASKED, ALU.is_ge, ALU.mult)
                dve.drain()
                for g in range(GQA):
                    for k in range(NKV):
                        dve.tensor_copy(MB[32 * g:32 * g + 32, k, :], RNK[32 * k:32 * k + 32, 0:32])
                dve.drain().then_inc(S["ranked"], 1)
                with dve.Fori(0, 4) as g4:
                    dve.wait_ge(S["kgroup_done"], g4 + 1)
                    for k in range(NKV):
                        biased(SS[:, k, bass.ds(g4 * 512, 512)], ds_[:, bass.ds(g4 * 512, 512)], k, PS[1][:, k, :])
                    dve.drain().then_inc(S["kgroup_evac"], 1)
                for k in range(NKV):
                    v = SS[:, k, 0:PAST].rearrange("p (j s) -> p j s", s=SEL)
                    tt(v, v, MB[:, k, :].unsqueeze(2).to_broadcast([P, 32, SEL]), ALU.add)
                dve.wait_ge(S["kgroup_done"], 5)
                for k in range(NKV):
                    biased(SW[:, k, 0:WIN], dw[:, 0:WIN], k, PS[1][:, k, :])
                dve.drain().then_inc(S["kgroup_evac"], 1)
                dve.tensor_reduce(SM[:, 6:8], SS, AXX, ALU.max)
                dve.tensor_reduce(SM[:, 8:10], SW, AXX, ALU.max)
                dve.drain()
                dve.tensor_scalar(SM[:, 6:10], SM[:, 6:10], -1.0, None, ALU.mult).then_inc(S["sw_max"], 1)
                dve.wait_ge(S["gsum_done"], 1)
                for k in range(NKV):
                    dve.tensor_scalar(SCM[:, k, :], SCM[:, k, :], GS[:, k, 0:1], None, ALU.mult)
                dve.drain().then_inc(S["sw_ready"], 1)
                dve.wait_ge(S["sw_exp"], 1)
                f = SM[:, 10:14]
                dve.tensor_scalar(f, f, TINY, None, ALU.max)
                dve.drain()
                dve.reciprocal(f, f)
                dve.drain()
                for i in range(2):
                    tt(f[:, 2 * i:2 * i + 2], f[:, 2 * i:2 * i + 2], GS[:, :, 1 + i], ALU.mult)
                dve.drain()
                for i, v in enumerate((SS, SW)):
                    for k in range(NKV):
                        dve.tensor_scalar(v[:, k, :], v[:, k, :], f[:, 2 * i + k:2 * i + k + 1], None, ALU.mult)
                    dve.drain().then_inc(S["sw_ready"], 1)
                dve.wait_ge(S["so_done"], 1)
                for k in range(NKV):
                    dve.tensor_copy(HC[:, SC + GQA * k:SC + GQA * k + GQA, SEQ:TOK],
                                    PS[1][:, k, 0:P].rearrange("p (g r) -> p g r", g=GQA)).then_inc(S["so_evac"], 1)
                norm_all(dve, "sn", lambda c: HC[:, c, :], lambda c: HC[:, c, :], C_NSSM, SC)
                dve.drain()
                norm_all(dve, "an", lambda c: HC[:, SC + c, :], lambda c: HC[:, SC + c, :], C_NATT, SC, stat=5)
                with dve.Fori(0, 4) as i:
                    for s in range(2):
                        dve.wait_ge(used[s], i + 11)
                        v = XT[:, bass.ds(4 * i + 2 * s, 2), :]
                        tt(v, PS[s][:, :, 0:TOK], v, ALU.add).then_inc(S["out_evac"], 1)
                dve.drain()
                norm_all(dve, "fn", lambda c: XT[:, c, :], lambda c: HC[:, c, :], C_FFN, KC)
                dve.drain()
                with dve.Fori(0, MF // 2) as i:
                    for m in range(2):
                        dve.wait_ge(S["silu_ready"], 2 * i + m + 1)
                        tt(HT[:, bass.ds(4 * i + 2 * m, 2), :], PS[2 * m + 1][:, :, 0:TOK], (NV, NR)[m][:, :, :], ALU.mult)\
                            .then_inc(S["gu_evac"], 1)
                with dve.Fori(0, 4) as i:
                    for m in range(2):
                        dve.wait_ge(S["down_done"], 2 * i + m + 1)
                        v = XT[:, bass.ds(4 * i + 2 * m, 2), :]
                        tt(v, PS[m][:, :, 0:TOK], v, ALU.add).then_inc(S["down_evac"], 1)

        nc.all_engine_barrier(sems_to_clear=range(handles[0].num, handles[-1].num + 1))

    with nc.Block() as block:
        @block.sync
        def _(sp):
            sp.dma_start(T["y"], XT[:, :, :]).then_inc(S["y_out"], 16)
            sp.wait_ge(S["y_out"], 16)
    stack.close()


def arrays_of(v):
    def blocks(w, k, cols):
        n = w.shape[2] // cols
        return w.reshape(L, k, P, n, cols).transpose(0, 3, 2, 1, 4).reshape(L * n, P, k * cols)

    def feature_major(x):
        return x.reshape(x.shape[0], -1, P).transpose(2, 1, 0)

    def gain(g):
        return g.reshape(L, -1, P).transpose(0, 2, 1)

    pool = v["cache_cmp_kv"].shape[1]
    a = {"consts": constant_table()[0], "ties": tie_table()}
    x = np.concatenate([v["x_prompt"].reshape(SEQ, D_MODEL), v["x_sample"].reshape(SMP, D_MODEL)])
    a["x"] = feature_major(x)
    a["pages"] = v["page_table"].reshape(1, NB * NPG)
    a["w_in"] = blocks(v["w_in"][:, :, :NTILE * P], KC, 256)
    a["w_gates"] = v["w_in"][:, :, NTILE * P:].reshape(L, KC, P, 24).transpose(0, 2, 1, 3).reshape(L, P, KC * 24)
    a["w_glu"] = blocks(v["ssm_w_glu"], SC, 256)
    a["w_out"] = blocks(v["w_out"], KC, 256)
    gate, up = (blocks(v[n], KC, 256).reshape(L, MF, 1, P, KC * 256) for n in ("w_ffn_gate", "w_ffn_up"))
    a["w_gu"] = np.concatenate([gate, up], 2).reshape(L * 2 * MF, P, KC * 256)
    a["w_down"] = v["w_ffn_down"].reshape(L, 4, 11, P, 8, 256).transpose(0, 4, 1, 3, 2, 5).reshape(L * 32, P, 11 * 256)
    w1 = np.stack([v["cmp_w1_k"], v["cmp_w1_v"]], 1).reshape(L, 2, 32, HD, HD)
    a["cmp_w1"] = w1.transpose(0, 1, 3, 2, 4).reshape(L * 2, P, 32 * HD)
    a["cmp_w2"] = np.stack([v["cmp_w2_k"], v["cmp_w2_v"]], 2).reshape(L, P, 2 * HD)
    a["params"] = np.concatenate(
        [gain(v[n]) for n in ("norm_mix", "norm_ffn", "norm_ssm_out", "norm_attn_out")]
        + [gain(v["ssm_d"].reshape(L, -1))]
        + [v[n][:, :, None] for n in ("q_norm", "k_norm_slc", "k_norm_win", "k_norm_cmp", "cmp_b1_k", "cmp_b1_v")], 2)
    pair = lambda t: t.reshape(L, NPAIR, P).transpose(0, 2, 1)
    dt = np.broadcast_to(v["ssm_log_dt"][:, :, None], (L, 64, 64))
    a["lam"] = np.concatenate([pair(v["ssm_a_re"]), pair(v["ssm_a_im"]), pair(dt)], 2)
    b = np.zeros((L, 2, 64, 2, NPAIR, 2, 16), np.float32)
    c = np.zeros((L, 2, 64, NPAIR, 2, 2, 16), np.float32)
    for r, (nb, nc_) in enumerate([("ssm_b_re", "ssm_c_re"), ("ssm_b_im", "ssm_c_im")]):
        bb = v[nb].reshape(L, NPAIR, 2, 64, 16)
        cc = v[nc_].reshape(L, NPAIR, 2, 16, 64)
        for m in range(2):
            b[:, m, :, r, :, m, :] = bb[:, :, m].transpose(0, 2, 1, 3)
            c[:, m, :, :, r, m, :] = cc[:, :, m].transpose(0, 3, 1, 2)
    a["ssm_b"] = b.reshape(L, P, 2048)
    a["ssm_c"] = c.reshape(L, P, 2048)
    h0 = v["state_ssm"].reshape(L, NB, NPAIR, 2, 64, 2)
    a["ssm_h0"] = h0.transpose(0, 3, 4, 2, 5, 1).reshape(L, P, NPAIR * 2 * NB)
    cc = v["cache_cmp_kv"].reshape(L * pool, 8, 16, 2, 2, HD)
    a["cache_cmp"] = cc.transpose(0, 5, 3, 4, 2, 1).reshape(L * pool, P, 512)
    cs = v["cache_slc_kv"].reshape(L * pool, PAGE, 2, 2, HD)
    a["cache_slc_k"] = cs[:, :, :, 0].transpose(0, 3, 2, 1).reshape(L * pool, P, 256)
    a["cache_slc_v"] = cs[:, :, :, 1].reshape(L * pool, P, 256)
    w = v["state_win_kv"].reshape(L * NB, WIN, 2, 2, HD)
    a["win_k"] = w[:, :, :, 0].transpose(0, 3, 2, 1).reshape(L * NB, P, 1024)
    a["win_v"] = w[:, :, :, 1].reshape(L * NB, 4, P, 2, HD).transpose(0, 2, 1, 3, 4).reshape(L * NB, P, 1024)
    a["win_rows"] = v["state_win_kv"].reshape(L, NB, WIN, 512)
    return {n: np.ascontiguousarray(t) for n, t in a.items()}


OUTS = {"y": (P, KC, TOK), "kv_new": (L, P, 12 * TOK), "win_kept": (L, NB, WIN - NT, 512),
        "win_zeros": (L, P, 1024), "ssm_last": (L, P, NPAIR * 2 * 9)}


def kernel(**inputs):
    import concourse.bacc as _bacc
    from concourse.bass_utils import run_bass_kernel_spmd as _run

    nc = _bacc.Bacc("TRN2", target_bir_lowering=False, num_devices=1)
    arrays = arrays_of({k: np.asarray(x) for k, x in inputs.items()})
    T = {n: nc.dram_tensor(f"in_{n}", a.shape, mybir.dt.from_np(a.dtype), kind="ExternalInput").ap()
         for n, a in arrays.items()}
    T |= {n: nc.dram_tensor(f"out_{n}", s, F32, kind="ExternalOutput").ap() for n, s in OUTS.items()}
    build(nc, T)
    got = _run(nc, [{f"in_{n}": a for n, a in arrays.items()}], core_ids=[0]).results[0]
    y = got["out_y"].transpose(2, 1, 0).reshape(TOK, D_MODEL)
    new = got["out_kv_new"].reshape(L, P, 3, 2, 2, TOK).transpose(2, 0, 5, 4, 3, 1)
    rows_p = new[:, :, :SEQ].reshape(3, L, 1, SEQ, 2, 2, HD)
    rows_s = new[:, :, SEQ:].reshape(3, L, NB, NT, 2, 2, HD)
    zeros = got["out_win_zeros"].reshape(L, 1, WIN - SEQ, 2, 2, HD)
    kept = got["out_win_kept"].reshape(L, NB, WIN - NT, 2, 2, HD)
    last = got["out_ssm_last"].reshape(L, 2, 64, NPAIR, 2, 9).transpose(0, 5, 3, 1, 2, 4).reshape(L, 9, 64, 64, 2)
    out = (y[:SEQ].reshape(1, SEQ, D_MODEL), y[SEQ:].reshape(NB, NT, D_MODEL), rows_p[0], rows_p[1],
           np.concatenate([zeros, rows_p[2]], 2), last[:, :1], rows_s[0], rows_s[1],
           np.concatenate([kept, rows_s[2]], 2), last[:, 1:])
    return tuple(np.ascontiguousarray(o) for o in out)
```

```python
from contextlib import ExitStack

import numpy as np

import concourse.bass as bass
from concourse import mybir

F32 = mybir.dt.float32
F32R = mybir.dt.float32r
I32 = mybir.dt.int32
ALU = mybir.AluOpType
ACT = mybir.ActivationFunctionType
AXX = mybir.AxisListType.X

P = 128
L = 2
D_MODEL, SEQ, NB, NT = 2048, 256, 8, 4
SMP = NB * NT
TOK = SEQ + SMP
PAST, PAGE, NPG, WIN = 2048, 128, 16, 512
KC = D_MODEL // P
D_FF = 5632
MF = D_FF // 256
NQ, NKV, GQA, HD = 8, 2, 4, 128
SC = 8
NCMP, NCMP_P = 127, 15
NBLK, NSEL, SEL = 33, 16, 64
CH = 16
NPAIR, QP = 32, 8
EPS = 1e-6
SCALE = HD ** -0.5
TINY = 1.1754943508222875e-38
MASKED = -1e30
FORCED = 1e4
STEP = 2 * TOK

T_Q, T_KC, T_VC, T_KS, T_VS, T_KW, T_VW, NTILE = 8, 16, 18, 20, 22, 24, 26, 28
C_MIX, C_FFN, C_NSSM, C_NATT, C_D, C_QN, C_KS, C_KW, C_KC, C_B1, NPAR = 0, 16, 32, 40, 48, 56, 57, 58, 59, 60, 62
K_ID, K_ONE, K_DS, K_DW, K_DC, K_DCP, K_D1, K_SLR, K_SLH, K_G, K_FRC = range(11)


def constant_table():
    r = np.arange(P)
    t, s = r[:, None], np.arange(SMP)[None, :]
    b, step, g = (r % 32) // NT, r % NT, r // 32
    big = -MASKED
    fresh = np.where((s // NT == b[:, None]) & (s % NT <= step[:, None]), step[:, None] - s % NT, big)
    past = PAST + step[:, None] - np.arange(PAST)[None, :]
    j = np.arange(WIN)[None, :]
    win = np.where(j > step[:, None], WIN + step[:, None] - j, big)
    c = np.arange(NCMP)[None, :]
    cmp_s = PAST + step[:, None] - 16 * c - 15.5
    cp = np.arange(NCMP_P)[None, :]
    cmp_p = [np.where(16 * cp + 31 <= t + 128 * n, t + 128 * n - 16 * cp - 15.5, big) for n in range(2)]
    causal = np.where(P + t - np.arange(SEQ)[None, :] >= 0, P + t - np.arange(SEQ)[None, :], big)
    slope = -(2.0 ** -np.arange(1, NQ + 1))
    rows = np.stack([slope[g], slope[4 + g]], 1)
    blk = np.arange(NBLK)
    force = np.where((blk == 0) | (blk >= 31), FORCED, 0.0)
    parts = [np.eye(P), np.ones((P, P)), np.concatenate([past, fresh], 1), np.concatenate([win, fresh], 1),
             cmp_s, np.concatenate(cmp_p, 1), causal, rows, np.tile(slope, (P, 1)),
             (r[:, None] % 32 == np.arange(32)[None, :]) * 1.0, np.tile(force, (P, 1))]
    at = np.cumsum([0] + [x.shape[1] for x in parts])
    return np.concatenate(parts, 1).astype(np.float32), [int(a) for a in at]


def tie_table():
    i = np.arange(NBLK)
    return np.tile((i[None, :] < i[:, None]).reshape(1, -1), (64, 1)).astype(np.float32)



SEMS = """consts_in x_in pages_in zero_set zero_out
params_in ssm_in gate_w_in w2_in slot0_full slot1_full slot0_used slot1_used slot0_freed slot1_freed wh_ready wl_ready split_used x_hi x_lo
mix_sq mix_stat mix_var mix_root mix_normed
lam_dt lam_xr lam_mag lam_sin bbar_ready bbar_turned bbar_evac c_slot bu_done bu_evac scan_done
state_kept y_done y_evac z_ready proj_evac gates_done gates_sig states_out
gated_step glu_done glu_sig glu_evac
qk_sq qk_stat qk_var qk_root qk_normed kv_out vt_done vr_ready qgain
cache0_full cache1_full cache0_used cache1_used conv_done conv_evac hid_pre hid_ready w2_done ck_evac
ckn_sq ckn_stat ckn_var ckn_root ck_normed
q_copied ps_done ps_max p_exp p_ready pt_done pt_evac po_done po_evac
qpad_ready cs_done cs_ready c_max c_exp c_prob gsum_done tie_in ranked gates_rows
kring0_more kring1_more kring2_more kring3_more kring0_full kring1_full kring2_full kring3_full kring_free kgroup_done kgroup_evac fresh_done fresh_evac
sw_max sw_exp sw_ready st_done st_evac
vbuf0_more vbuf1_more vbuf0_full vbuf1_full vwin0_full vwin1_full vring_free so_done so_evac
sn_sq sn_stat sn_var sn_root sn_normed an_sq an_stat an_var an_root an_normed
out_step out_evac fn_sq fn_stat fn_var fn_root fn_normed
gu_done silu_ready gu_evac down_done down_evac win_copied x_out y_out""".split()


def build(nc, T):
    _, at = constant_table()
    stack = ExitStack()
    handles = [nc.alloc_semaphore(n) for n in SEMS]
    assert [h.num for h in handles] == list(range(handles[0].num, handles[0].num + len(SEMS)))
    S = dict(zip(SEMS, handles))

    def sb(name, shape, dt=F32):
        return stack.enter_context(nc.sbuf_tensor(name, shape, dt))

    CT = sb("consts", [P, at[-1]])

    def const(i):
        return CT[:, at[i]:at[i + 1]]
    ident, ones = const(K_ID), const(K_ONE)
    XT = sb("residual", [P, KC, TOK])
    WR = sb("weight_slots", [P, 2, 16, 256])
    HC = sb("normed", [P, KC, TOK])
    PR = sb("params", [P, NPAR])
    SQ = sb("squares", [P, 2, TOK])
    NV = sb("norm_var", [P, 2, TOK])
    NR = sb("norm_rstd", [P, 2, TOK])
    PG = sb("page_numbers", [1, NB * NPG], I32)
    SM = sb("smalls", [P, 64])
    HT_SIZE, SPLIT = 2 * MF * TOK, 8 * 256
    with ExitStack() as late:
        XH = late.enter_context(nc.sbuf_tensor("normed_hi", [P, KC, TOK], F32R))
        XL = late.enter_context(nc.sbuf_tensor("normed_lo", [P, KC, TOK], F32R))
        WH = late.enter_context(nc.sbuf_tensor("weights_hi", [P, 2, SPLIT], F32R))
        WL = late.enter_context(nc.sbuf_tensor("weights_lo", [P, 2, SPLIT], F32R))
        HT = late.enter_context(nc.sbuf_tensor("ffn_hidden", [P, 2 * MF, TOK], F32))
    PJ = sb("projected", [P, NTILE, TOK])
    ZB = sb("ssm_out", [P, SC, TOK])
    W2 = sb("cmp_w2", [P, 2, HD])
    GT = sb("gates_t", [24, TOK])
    GR = sb("gates_rows", [P, 3, 24])
    GS = sb("gates_sample", [P, NKV, 3])
    VRF = sb("v_rows", [P, 3 * 2 * 2 * HD])
    VR = VRF[:, :].rearrange("p (t b h d) -> p t b h d", t=3, b=2, h=2)
    WG = VRF[:, 0:KC * 24].rearrange("p (k x) -> p k x", k=KC)
    ARENA = 17800
    AR = sb("arena", [P, ARENA])
    PS = [stack.enter_context(nc.psum_tensor(f"banks{i}", [P, 2, 512], F32)) for i in range(4)]

    def bank(i):
        return PS[i // 2][:, i % 2, :]

    def carve(sizes):
        out, o = [], 0
        for n in sizes:
            out.append(AR[:, o:o + n])
            o += n
        assert o <= ARENA, o
        return out

    s_hs, s_bn, s_cb, s_bbn, s_bbs, s_cbs, s_t1, s_t2, s_pwr, s_pwi, s_h0, s_hl, s_ca, s_c1, s_c2, s_lam = carve(
        [QP * 2 * TOK, 2048, 2048, 512, 512, 512, 1920, 1920, 512, 512, 512, 576, 256, 256, 256, 26 * 32])
    HS = s_hs.rearrange("p (j r t) -> p j r t", j=QP, r=2)
    BN = s_bn.rearrange("p (r j x) -> p r j x", r=2, j=NPAIR)
    CB = s_cb.rearrange("p (j r x) -> p j r x", j=NPAIR, r=2)
    BBN = s_bbn.rearrange("p (r j x) -> p r j x", r=2, j=QP)
    BBS = s_bbs.rearrange("p (r t x) -> p r t x", r=2, t=2)
    CBS = s_cbs.rearrange("p (j r x) -> p j r x", j=QP, r=2)
    PWR = s_pwr.rearrange("p (j i) -> p j i", j=NPAIR)
    PWI = s_pwi.rearrange("p (j i) -> p j i", j=NPAIR)
    H0 = s_h0.rearrange("p (j r b) -> p j r b", j=NPAIR, r=2)
    HL = s_hl.rearrange("p (j r b) -> p j r b", j=NPAIR, r=2)
    CA = s_ca.rearrange("p (j r c) -> p j r c", j=QP, r=2)

    def lam(i, n=1):
        return s_lam[:, 32 * i:32 * (i + n)]
    c_t0, c_t1, c_hid, c_hb = carve([8192, 8192, 508, 256])
    CTB = [x.rearrange("p (g h k i c) -> p g h k i c", g=NPG, h=2, k=2, i=16) for x in (c_t0, c_t1)]
    HID = [c_hid[:, 254 * i:254 * i + 254] for i in range(2)]
    ubuf = PJ[:, 0:8, :].rearrange("p a b -> p (a b)")
    zbuf = ZB[:, :, :].rearrange("p a b -> p (a b)")
    CW = 2 * NCMP
    CKP = ubuf[:, 0:CW].rearrange("p (h c) -> p h c", h=2)[:, :, 0:NCMP_P]
    CK = ubuf[:, CW:CW * (NB + 1)].rearrange("p (b h c) -> p b h c", b=NB, h=2)
    CVP = zbuf[:, 0:256].rearrange("p (h d) -> p h d", h=2)
    CV = zbuf[:, 256:2304].rearrange("p (b h d) -> p b h d", b=NB, h=2)
    class Head:
        def __init__(self, j):
            buf = WR[:, 1, :, :].rearrange("p a b -> p (a b)")[:, 1824 * j:1824 * j + 1824]
            self.p1 = buf[:, 0:512].rearrange("p (b s) -> p b s", b=2)
            self.p0 = buf[:, 512:768].rearrange("p (b s) -> p b s", b=2)
            self.pc = buf[:, 768:798].rearrange("p (t s) -> p t s", t=2)
            self.pt = buf[:, 800:1568].rearrange("p (n s) -> p n s", n=6)
            self.ptc = buf[0:NCMP_P, 1568:1824]
            self.q = SQ[:, :, :].rearrange("p a b -> p (a b)")[:, 256 * j:256 * j + 256].rearrange("p (t s) -> p t s", t=2)
            self.s1, self.s0 = bank(4 * j), bank(4 * j + 1)
            self.m, self.d = SM[:, 16 * j:16 * j + 6], SM[:, 16 * j + 8:16 * j + 14]
    HEADS = [Head(0), Head(1)]
    NS, NW = PAST + SMP, WIN + SMP
    a_s, a_w, a_c, a_ring, a_qp, a_qa, a_pt = carve([2 * NS, 2 * NW, 2 * NCMP, 4096, 2048, 256, 2 * 23 * 128])
    SS = a_s.rearrange("p (k s) -> p k s", k=2)
    SW = a_w.rearrange("p (k s) -> p k s", k=2)
    SCM = a_c.rearrange("p (k s) -> p k s", k=2)
    KR = [a_ring[:, 1024 * n:1024 * n + 1024].rearrange("p (g h s) -> p g h s", g=4, h=2) for n in range(4)]
    vbufs = [(a_ring, a_qp[:, 0:1024]), (a_s, a_qp[:, 1024:2048])]
    VG = [[r[:, 1024 * n:1024 * n + 1024].rearrange("p (g h d) -> p g h d", g=4, h=2) for n in range(4)]
          + [w_.rearrange("p (g h d) -> p g h d", g=4, h=2)] for r, w_ in vbufs]
    QPF = a_qp
    QPD = a_qp.rearrange("p (k b r) -> p k b r", k=2, b=NB)
    QA = a_qa.rearrange("p (k r) -> p k r", k=2)
    PTS = a_pt.rearrange("p (n k r) -> p n k r", n=23, k=2)
    SEL3 = a_pt[0:64, 0:3267].rearrange("p (n a) -> p n a", n=3)
    PPD = a_pt[0:64, 3267:3399]
    SCR = a_pt[0:64, 3400:3433]
    SUM2 = a_pt[0:64, 3440:3504]
    RNK = a_pt[0:64, 3510:3543]
    MB = a_pt[:, 3550:3614].rearrange("p (k j) -> p k j", k=2)

    J_IN, J_GLU, J_W1, J_OUT, J_GU, J_DN = 0, 14, 18, 20, 28, 72
    full = [S["slot0_full"], S["slot1_full"]]
    used = [S["slot0_used"], S["slot1_used"]]
    freed = [S["slot0_freed"], S["slot1_freed"]]
    U_GU, U_DN = 16, 16 + 88
    DR = 11

    with nc.Block() as block:
        @block.sync
        def _(sp):
            sp.dma_start(CT[:, :], T["consts"]).then_inc(S["consts_in"], 16)
            sp.dma_start(XT[:, :, :], T["x"]).then_inc(S["x_in"], 16)
            sp.dma_start(PG[:, :], T["pages"]).then_inc(S["pages_in"], 16)
            sp.wait_ge(S["zero_set"], 1)
            for i in range(L):
                sp.dma_start(T["win_zeros"][i], AR[:, 0:1024]).then_inc(S["zero_out"], 16)
            sp.wait_ge(S["consts_in"], 16)
            sp.wait_ge(S["x_in"], 16)
            sp.wait_ge(S["pages_in"], 16)
            sp.wait_ge(S["zero_out"], 16 * L)

        @block.vector
        def _(dve):
            dve.memset(AR[:, 0:1024], 0.0).then_inc(S["zero_set"], 1)
    nc.all_engine_barrier(sems_to_clear=range(handles[0].num, handles[-1].num + 1))

    with nc.Fori(0, L) as lay:
        with nc.Block() as block:
            def pages(eng, name, ring, n, i, free, count, sem):
                first = 0 if eng is nc.sync else 2
                p = [eng.value_load(PG[0:1, bass.ds(i + first + g, 1)], min_val=0, max_val=159) for g in range(2)]
                eng.wait_ge(free, count)
                for g in range(2):
                    at_ = 1024 * n + (first + g) * 256
                    eng.dma_start(ring[:, at_:at_ + 256],
                                  T[name][bass.ds(lay * 160 + p[g], 1)].rearrange("a p x -> p (a x)")).then_inc(sem, 16)

            def values(eng, i, hb, half):
                b = 2 * i + hb
                for n in range(4):
                    if n == 0:
                        eng.wait_ge(*((S["st_done"], 12) if hb else (S["kring_free"], 44)))
                    pages(eng, "cache_slc_v", vbufs[hb][0], n, b * NPG + n * 4, S["vring_free"], b * 5 + n + 1,
                          S[f"vbuf{hb}_{half}"])

            @block.sync
            def _(sp):
                def slot_load(n, later, dst, src):
                    if n >= 2 or not isinstance(later, int):
                        sp.wait_ge(used[n % 2], n // 2 + later)
                    sp.dma_start(dst, src).then_inc(full[n % 2], 16)

                def slot(n, k=16):
                    return WR[:, n % 2, 0:k, :].rearrange("p k x -> p (k x)")

                def row(name, i):
                    return T[name][bass.ds(i, 1)].rearrange("a p x -> p (a x)")

                def stream(name, first, count, k=16, peel=0, skip=0):
                    for i in range(peel):
                        slot_load(first + i, 0, slot(i, k), row(name, lay * count + i))
                    with sp.Fori(peel // 2 + skip, count // 2) as i:
                        for s in range(2):
                            if first < J_OUT:
                                sp.wait_ge(used[s], first // 2 + i)
                            else:
                                sp.wait_ge(freed[s], (first - J_OUT) // 2 + i)
                            sp.dma_start(slot(s, k), row(name, lay * count + 2 * i + s)).then_inc(full[s], 16)

                stream("w_in", J_IN, 14, peel=2)
                sp.dma_start(T["win_kept"][bass.ds(lay, 1)].rearrange("a b r x -> (a b) r x"),
                             T["win_rows"][bass.ds(lay, 1)].rearrange("a b r x -> (a b) r x")[:, NT:WIN, :])\
                    .then_inc(S["win_copied"], 16)
                stream("w_glu", J_GLU, 4, k=8)
                for k in range(2):
                    slot_load(J_W1 + k, 0, slot(k), row("cmp_w1", lay * 2 + k))
                slot_load(J_OUT, 0, slot(0), row("w_out", lay * 8))
                sp.wait_ge(S["cache0_used"], 5)
                sp.wait_ge(S["cache1_used"], 5)
                for b in range(NB):
                    sp.wait_ge(S["kring_free"], b + 1)
                    sp.dma_start(a_ring[:, 1024 * (b % 4):1024 * (b % 4) + 1024],
                                 row("win_k", lay * NB + b)).then_inc(S[f"kring{b % 4}_full"], 16)
                with sp.Fori(0, 4) as g4:
                    for b in range(NB):
                        pages(sp, "cache_slc_k", a_ring, b % 4, g4 * 4 + b * NPG, S["kring_free"], g4 * 8 + b + 9, S[f"kring{b % 4}_full"])
                sp.wait_ge(S["kring_free"], 44)
                with sp.Fori(0, NB // 2) as i:
                    for hb in range(2):
                        values(sp, i, hb, "full")
                        b = 2 * i + hb
                        sp.wait_ge(S["vring_free"], b * 5 + 5)
                        sp.dma_start(vbufs[hb][1], row("win_v", lay * NB + b)).then_inc(S[f"vwin{hb}_full"], 16)
                sp.wait_ge(S["po_done"], NQ)
                sp.wait_ge(used[1], J_OUT // 2)
                sp.dma_start(slot(1), row("w_out", lay * 8 + 1)).then_inc(full[1], 16)
                stream("w_out", J_OUT, 8, skip=1)
                stream("w_gu", J_GU, 44)
                stream("w_down", J_DN, 2 * DR)
                sp.wait_ge(S["win_copied"], 16)

            @block.gpsimd
            def _(pool):
                def row(name, i):
                    return T[name][bass.ds(i, 1)].rearrange("a p x -> p (a x)")
                pool.dma_start(PR[:, :], row("params", lay)).then_inc(S["params_in"], 16)
                pool.dma_start(lam(0, 3), row("lam", lay)).then_inc(S["ssm_in"], 16)
                pool.dma_start(s_bn, row("ssm_b", lay)).then_inc(S["ssm_in"], 16)
                pool.dma_start(s_cb, row("ssm_c", lay)).then_inc(S["ssm_in"], 16)
                pool.dma_start(s_h0, row("ssm_h0", lay)).then_inc(S["ssm_in"], 16)
                pool.dma_start(VRF[:, 0:KC * 24], row("w_gates", lay)).then_inc(S["gate_w_in"], 16)
                pool.dma_start(W2[:, :, :].rearrange("p k d -> p (k d)"), row("cmp_w2", lay)).then_inc(S["w2_in"], 16)
                with pool.Fori(0, 4) as q:
                    pool.wait_ge(S["scan_done"], q + 1)
                    pool.tensor_copy(HL[:, bass.ds(q * QP, QP), :, 0:1], HS[:, :, :, SEQ - 1:SEQ])
                    pool.tensor_copy(HL[:, bass.ds(q * QP, QP), :, 1:9], HS[:, :, :, SEQ + NT - 1:TOK:NT])\
                        .then_inc(S["state_kept"], 2)
                pool.wait_ge(S["state_kept"], 8)
                pool.dma_start(row("ssm_last", lay), s_hl).then_inc(S["states_out"], 16)
                pool.wait_ge(S["qk_normed"], 6)
                pool.wait_ge(S["proj_evac"], 16)
                pool.dma_start(row("kv_new", lay), PJ[:, T_KC:NTILE, :].rearrange("p m t -> p (m t)"))\
                    .then_inc(S["kv_out"], 16)
                pool.wait_ge(S["states_out"], 16)
                pool.wait_ge(S["y_evac"], 5)
                pool.wait_ge(S["scan_done"], 4)
                with pool.Fori(0, NB // 2) as b2:
                    for h in range(2):
                        with pool.Fori(0, NPG) as g:
                            pool.wait_ge(S[f"cache{h}_used"], b2 + 1)
                            page = pool.value_load(PG[0:1, bass.ds(b2 * 2 * NPG + h * NPG + g, 1)], min_val=0, max_val=159)
                            pool.dma_start(AR[:, bass.ds(8192 * h + g * 512, 512)], row("cache_cmp", lay * 160 + page))\
                                .then_inc(S[f"cache{h}_full"], 16)
                pool.wait_ge(S["cache0_used"], 5)
                pool.wait_ge(S["cache1_used"], 5)
                pool.dma_start(SEL3[:, 2, :], T["ties"]).then_inc(S["tie_in"], 16)
                pool.wait_ge(S["ck_normed"], NB + 1)
                with pool.Fori(0, NQ // 2) as i:
                    for j in range(2):
                        pool.wait_ge(S["ps_done"], 2 * i + j + 1)
                        pool.tensor_copy(HEADS[j].q, PJ[:, bass.ds(2 * i + j + T_Q, 1), 0:SEQ]
                                         .rearrange("p a (t s) -> p (a t) s", t=2)).then_inc(S["q_copied"], 1)
                    for b in range(NB):
                        pages(pool, "cache_slc_k", a_ring, b % 4, i * 4 + b * NPG, S["kring_free"], i * 8 + b + 9, S[f"kring{b % 4}_more"])
                with pool.Fori(0, NB // 2) as i:
                    for hb in range(2):
                        values(pool, i, hb, "more")
                for n in range(8):
                    pool.wait_ge(S["x_hi"], n + 1)
                    c = slice(4 * (n % 4), 4 * (n % 4) + 4)
                    pool.tensor_tensor(XL[:, c, :], HC[:, c, :], XH[:, c, :].bitcast(F32), ALU.subtract).then_inc(S["x_lo"], 1)
                for n, v in [("params_in", 16), ("ssm_in", 64), ("gate_w_in", 16), ("w2_in", 16), ("states_out", 16),
                             ("kv_out", 16), ("tie_in", 16), ("cache0_full", 1024), ("cache1_full", 1024)] \
                        + [(f"kring{i}_more", 256) for i in range(4)] + [(f"vbuf{i}_more", 512) for i in range(2)]:
                    pool.wait_ge(S[n], v)
                pool.dma_reset(range(handles[0].num, handles[-1].num + 1))

            def norm_squares(act, n, src, count, before=None):
                for c in range(count):
                    if c >= 2:
                        act.wait_ge(S[n + "_stat"], c - 1)
                    act.activation(SQ[:, c % 2, :], src(c), ACT.Square).then_inc(S[n + "_sq"], 1)

            def norm_sum(pe, n, count, dst):
                for c in range(count):
                    pe.wait_ge(S[n + "_sq"], c + 1)
                    pe.matmul(dst, ones, SQ[:, c % 2, :], start=c == 0, stop=c == count - 1).then_inc(S[n + "_stat"], 1)

            def norm_root(act, n, k, v, r):
                act.wait_ge(S[n + "_var"], k)
                act.activation(r, v, ACT.Sqrt).then_inc(S[n + "_root"], 1)

            def norm_var(dve, n, k, stat, v, width):
                dve.wait_ge(S[n + "_stat"], k)
                dve.tensor_scalar(v, stat, 1.0 / width, EPS, ALU.mult, ALU.add).then_inc(S[n + "_var"], 1)

            def norm_recip(dve, n, k, v, r, t):
                dve.wait_ge(S[n + "_root"], k)
                dve.reciprocal(r, r)
                dve.drain()
                dve.tensor_tensor(t, r, r, ALU.mult)
                dve.drain()
                dve.scalar_tensor_tensor(out=t, in0=t, scalar=-0.5, in1=v, op0=ALU.mult, op1=ALU.mult)
                dve.drain()
                dve.scalar_tensor_tensor(out=r, in0=t, scalar=1.5, in1=r, op0=ALU.add, op1=ALU.mult)
                dve.drain()

            def norm_all(dve, n, src, dst, gain, count, stat=4):
                norm_var(dve, n, count, bank(stat)[:, 0:TOK], NV[:, 0, :], count * P)
                norm_recip(dve, n, 1, NV[:, 0, :], NR[:, 0, :], NV[:, 1, :])
                for c in range(count):
                    dve.scalar_tensor_tensor(out=dst(c), in0=src(c), scalar=PR[:, gain + c:gain + c + 1],
                                             in1=NR[:, 0, :], op0=ALU.mult, op1=ALU.mult).then_inc(S[n + "_normed"], 1)

            QK = [T_Q, T_Q + 2, T_Q + 4, T_Q + 6, T_KS, T_KW]
            QKG = [C_QN] * 4 + [C_KS, C_KW]

            @block.tensor
            def _(pe):
                for n, v in (("cache0_used", 1), ("cache1_used", 1), ("ps_done", 2), ("pt_done", 2)):
                    pe.drain().then_inc(S[n], v)
                norm_sum(pe, "mix", KC, bank(4)[:, 0:TOK])

                def products(s, wait, rhs, banks_, k=16, start=True, stop=True, first=0):
                    pe.wait_ge(full[s], wait)
                    for m in range(2):
                        for c in range(k):
                            mm = pe.matmul(banks_[:, m, 0:TOK], WR[:, s, c, 128 * m:128 * m + 128], rhs(first + c),
                                           start=start and c == 0, stop=stop and c == k - 1)
                    mm.then_inc(used[s], 1)

                def hc(c):
                    return HC[:, c, :]

                pe.wait_ge(S["mix_normed"], KC)
                with pe.Fori(0, 2) as i:
                    for s in range(2):
                        pe.wait_ge(S["proj_evac"], 2 * i + s + 1)
                        products(s, 16 + 16 * i, hc, PS[s])

                def turn_b(n):
                    pe.wait_ge(S["bbar_ready"], n)
                    for r in range(2):
                        for t in range(2):
                            mm = pe.transpose(bank(4)[:, 256 * r + 128 * t:256 * r + 128 * t + 128],
                                              BBN[:, r, 4 * t:4 * t + 4, :].rearrange("p j x -> p (j x)"), ident)
                    mm.then_inc(S["bbar_turned"], 1)

                def bu(q, n):
                    pe.wait_ge(S["bbar_evac"], n)
                    for j in range(QP):
                        o = 32 * (j % 4)
                        for r in range(2):
                            k = 2 * j + r
                            pe.wait_ge(S["bu_evac"], q * 16 + k + 1)
                            pe.matmul(bank(6 + k % 2)[:, 0:TOK], BBS[o:o + 32, r, j // 4, :],
                                      NV[o:o + 32, j // 4, :],
                                      start=True, stop=True).then_inc(S["bu_done"], 1)

                def y_out(n, b_read):
                    pe.wait_ge(S["scan_done"], n)
                    pe.wait_ge(S["c_slot"], n)
                    pe.wait_ge(S["bbar_evac"], b_read)
                    for j in range(QP):
                        o = 32 * (j % 4)
                        for r in range(2):
                            mm = pe.matmul(PS[2][o:o + 32, j // 4, 0:TOK], CBS[:, j, r, :], HS[:, j, r, :],
                                           start=r == 0, stop=r == 1, tile_position=(0, o))
                    mm.then_inc(S["y_done"], 1)

                pe.wait_ge(S["proj_evac"], 6)
                turn_b(1)
                bu(0, 1)
                with pe.Fori(0, 3) as q:
                    pe.wait_ge(S["y_evac"], q + 1)
                    turn_b(q + 2)
                    for s in range(2):
                        pe.wait_ge(S["proj_evac"], 2 * q + s + 5)
                        products(s, 48 + 16 * q, hc, PS[s])
                    y_out(q + 1, q + 2)
                    bu(q + 1, q + 2)
                with pe.Fori(0, 2) as i:
                    for s in range(2):
                        pe.wait_ge(S["proj_evac"], 2 * i + s + 11)
                        products(s, 96 + 16 * i, hc, PS[s])
                pe.wait_ge(S["gate_w_in"], 16)
                pe.wait_ge(S["proj_evac"], 16)
                for c in range(KC):
                    mm = pe.matmul(bank(0)[0:24, 0:TOK], WG[:, c, :], HC[:, c, :], start=c == 0, stop=c == KC - 1)
                mm.then_inc(S["gates_done"], 1)
                y_out(4, 4)
                pe.wait_ge(S["y_evac"], 5)
                for n in range(6):
                    pe.wait_ge(S["qk_sq"], n + 1)
                    if n:
                        pe.wait_ge(S["qk_var"], n)
                    for m in range(2):
                        mm = pe.matmul(PS[2][:, m, 0:TOK], ones, SQ[:, m, :], start=True, stop=True)
                    mm.then_inc(S["qk_stat"], 1)
                pe.wait_ge(S["gates_sig"], 1)
                pe.wait_ge(S["bu_evac"], 66)
                for t in range(3):
                    n = P if t < 2 else SMP
                    b_ = bank([1, 6, 7][t])
                    for i, tile in enumerate([T_VS, T_VS + 1, T_VW, T_VW + 1]):
                        pe.transpose(b_[0:n, 128 * i:128 * i + 128], PJ[:, tile, P * t:P * t + n], ident)
                    pe.transpose(bank(0)[0:n, 32 * t:32 * t + 24], GT[0:24, P * t:P * t + n], ident[0:24, 0:24])\
                        .then_inc(S["vt_done"], 1)
                pe.wait_ge(S["z_ready"], 1)
                pe.wait_ge(S["vr_ready"], 3)
                with pe.Fori(0, 2) as i:
                    for s in range(2):
                        pe.wait_ge(S["glu_evac"], 2 * i + s + 1)
                        products(s, 128 + 16 * i, lambda c: ZB[:, c, :], PS[s], k=8)
                pe.wait_ge(S["glu_evac"], 6)
                pe.wait_ge(S["w2_in"], 16)
                for k in range(2):
                    pe.wait_ge(full[k], 16 * (J_W1 // 2 + 1))
                W1 = [WR[:, k, :, :].rearrange("p a b -> p (a b)").rearrange("p (l h) -> p l h", h=HD) for k in range(2)]
                for k in range(2):
                    for l in range(32):
                        mm = pe.matmul(bank(k)[:, 0:2 * NCMP_P], W1[k][:, l, :],
                                       PJ[:, T_KC + 2 * k:T_KC + 2 * k + 2, l:l + 16 * (NCMP_P - 1) + 1:16],
                                       start=l == 0, stop=l == 31)
                    mm.then_inc(S["conv_done"], 1)

                def second(k, item):
                    pe.wait_ge(S["hid_ready"], 2 * item + k + 1)
                    pe.wait_ge(S["ck_evac"], 2 * item + k + 1)
                    if k == 0:
                        mm = pe.matmul(bank(2)[:, 0:CW], W2[:, 0, :], HID[0], start=True, stop=True)
                    else:
                        for h in range(2):
                            mm = pe.matmul(bank(3)[0:NCMP, 128 * h:128 * h + 128], HID[1][:, NCMP * h:NCMP * h + NCMP],
                                           W2[:, 1, :], start=True, stop=True)
                    mm.then_inc(S["w2_done"], 1)

                def ck_sum(item):
                    pe.wait_ge(S["ckn_sq"], item + 1)
                    pe.matmul(bank(4)[:, 0:CW], ones, SQ[:, 0, 0:CW], start=True, stop=True).then_inc(S["ckn_stat"], 1)

                second(0, 0)
                with pe.Fori(0, NB // 2) as b2:
                    for hb in range(2):
                        item = 2 * b2 + hb
                        pe.wait_ge(S[f"cache{hb}_full"], b2 * 256 + 256)
                        for k in range(2):
                            pe.wait_ge(S["conv_evac"], 2 * item + k + 1)
                            for half in range(2):
                                for i in range(16):
                                    mm = pe.matmul(bank(k)[:, 256 * half:256 * half + 256]
                                                   .rearrange("p (h g c) -> p h g c", h=2, g=NPG),
                                                   W1[k][:, 16 * half + i, :],
                                                   CTB[hb][:, :, :, k, i, :].rearrange("p g h c -> p h g c"),
                                                   start=i == 0, stop=i == 15)
                            mm.then_inc(S["conv_done"], 1)
                            if k == 0:
                                second(1, item)
                                ck_sum(item)
                        pe.drain().then_inc(S[f"cache{hb}_used"], 1)
                        second(0, item + 1)
                second(1, NB)
                ck_sum(NB)
                for s in range(2):
                    pe.drain().then_inc(used[s], 1)
                pe.drain().then_inc(S["split_used"], 2)
                pe.drain().then_inc(S["kring_free"], 4)
                pe.drain().then_inc(S["vring_free"], 10)
                pe.wait_ge(S["ck_normed"], NB + 1)
                pe.wait_ge(S["qpad_ready"], 1)
                for k in range(NKV):
                    for b in range(NB):
                        mm = pe.matmul(bank(k)[:, 0:NCMP], QPD[:, k, b, :], CK[:, b, k, :], start=b == 0, stop=b == NB - 1)
                mm.then_inc(S["cs_done"], 1)
                for k in range(NKV):
                    pe.matmul(bank(7)[:, 64 * k:64 * k + 32], QA[:, k, :], PJ[:, T_KS + k, SEQ:TOK], start=True, stop=True)
                    mm = pe.matmul(bank(7)[:, 64 * k + 32:64 * k + 64], QA[:, k, :], PJ[:, T_KW + k, SEQ:TOK],
                                   start=True, stop=True)
                mm.then_inc(S["fresh_done"], 1)

                def keys(b, count, more=None):
                    pe.wait_ge(S[f"kring{b % 4}_full"], count)
                    if more is not None:
                        pe.wait_ge(S[f"kring{b % 4}_more"], more)
                    for k in range(NKV):
                        mm = pe.matmul(PS[1][:, k, :].rearrange("p (g s) -> p g s", g=4), QPD[:, k, b, :],
                                       KR[b % 4][:, :, k, :], start=b == 0, stop=b == NB - 1)
                    mm.then_inc(S["kring_free"], 1)
                    if b == NB - 1:
                        pe.drain().then_inc(S["kgroup_done"], 1)

                pe.wait_ge(S["kgroup_evac"], 1)
                for b in range(NB):
                    keys(b, 16 * (b // 4 + 1))
                pe.wait_ge(S["c_prob"], 1)
                for k in range(NKV):
                    mm = pe.matmul(bank(6)[32 * k:32 * k + 32, 0:NCMP], const(K_G), SCM[:, k, :], start=True, stop=True,
                                   tile_position=(0, 32 * k))
                mm.then_inc(S["gsum_done"], 1)

                def scores(n, h, k):
                    pe.wait_ge(S["q_copied"], n + 1)
                    pe.wait_ge(S["po_evac"], n + 1)
                    for t in range(2):
                        w = P * (t + 1)
                        for br, tile in enumerate((T_KS, T_KW)):
                            pe.matmul((h.s0, h.s1)[t][:, w * br:w * br + w], h.q[:, t, :], PJ[:, tile + k, 0:w],
                                      start=True, stop=True)
                        mm = pe.matmul(h.s0[:, 256 + NCMP_P * t:256 + NCMP_P * t + NCMP_P], h.q[:, t, :], CKP[:, k, :],
                                       start=True, stop=True)
                    mm.then_inc(S["ps_done"], 1)

                def turn_p(n, h):
                    pe.wait_ge(S["p_ready"], n + 1)
                    pe.wait_ge(S["pt_evac"], n + 1)
                    for br in range(2):
                        pe.transpose(bank(6)[:, 256 * br:256 * br + P], h.p0[:, br, :], ident)
                        pe.transpose(bank(6)[:, 256 * br + P:256 * br + 256], h.p1[:, br, 0:P], ident)
                        pe.transpose(bank(7)[:, P * br:P * br + P], h.p1[:, br, P:SEQ], ident)
                    for t in range(2):
                        mm = pe.transpose(bank(7)[0:NCMP_P, 256 + P * t:256 + P * t + P], h.pc[:, t, :], ident)
                    mm.then_inc(S["pt_done"], 1)

                def weigh(n, h, k):
                    pe.wait_ge(S["pt_evac"], n + 2)
                    o = h.s1
                    pe.matmul(o[:, 0:SEQ], VR[:, 0, 0, k, :], h.pt[:, 0:2, :], start=True, stop=False, skip_group_check=True)
                    pe.matmul(o[:, P:SEQ], VR[:, 1, 0, k, :], h.pt[:, 4, :], start=False, stop=False, skip_group_check=True)
                    pe.matmul(o[:, P:SEQ], VR[:, 1, 1, k, :], h.pt[:, 5, :], start=False, stop=False, skip_group_check=True)
                    pe.matmul(o[:, 0:SEQ], VR[:, 0, 1, k, :], h.pt[:, 2:4, :], start=False, stop=False, skip_group_check=True)
                    pe.matmul(o[:, 0:SEQ], CVP[0:NCMP_P, k, :], h.ptc, start=False, stop=True, skip_group_check=True)\
                        .then_inc(S["po_done"], 1)

                for k in range(NKV):
                    with pe.Fori(0, 2) as i:
                        n, g4 = 2 * i + GQA * k, i + 2 * k
                        a, b_ = HEADS
                        scores(n, a, k)
                        scores(n + 1, b_, k)
                        pe.wait_ge(S["kgroup_evac"], g4 + 2)
                        for b in range(NB):
                            if b == 4:
                                turn_p(n, a)
                            if b == 6:
                                weigh(n, a, k)
                                turn_p(n + 1, b_)
                            keys(b, g4 * 64 + 32 * (b // 4) + 64, g4 * 64 + 32 * (b // 4) + 32)
                        weigh(n + 1, b_, k)
                banks_ = [0, 1, 4, 5, 6, 7]
                pe.wait_ge(S["ranked"], 1)
                pe.wait_ge(S["fresh_evac"], 1)
                pe.wait_ge(S["sw_ready"], 3)
                blocks = [(SS, x, P) for x in range(16)] + [(SS, 16, SMP)] + [(SW, x, P) for x in range(4)] \
                    + [(SW, 4, SMP)] + [(SCM, 0, NCMP)]
                for n in range(12):
                    if n >= 6:
                        pe.wait_ge(S["st_evac"], n - 5)
                    for m, (src, x, w) in enumerate(blocks[2 * n:2 * n + 2]):
                        for k in range(NKV):
                            mm = pe.transpose(bank(banks_[n % 6])[0:w, 256 * m + 128 * k:256 * m + 128 * k + 128],
                                              src[:, k, P * x:P * x + w], ident)
                    mm.then_inc(S["st_done"], 1)
                pe.wait_ge(S["st_evac"], 12)
                for k in range(NKV):
                    o = PS[1][:, k, 0:P]
                    pe.matmul(o, VR[0:SMP, 2, 0, k, :], PTS[0:SMP, 16, k, :], start=True, stop=False, skip_group_check=True)
                    pe.matmul(o, VR[0:SMP, 2, 1, k, :], PTS[0:SMP, 21, k, :], start=False, stop=False, skip_group_check=True)
                    for b in range(NB):
                        pe.matmul(o.rearrange("p (g r) -> p g r", g=GQA)[:, :, NT * b:NT * b + NT], CV[0:NCMP, b, k, :],
                                  PTS[0:NCMP, 22, k, :].rearrange("p (g r) -> p g r", g=GQA)[:, :, NT * b:NT * b + NT],
                                  start=False, stop=False, skip_group_check=True)
                with pe.Fori(0, NB // 2) as i:
                    for hb in range(2):
                        b = 2 * i + hb
                        for n in range(5):
                            if n == 0:
                                for half in ("full", "more"):
                                    pe.wait_ge(S[f"vbuf{hb}_{half}"], i * 128 + 128)
                            if n == 4:
                                pe.wait_ge(S[f"vwin{hb}_full"], i * 16 + 16)
                            for g in range(4):
                                blk = 4 * n + g if n < 4 else 17 + g
                                for k in range(NKV):
                                    mm = pe.matmul(PS[1][:, k, 0:P].rearrange("p (g r) -> p g r", g=GQA)[:, :, bass.ds(b * NT, NT)],
                                                   VG[hb][n][:, g, k, :],
                                                   PTS[:, blk, k, :].rearrange("p (g r) -> p g r", g=GQA)[:, :, bass.ds(b * NT, NT)],
                                                   start=False, stop=False, skip_group_check=True)
                            mm.then_inc(S["vring_free"], 1)
                pe.drain().then_inc(S["so_done"], 1)
                norm_sum(pe, "sn", SC, bank(4)[:, 0:TOK])
                norm_sum(pe, "an", SC, bank(5)[:, 0:TOK])
                pe.wait_ge(S["x_lo"], 4)
                def half(u, hf, outs, k, rhs, begin, more=None):
                    pe.wait_ge(S["wl_ready"], u + hf + 1)
                    w = len(outs) * P
                    for m, out in enumerate(outs):
                        if more is not None:
                            more(m)
                        for c in range(k):
                            col = slice(c * w + P * m, c * w + P * m + P)
                            for i, (wt, x) in enumerate(((WH, XH), (WH, XL), (WL, XH))):
                                mm = pe.matmul(out, wt[:, hf, col], x[:, rhs + c, :], start=begin and c == 0 and i == 0,
                                               stop=hf == 1 and c == k - 1 and i == 2, skip_group_check=True)
                    mm.then_inc(S["split_used"], 1)

                with pe.Fori(0, 4) as i:
                    for s in range(2):
                        pe.wait_ge(S["out_evac"], 2 * i + s + 1)
                        for hf in range(2):
                            half(4 * i + 2 * s, hf, [PS[s][:, m, 0:TOK] for m in range(2)], 8, 8 * hf, hf == 0)
                norm_sum(pe, "fn", KC, bank(4)[:, 0:TOK])
                pe.wait_ge(S["x_lo"], 8)
                with pe.Fori(0, MF // 2) as i:
                    for m in range(2):
                        pe.wait_ge(S["gu_evac"], 2 * i + m + 1)
                        for s in range(2):
                            for hf in range(2):
                                half(U_GU + 8 * i + 4 * m + 2 * s, hf, [PS[2 * m + s][:, t, 0:TOK] for t in range(2)], 8, 8 * hf, hf == 0)
                        pe.drain().then_inc(S["gu_done"], 1)
                pe.wait_ge(S["gu_evac"], MF + 2)
                for r in range(2):
                    def down(j, begin=False):
                        for hf in range(2):
                            half(U_DN + 2 * DR * r + 2 * j, hf, [bank(m)[:, 0:TOK] for m in range(8)], 2, 2 * hf, begin and hf == 0,
                                 (lambda m: pe.wait_ge(S["down_evac"], 4 * r + m // 2 + 1)) if begin and hf == 0 else None)
                    down(0, True)
                    with pe.Fori(0, DR // 2) as i:
                        for s in range(2):
                            down(2 * i + s + 1)
                    pe.drain().then_inc(S["down_done"], 1)

            @block.scalar
            def _(act):
                def evac(dst, src, sem, by=1):
                    act.activation(dst, src, ACT.Copy).then_inc(S[sem], by)

                act.wait_ge(S["params_in"], 16)
                act.drain().then_inc(S["proj_evac"], 2)
                act.drain().then_inc(S["bu_evac"], 2)
                act.drain().then_inc(S["pt_evac"], 1)
                norm_squares(act, "mix", lambda c: XT[:, c, :], KC)
                norm_root(act, "mix", 1, NV[:, 0, :], NR[:, 0, :])
                act.wait_ge(S["ssm_in"], 64)
                act.activation(lam(3), lam(2), ACT.Exp).then_inc(S["lam_dt"], 1)
                act.wait_ge(S["lam_xr"], 1)
                act.activation(lam(6), lam(4), ACT.Exp).then_inc(S["lam_mag"], 1)
                act.activation(lam(9), lam(7), ACT.Sin)
                act.activation(lam(10), lam(8), ACT.Sin).then_inc(S["lam_sin"], 1)
                with act.Fori(0, 2) as i:
                    for s in range(2):
                        act.wait_ge(used[s], i + 1)
                        evac(PJ[:, bass.ds(4 * i + 2 * s, 2), :], PS[s][:, :, 0:TOK], "proj_evac")

                def b_slot(q):
                    act.wait_ge(S["proj_evac"], 6)
                    act.wait_ge(S["bbar_turned"], q + 1)
                    act.activation(NV[:, :, :], PJ[:, bass.ds(2 * q, 2), :], ACT.Copy)
                    act.activation(s_bbs, bank(4), ACT.Copy)
                    act.drain().then_inc(S["bbar_evac"], 1)

                def c_slot(q):
                    act.activation(CBS[:, :, 0, :], CB[:, bass.ds(q * QP, QP), 0, :], ACT.Copy)
                    act.mul(CBS[:, :, 1, :], CB[:, bass.ds(q * QP, QP), 1, :], -1.0)
                    act.drain().then_inc(S["c_slot"], 1)

                def states(q):
                    for k in range(16):
                        act.wait_ge(S["bu_done"], q * 16 + k + 1)
                        evac(HS[:, k // 2, k % 2, :], bank(6 + k % 2)[:, 0:TOK], "bu_evac")

                b_slot(0)
                c_slot(0)
                states(0)
                with act.Fori(0, 3) as q:
                    b_slot(q + 1)
                    for s in range(2):
                        act.wait_ge(used[s], q + 3)
                        evac(PJ[:, bass.ds(4 * q + 8 + 2 * s, 2), :], PS[s][:, :, 0:TOK], "proj_evac")
                    act.wait_ge(S["y_done"], q + 1)
                    c_slot(q + 1)
                    act.wait_ge(S["state_kept"], 2 * q + 2)
                    states(q + 1)
                with act.Fori(0, 2) as i:
                    for s in range(2):
                        act.wait_ge(used[s], i + 6)
                        evac(PJ[:, bass.ds(4 * i + 20 + 2 * s, 2), :], PS[s][:, :, 0:TOK], "proj_evac")
                act.wait_ge(S["gates_done"], 1)
                act.activation(GT[:, :], bank(0)[0:24, 0:TOK], ACT.Sigmoid).then_inc(S["gates_sig"], 1)
                act.wait_ge(S["y_evac"], 5)
                act.activation(ZB[:, :, :], ZB[:, :, :], ACT.Gelu_apprx_tanh).then_inc(S["z_ready"], 1)
                for n, tile in enumerate(QK):
                    if n:
                        act.wait_ge(S["qk_normed"], n)
                    act.activation(SQ[:, :, :], PJ[:, tile:tile + 2, :], ACT.Square).then_inc(S["qk_sq"], 1)
                    norm_root(act, "qk", n + 1, NV[:, :, :], NR[:, :, :])
                act.wait_ge(S["qk_normed"], 6)
                with act.Fori(0, 2) as i:
                    for s in range(2):
                        act.wait_ge(used[s], i + 8)
                        act.wait_ge(S["glu_evac"], 2 * i + s + 1)
                        act.activation((NV, NR)[s][:, :, :], PS[s][:, :, 0:TOK], ACT.Sigmoid).then_inc(S["glu_sig"], 1)

                def hidden(k, n):
                    act.wait_ge(S["hid_pre"], n)
                    act.activation(HID[k], HID[k], ACT.Gelu_apprx_tanh,
                                   bias=PR[:, C_B1 + k:C_B1 + k + 1]).then_inc(S["hid_ready"], 1)

                def squares(item):
                    act.wait_ge(S["ck_evac"], 2 * item + 3)
                    act.activation(SQ[:, 0, 0:CW], ubuf[:, bass.ds(item * CW, CW)], ACT.Square).then_inc(S["ckn_sq"], 1)

                for k in range(2):
                    hidden(k, k + 1)
                squares(0)
                with act.Fori(0, NB) as item:
                    hidden(0, 2 * item + 3)
                    norm_root(act, "ckn", item + 1, NV[:, 0, 0:CW], NR[:, 0, 0:CW])
                    hidden(1, 2 * item + 4)
                    squares(item + 1)
                norm_root(act, "ckn", NB + 1, NV[:, 0, 0:CW], NR[:, 0, 0:CW])
                act.wait_ge(S["c_max"], 1)
                for k in range(NKV):
                    act.activation(SCM[:, k, :], SCM[:, k, :], ACT.Exp, bias=SM[:, 32 + k:33 + k], accum_out=SM[:, 34 + k:35 + k])
                act.drain().then_inc(S["c_exp"], 1)
                with act.Fori(0, NQ // 2) as i:
                    for j, h in enumerate(HEADS):
                        act.wait_ge(S["ps_max"], 2 * i + j + 1)
                        for c, v in enumerate([h.p1[:, 0], h.p1[:, 1], h.p0[:, 0], h.p0[:, 1], h.pc[:, 0], h.pc[:, 1]]):
                            act.activation(v, v, ACT.Exp, bias=h.m[:, c:c + 1], accum_out=h.d[:, c:c + 1])
                        act.drain().then_inc(S["p_exp"], 1)
                    for j, h in enumerate(HEADS):
                        act.wait_ge(S["pt_done"], 2 * i + j + 3)
                        act.activation(h.pt[:, 0:4, :].rearrange("p n s -> p (n s)"), bank(6), ACT.Copy)
                        act.activation(h.pt[:, 4:6, :].rearrange("p n s -> p (n s)"), bank(7)[:, 0:256], ACT.Copy)
                        act.activation(h.ptc, bank(7)[0:NCMP_P, 256:512], ACT.Copy)
                        act.drain().then_inc(S["pt_evac"], 1)
                act.wait_ge(S["sw_max"], 1)
                for k in range(NKV):
                    for i, v in enumerate((SS, SW)):
                        act.activation(v[:, k, :], v[:, k, :], ACT.Exp, bias=SM[:, 54 + 2 * i + k:55 + 2 * i + k],
                                       accum_out=SM[:, 58 + 2 * i + k:59 + 2 * i + k])
                act.drain().then_inc(S["sw_exp"], 1)
                widths = [P] * 16 + [SMP] + [P] * 4 + [SMP] + [NCMP]
                for n in range(12):
                    act.wait_ge(S["st_done"], n + 1)
                    w = widths[2 * n:2 * n + 2]
                    src = bank([0, 1, 4, 5, 6, 7][n % 6])
                    if len(set(w)) == 1:
                        act.activation(PTS[0:w[0], 2 * n:2 * n + len(w), :, :].rearrange("p n k r -> p (n k r)"),
                                       src[0:w[0], 0:256 * len(w)], ACT.Copy)
                    else:
                        for m in range(2):
                            act.activation(PTS[0:w[m], 2 * n + m, :, :].rearrange("p k r -> p (k r)"),
                                           src[0:w[m], 256 * m:256 * m + 256], ACT.Copy)
                    act.drain().then_inc(S["st_evac"], 1)
                norm_squares(act, "sn", lambda c: HC[:, c, :], SC)
                norm_root(act, "sn", 1, NV[:, 0, :], NR[:, 0, :])
                act.wait_ge(S["sn_stat"], SC)
                act.wait_ge(S["so_evac"], 2)
                norm_squares(act, "an", lambda c: HC[:, SC + c, :], SC)
                norm_root(act, "an", 1, NV[:, 0, :], NR[:, 0, :])
                act.wait_ge(S["an_stat"], SC)

                def high(s, full_, u, hidden_=None):
                    for hf in range(2):
                        if hf == 0:
                            act.wait_ge(full[s], full_)
                        act.wait_ge(S["split_used"], u + hf + 1)
                        w = act.activation(WH[:, hf, :], WR[:, s, 8 * hf:8 * hf + 8, :].rearrange("p a b -> p (a b)"), ACT.Copy)
                        if hidden_ is not None:
                            w = act.activation(XH[:, 2 * hf:2 * hf + 2, :], HT[:, bass.ds(hidden_ + 2 * hf, 2), :], ACT.Copy)
                        act.drain().then_inc(S["wh_ready"], 1)

                def high_x(n, sem, count):
                    act.wait_ge(S[sem], count)
                    c = slice(4 * (n % 4), 4 * (n % 4) + 4)
                    act.activation(XH[:, c, :], HC[:, c, :], ACT.Copy).then_inc(S["x_hi"], 1)

                F_OUT, F_GU, F_DN = (16 * (j // 2 + 1) for j in (J_OUT, J_GU, J_DN))
                for n in range(4):
                    high_x(n, "an_normed" if n >= 2 else "sn_normed", 4 * (n % 2) + 4)
                with act.Fori(0, 4) as i:
                    for s in range(2):
                        high(s, F_OUT + 16 * i, 4 * i + 2 * s)
                act.wait_ge(S["out_evac"], 10)
                norm_squares(act, "fn", lambda c: XT[:, c, :], KC)
                norm_root(act, "fn", 1, NV[:, 0, :], NR[:, 0, :])
                for n in range(4, 8):
                    high_x(n, "fn_normed", 4 * (n - 4) + 4)

                def high_pair(p):
                    for s in range(2):
                        high(s, F_GU + 16 * p, U_GU + 4 * p + 2 * s)

                def silu(p, m):
                    act.wait_ge(S["gu_done"], p + 1)
                    act.wait_ge(S["gu_evac"], p + 1)
                    act.activation((NV, NR)[m][:, :, :], PS[2 * m][:, :, 0:TOK], ACT.Silu).then_inc(S["silu_ready"], 1)

                high_pair(0)
                with act.Fori(0, MF // 2 - 1) as i:
                    for m in range(2):
                        high_pair(2 * i + m + 1)
                        silu(2 * i + m, m)
                high_pair(MF - 1)
                for m in range(2):
                    silu(MF - 2 + m, m)
                act.wait_ge(S["split_used"], U_DN + 2)
                act.wait_ge(S["gu_evac"], MF + 2)
                for r in range(2):
                    def down(j, s):
                        n = DR * r + j
                        high(s, 16 * ((J_DN + n - s) // 2 + 1), U_DN + 2 * n, 4 * j)
                    down(0, r)
                    with act.Fori(0, DR // 2) as i:
                        for t in range(2):
                            s = (r + t + 1) % 2
                            n = DR * r + t + 1
                            high(s, 16 * i + 16 * ((J_DN + n - s) // 2 + 1), 4 * i + U_DN + 2 * n, 8 * i + 4 * t + 4)

            @block.vector
            def _(dve):
                def tt(out, a, b, op):
                    return dve.tensor_tensor(out, a, b, op)

                for n, v in (("glu_evac", 2), ("out_evac", 2), ("gu_evac", 2), ("down_evac", 4),
                             ("y_evac", 1), ("po_evac", 2), ("kgroup_evac", 1), ("ck_evac", 2)):
                    dve.drain().then_inc(S[n], v)
                dve.wait_ge(S["params_in"], 16)
                norm_all(dve, "mix", lambda c: XT[:, c, :], lambda c: HC[:, c, :], C_MIX, KC)
                dve.tensor_scalar(PR[:, C_QN:C_QN + 1], PR[:, C_QN:C_QN + 1], SCALE, None, ALU.mult).then_inc(S["qgain"], 1)
                dve.wait_ge(S["lam_dt"], 1)
                LRE, LIM, DT, XR, XI, MAG, RA, RH, SN, SH, AR_, AI_, T1, T2 = (lam(i) for i in (0, 1, 3, 4, 5, 6, 7, 8, 9, 10, 11, 12, 13, 14))
                CR, CI, NR_, DEN, AIN = lam(15), lam(16), lam(17), lam(18), lam(19)
                tt(XR, LRE, DT, ALU.mult)
                tt(XI, LIM, DT, ALU.mult)
                dve.drain()
                magic = 12582912.0
                dve.tensor_scalar(T1, XI, float(1 / (2 * np.pi)), magic, ALU.mult, ALU.add)
                dve.drain()
                dve.tensor_scalar(T1, T1, -magic, None, ALU.add)
                dve.drain()
                c1 = 6.28125
                c2 = float(np.float32(2 * np.pi - c1))
                c3 = float(2 * np.pi - c1 - c2)
                dve.scalar_tensor_tensor(out=RA, in0=T1, scalar=-c1, in1=XI, op0=ALU.mult, op1=ALU.add)
                dve.drain()
                dve.scalar_tensor_tensor(out=RA, in0=T1, scalar=-c2, in1=RA, op0=ALU.mult, op1=ALU.add)
                dve.drain()
                dve.scalar_tensor_tensor(out=RA, in0=T1, scalar=-c3, in1=RA, op0=ALU.mult, op1=ALU.add)
                dve.drain()
                dve.tensor_scalar(RA, RA, 3.1415925, -3.1415925, ALU.min, ALU.max)
                dve.drain()
                dve.tensor_scalar(RH, RA, 0.5, None, ALU.mult)
                dve.drain().then_inc(S["lam_xr"], 1)
                dve.wait_ge(S["lam_sin"], 1)
                tt(T1, SH, SH, ALU.mult)
                tt(AI_, MAG, SN, ALU.mult)
                dve.drain()
                dve.tensor_scalar(T1, T1, -2.0, 1.0, ALU.mult, ALU.add)
                dve.drain()
                tt(AR_, MAG, T1, ALU.mult)
                dve.drain()
                tt(T1, LRE, LRE, ALU.mult)
                tt(T2, LIM, LIM, ALU.mult)
                dve.drain()
                tt(DEN, T1, T2, ALU.add)
                dve.tensor_scalar(NR_, AR_, -1.0, None, ALU.add)
                dve.tensor_scalar(AIN, AI_, -1.0, None, ALU.mult)
                dve.drain()
                dve.reciprocal(DEN, DEN)
                tt(T1, NR_, LRE, ALU.mult)
                tt(T2, AI_, LIM, ALU.mult)
                dve.drain()
                tt(CR, T1, T2, ALU.add)
                dve.drain()
                tt(CR, CR, DEN, ALU.mult)
                dve.drain()
                tt(T1, AI_, LRE, ALU.mult)
                tt(T2, NR_, LIM, ALU.mult)
                dve.drain()
                tt(CI, T1, T2, ALU.subtract)
                dve.drain()
                tt(CI, CI, DEN, ALU.mult)

                def cmul(outr, outi, ar, ai, br, bi, t1, t2):
                    tt(t1, ar, br, ALU.mult)
                    tt(t2, ai, bi, ALU.mult)
                    dve.drain()
                    tt(outr, t1, t2, ALU.subtract)
                    dve.drain()
                    tt(t1, ar, bi, ALU.mult)
                    tt(t2, ai, br, ALU.mult)
                    dve.drain()
                    tt(outi, t1, t2, ALU.add)
                    dve.drain()

                dve.tensor_copy(PWR[:, :, 0], AR_)
                dve.tensor_copy(PWI[:, :, 0], AI_)
                dve.drain()
                for k in (1, 2, 4, 8):
                    tr = s_t1[:, 0:32 * k].rearrange("p (j i) -> p j i", i=k)
                    ti = s_t2[:, 0:32 * k].rearrange("p (j i) -> p j i", i=k)
                    cmul(PWR[:, :, k:2 * k], PWI[:, :, k:2 * k], PWR[:, :, 0:k], PWI[:, :, 0:k],
                         PWR[:, :, k - 1:k].to_broadcast([P, NPAIR, k]), PWI[:, :, k - 1:k].to_broadcast([P, NPAIR, k]), tr, ti)
                AP_ = [(PWR[:, :, 15], PWI[:, :, 15])] + [(lam(20 + 2 * i), lam(21 + 2 * i)) for i in range(3)]
                for i in range(3):
                    cmul(*AP_[i + 1], *AP_[i], *AP_[i], T1, T2)

                def bbar(q, n):
                    if n is not None:
                        dve.wait_ge(S["bbar_turned"], n)
                    sl = bass.ds(q * QP, QP)
                    b_ = [BN[:, r, sl, :] for r in range(2)]
                    cr, ci = (v[:, sl].unsqueeze(2).to_broadcast([P, QP, 32]) for v in (CR, CI))
                    t1, t2 = (v.rearrange("p (j x) -> p j x", j=QP) for v in (s_c1, s_c2))
                    cmul(BBN[:, 0], BBN[:, 1], cr, ci, b_[0], b_[1], t1, t2)
                    dve.drain().then_inc(S["bbar_ready"], 1)

                def swapped(v):
                    a = [list(x) for x in v.ap]
                    step, n = a[2]
                    return bass.AP(v.tensor, v.offset + step, [a[0], a[1], [-step, n]] + a[3:])

                ARQ, AIQ = s_lam[:, 0:8], s_lam[:, 8:24].rearrange("p (j r) -> p j r", r=2)

                def scan(q):
                    sl = bass.ds(q * QP, QP)

                    def coef(pr, pi):
                        dve.tensor_copy(ARQ, pr[:, sl])
                        dve.tensor_copy(AIQ[:, :, 1], pi[:, sl])
                        dve.tensor_scalar(AIQ[:, :, 0], pi[:, sl], -1.0, None, ALU.mult)
                        dve.drain()

                    def advance(prev, cur, n):
                        t1 = s_c1[:, 0:QP * 2 * n].rearrange("p (j r c) -> p j r c", j=QP, r=2)
                        t2 = s_c2[:, 0:QP * 2 * n].rearrange("p (j r c) -> p j r c", j=QP, r=2)
                        tt(t1, prev, ARQ.unsqueeze(2).unsqueeze(3).to_broadcast([P, QP, 2, n]), ALU.mult)
                        tt(t2, swapped(prev), AIQ.unsqueeze(3).to_broadcast([P, QP, 2, n]), ALU.mult)
                        dve.drain()
                        tt(cur, cur, t1, ALU.add)
                        dve.drain()
                        tt(cur, cur, t2, ALU.add)
                        dve.drain()

                    coef(PWR[:, :, 0], PWI[:, :, 0])
                    dve.tensor_copy(CA[:, :, :, 0:NB], H0[:, sl, :, :])
                    dve.drain()
                    advance(CA[:, :, :, 0:NB], HS[:, :, :, SEQ:TOK:NT], NB)
                    for i in range(1, NT):
                        advance(HS[:, :, :, SEQ + i - 1:TOK:NT], HS[:, :, :, SEQ + i:TOK:NT], NB)
                    for i in range(1, CH):
                        advance(HS[:, :, :, i - 1:SEQ:CH], HS[:, :, :, i:SEQ:CH], CH)
                    dve.tensor_copy(CA, HS[:, :, :, CH - 1:SEQ:CH])
                    for i, d in enumerate((1, 2, 4, 8)):
                        coef(*AP_[i])
                        advance(CA[:, :, :, 0:CH - d], CA[:, :, :, d:CH], CH - d)
                    for r in range(2):
                        t1, t2 = (v.rearrange("p (j c i) -> p j c i", j=QP, c=CH - 1) for v in (s_t1, s_t2))
                        pr, pi = (v[:, sl, :].unsqueeze(2).to_broadcast([P, QP, CH - 1, CH]) for v in (PWR, PWI))
                        own = CA[:, :, r, 0:CH - 1].unsqueeze(3).to_broadcast([P, QP, CH - 1, CH])
                        other = CA[:, :, 1 - r, 0:CH - 1].unsqueeze(3).to_broadcast([P, QP, CH - 1, CH])
                        tt(t1, pr, own, ALU.mult)
                        tt(t2, pi, other, ALU.mult)
                        dve.drain()
                        tt(t1, t1, t2, ALU.add if r else ALU.subtract)
                        dve.drain()
                        h = HS[:, :, r, CH:SEQ].rearrange("p j (c i) -> p j c i", i=CH)
                        tt(h, h, t1, ALU.add)
                        dve.drain()
                    dve.drain().then_inc(S["scan_done"], 1)

                def y_evac(q, n):
                    dve.wait_ge(S["y_done"], n)
                    for t in range(2):
                        dve.scalar_tensor_tensor(out=ZB[:, bass.ds(2 * q + t, 1), :].rearrange("p a t -> p (a t)"),
                                                 in0=PJ[:, bass.ds(2 * q + t, 1), :].rearrange("p a t -> p (a t)"),
                                                 scalar=PR[:, bass.ds(C_D + 2 * q + t, 1)],
                                                 in1=PS[2][:, t, 0:TOK], op0=ALU.mult, op1=ALU.add)
                    dve.drain().then_inc(S["y_evac"], 1)

                bbar(0, None)
                with dve.Fori(0, 3) as q:
                    bbar(q + 1, q + 1)
                    dve.wait_ge(S["bu_evac"], 16 * q + 18)
                    scan(q)
                    y_evac(q, q + 1)
                dve.wait_ge(S["bu_evac"], 66)
                scan(3)
                dve.wait_ge(S["proj_evac"], 16)
                y_evac(3, 4)
                for n, tile in enumerate(QK):
                    norm_var(dve, "qk", n + 1, PS[2][:, :, 0:TOK], NV[:, :, :], HD)
                    norm_recip(dve, "qk", n + 1, NV[:, :, :], NR[:, :, :], SQ[:, :, :])
                    dve.scalar_tensor_tensor(out=PJ[:, tile:tile + 2, :], in0=PJ[:, tile:tile + 2, :],
                                             scalar=PR[:, QKG[n]:QKG[n] + 1], in1=NR[:, :, :],
                                             op0=ALU.mult, op1=ALU.mult)
                    dve.drain().then_inc(S["qk_normed"], 1)
                for t in range(3):
                    n = P if t < 2 else SMP
                    if t == 0:
                        dve.wait_ge(S["vt_done"], 3)
                    dve.tensor_copy(VRF[0:n, 512 * t:512 * t + 512], bank([1, 6, 7][t])[0:n, :])
                    dve.tensor_copy(GR[0:n, t, :], bank(0)[0:n, 32 * t:32 * t + 24])
                    dve.drain().then_inc(S["vr_ready"], 1)
                for g in range(GQA):
                    for k in range(NKV):
                        at_ = 3 * (GQA * k + g)
                        dve.tensor_copy(GS[32 * g:32 * g + 32, k, :], GR[0:SMP, 2, at_:at_ + 3])
                with dve.Fori(0, 2) as i:
                    for s in range(2):
                        dve.wait_ge(S["glu_sig"], 2 * i + s + 1)
                        tt(HC[:, bass.ds(4 * i + 2 * s, 2), :], ZB[:, bass.ds(4 * i + 2 * s, 2), :], (NV, NR)[s][:, :, :], ALU.mult)\
                            .then_inc(S["glu_evac"], 1)
                def pre(k, item):
                    dve.wait_ge(S["conv_done"], 2 * item + k + 1)
                    hid = HID[k].rearrange("p (h c) -> p h c", h=2)
                    if isinstance(item, int):
                        dve.tensor_copy(hid[:, :, 0:NCMP_P], bank(k)[:, 0:2 * NCMP_P].rearrange("p (h c) -> p h c", h=2))
                    else:
                        dve.tensor_copy(c_hb, bank(k)[:, 256:512])
                        dve.drain()
                        tt(hid, bank(k)[:, 0:256].rearrange("p (h c) -> p h c", h=2)[:, :, 0:NCMP],
                           c_hb.rearrange("p (h c) -> p h c", h=2)[:, :, 1:128], ALU.add)
                    dve.drain().then_inc(S["hid_pre"], 1)
                    dve.drain().then_inc(S["conv_evac"], 1)

                def ck_out(item):
                    dve.wait_ge(S["w2_done"], 2 * item + 1)
                    dve.tensor_copy(ubuf[:, bass.ds(item * CW, CW)], bank(2)[:, 0:CW]).then_inc(S["ck_evac"], 1)

                def cv_out(item):
                    dve.wait_ge(S["w2_done"], 2 * item + 2)
                    dve.tensor_copy(zbuf[0:NCMP, bass.ds(item * 256, 256)], bank(3)[0:NCMP, 0:256]).then_inc(S["ck_evac"], 1)

                def ck_norm(item):
                    v, r = NV[:, 0, 0:CW], NR[:, 0, 0:CW]
                    norm_var(dve, "ckn", item + 1, bank(4)[:, 0:CW], v, HD)
                    norm_recip(dve, "ckn", item + 1, v, r, SQ[:, 1, 0:CW])
                    c = ubuf[:, bass.ds(item * CW, CW)]
                    dve.scalar_tensor_tensor(out=c, in0=c, scalar=PR[:, C_KC:C_KC + 1], in1=r, op0=ALU.mult, op1=ALU.mult)
                    dve.drain().then_inc(S["ck_normed"], 1)

                dve.wait_ge(S["glu_evac"], 6)
                for k in range(2):
                    dve.memset(HID[k], 0.0)
                dve.drain()
                for k in range(2):
                    pre(k, 0)
                ck_out(0)
                with dve.Fori(0, NB) as item:
                    pre(0, item + 1)
                    cv_out(item)
                    ck_norm(item)
                    pre(1, item + 1)
                    ck_out(item + 1)
                cv_out(NB)
                ck_norm(NB)
                dve.memset(QPF, 0.0)
                dve.drain()
                for k in range(NKV):
                    for g in range(GQA):
                        base = QPD[:, k, 0, 32 * g:32 * g + NT]
                        dst = bass.AP(base.tensor, base.offset, [list(base.ap[0]), [P + NT, NB], [1, NT]])
                        dve.tensor_copy(dst, PJ[:, T_Q + GQA * k + g, SEQ:TOK].rearrange("p (b t) -> p b t", b=NB))
                    dve.tensor_copy(QA[:, k, :].rearrange("p (g r) -> p g r", g=GQA), PJ[:, T_Q + GQA * k:T_Q + GQA * k + GQA, SEQ:TOK])
                dve.drain().then_inc(S["qpad_ready"], 1)
                ds_, dw, dc, slr = const(K_DS), const(K_DW), const(K_DC), const(K_SLR)

                def biased(out, dist, k, scores):
                    dve.scalar_tensor_tensor(out=out, in0=dist, scalar=slr[:, k:k + 1], in1=scores, op0=ALU.mult, op1=ALU.add)

                dve.wait_ge(S["cs_done"], 1)
                for k in range(NKV):
                    biased(SCM[:, k, :], dc, k, bank(k)[:, 0:NCMP])
                dve.drain()
                dve.tensor_reduce(SM[:, 32:34], SCM, AXX, ALU.max)
                dve.drain()
                dve.tensor_scalar(SM[:, 32:34], SM[:, 32:34], -1.0, None, ALU.mult).then_inc(S["c_max"], 1)
                dve.wait_ge(S["fresh_done"], 1)
                for k in range(NKV):
                    biased(SS[:, k, PAST:NS], ds_[:, PAST:NS], k, bank(7)[:, 64 * k:64 * k + 32])
                    biased(SW[:, k, WIN:NW], dw[:, WIN:NW], k, bank(7)[:, 64 * k + 32:64 * k + 64])
                dve.drain().then_inc(S["fresh_evac"], 1)
                mxs, mxw = (SM[:, o:o + 2 * c].rearrange("p (k g) -> p k g", k=2) for o, c in ((40, 5), (50, 2)))
                dve.tensor_reduce(mxs[:, :, 4], SS[:, :, PAST:NS], AXX, ALU.max)
                dve.tensor_reduce(mxw[:, :, 1], SW[:, :, WIN:NW], AXX, ALU.max)
                dve.wait_ge(S["c_exp"], 1)
                dve.tensor_scalar(SM[:, 34:36], SM[:, 34:36], TINY, None, ALU.max)
                dve.drain()
                dve.reciprocal(SM[:, 34:36], SM[:, 34:36])
                dve.drain()
                for k in range(NKV):
                    dve.tensor_scalar(SCM[:, k, :], SCM[:, k, :], SM[:, 34 + k:35 + k], None, ALU.mult)
                dve.drain()
                dve.scalar_tensor_tensor(out=SCM, in0=SCM, scalar=TINY, in1=SCM, op0=ALU.is_ge, op1=ALU.mult)
                dve.drain().then_inc(S["c_prob"], 1)
                dve.wait_ge(S["kgroup_done"], 1)
                for k in range(NKV):
                    biased(SW[:, k, 0:WIN], dw[:, 0:WIN], k, PS[1][:, k, :])
                dve.drain().then_inc(S["kgroup_evac"], 1)
                dve.tensor_reduce(mxw[:, :, 0], SW[:, :, 0:WIN], AXX, ALU.max)
                dve.memset(PPD, 0.0)
                dve.memset(SCR, 0.0)
                dve.drain()
                dve.wait_ge(S["gsum_done"], 1)
                dve.tensor_copy(PPD[:, 1:128], bank(6)[0:64, 0:NCMP])
                dve.drain()
                dve.tensor_reduce(SUM2[:, 0:32], PPD[:, 1:129].rearrange("p (j c) -> p j c", c=4), AXX, ALU.add)
                dve.tensor_reduce(SUM2[:, 32:64], PPD[:, 0:128].rearrange("p (j c) -> p j c", c=4), AXX, ALU.add)
                dve.drain()
                tt(SCR[:, 0:32], SUM2[:, 0:32], SUM2[:, 32:64], ALU.add)
                dve.drain()
                tt(SCR, SCR, const(K_FRC)[0:64, :], ALU.max)
                dve.drain()
                other = SCR.unsqueeze(1).to_broadcast([64, NBLK, NBLK])
                own = SCR.unsqueeze(2).to_broadcast([64, NBLK, NBLK])
                sel = [SEL3[:, n, :].rearrange("p (j i) -> p j i", j=NBLK) for n in range(3)]
                tt(sel[0], other, own, ALU.is_gt)
                tt(sel[1], other, own, ALU.is_equal)
                dve.drain()
                dve.wait_ge(S["tie_in"], 16)
                tt(sel[1], sel[1], sel[2], ALU.mult)
                dve.drain()
                tt(sel[0], sel[0], sel[1], ALU.add)
                dve.drain()
                dve.tensor_reduce(RNK, sel[0], AXX, ALU.add)
                dve.drain()
                dve.tensor_scalar(RNK, RNK, float(NSEL), MASKED, ALU.is_ge, ALU.mult)
                dve.drain()
                for g in range(GQA):
                    for k in range(NKV):
                        dve.tensor_copy(MB[32 * g:32 * g + 32, k, :], RNK[32 * k:32 * k + 32, 0:32])
                dve.drain().then_inc(S["ranked"], 1)
                d1, dcp, slh = const(K_D1), const(K_DCP), const(K_SLH)

                def prompt_bias(n, h):
                    dve.wait_ge(S["ps_done"], n + 3)
                    dve.wait_ge(S["pt_done"], n + 1)
                    slope = slh[:, bass.ds(n, 1)]
                    for v, ps, w in ((h.p1, h.s1, 256), (h.p0, h.s0, 128)):
                        dve.scalar_tensor_tensor(out=v, in0=d1[:, SEQ - w:SEQ].unsqueeze(1).to_broadcast([P, 2, w]), scalar=slope,
                                                 in1=ps[:, 0:2 * w].rearrange("p (b s) -> p b s", b=2),
                                                 op0=ALU.mult, op1=ALU.add)
                    dve.scalar_tensor_tensor(out=h.pc, in0=dcp, scalar=slope, in1=h.s0[:, 256:256 + 2 * NCMP_P],
                                             op0=ALU.mult, op1=ALU.add)
                    dve.drain()
                    for c, v in enumerate((h.p1, h.p0, h.pc)):
                        dve.tensor_reduce(h.m[:, 2 * c:2 * c + 2], v, AXX, ALU.max)
                    dve.drain()
                    dve.tensor_scalar(h.m, h.m, -1e20, -1.0, ALU.max, ALU.mult).then_inc(S["ps_max"], 1)

                def prompt_scale(n, h):
                    dve.wait_ge(S["p_exp"], n + 1)
                    f = h.d
                    dve.tensor_scalar(f, f, TINY, None, ALU.max)
                    dve.drain()
                    dve.reciprocal(f, f)
                    dve.drain()
                    tt(f[:, 0:2], f[:, 0:2], GR[:, 1, bass.ds(3 * n + 1, 2)], ALU.mult)
                    tt(f[:, 2:4], f[:, 2:4], GR[:, 0, bass.ds(3 * n + 1, 2)], ALU.mult)
                    tt(f[:, 4:6], f[:, 4:6], GR[:, 0:2, bass.ds(3 * n, 1)].rearrange("p t a -> p (t a)"), ALU.mult)
                    dve.drain()
                    for c, (v, w) in enumerate(((h.p1, 256), (h.p0, 128), (h.pc, NCMP_P))):
                        tt(v, v, f[:, 2 * c:2 * c + 2].unsqueeze(2).to_broadcast([P, 2, w]), ALU.mult)
                    dve.drain().then_inc(S["p_ready"], 1)

                def prompt_out(n, h):
                    dve.wait_ge(S["po_done"], n + 1)
                    dve.tensor_copy(HC[:, bass.ds(n + SC, 1), 0:SEQ].rearrange("p a s -> p (a s)"), h.s1[:, 0:SEQ])\
                        .then_inc(S["po_evac"], 1)

                with dve.Fori(0, 4) as i:
                    a, b_ = HEADS
                    n = 2 * i
                    prompt_bias(n, a)
                    prompt_bias(n + 1, b_)
                    prompt_scale(n, a)
                    prompt_scale(n + 1, b_)
                    prompt_out(n, a)
                    dve.wait_ge(S["kgroup_done"], i + 2)
                    for k in range(NKV):
                        biased(SS[:, k, bass.ds(i * 512, 512)], ds_[:, bass.ds(i * 512, 512)], k, PS[1][:, k, :])
                    dve.drain().then_inc(S["kgroup_evac"], 1)
                    prompt_out(n + 1, b_)
                    for k in range(NKV):
                        v = SS[:, k, bass.ds(i * 512, 512)].rearrange("p (j s) -> p j s", s=SEL)
                        tt(v, v, MB[:, k, bass.ds(i * 8, 8)].unsqueeze(2).to_broadcast([P, 8, SEL]), ALU.add)
                    dve.drain()
                    for k in range(NKV):
                        dve.tensor_reduce(mxs[:, k, bass.ds(i, 1)], SS[:, k, bass.ds(i * 512, 512)], AXX, ALU.max)
                dve.drain()
                dve.tensor_reduce(SM[:, 54:56], mxs, AXX, ALU.max)
                dve.tensor_reduce(SM[:, 56:58], mxw, AXX, ALU.max)
                dve.drain()
                dve.tensor_scalar(SM[:, 54:58], SM[:, 54:58], -1.0, None, ALU.mult).then_inc(S["sw_max"], 1)
                dve.wait_ge(S["gsum_done"], 1)
                for k in range(NKV):
                    dve.tensor_scalar(SCM[:, k, :], SCM[:, k, :], GS[:, k, 0:1], None, ALU.mult)
                dve.drain().then_inc(S["sw_ready"], 1)
                dve.wait_ge(S["sw_exp"], 1)
                f = SM[:, 58:62]
                dve.tensor_scalar(f, f, TINY, None, ALU.max)
                dve.drain()
                dve.reciprocal(f, f)
                dve.drain()
                for i in range(2):
                    tt(f[:, 2 * i:2 * i + 2], f[:, 2 * i:2 * i + 2], GS[:, :, 1 + i], ALU.mult)
                dve.drain()
                for i, v in enumerate((SS, SW)):
                    for k in range(NKV):
                        dve.tensor_scalar(v[:, k, :], v[:, k, :], f[:, 2 * i + k:2 * i + k + 1], None, ALU.mult)
                    dve.drain().then_inc(S["sw_ready"], 1)
                dve.wait_ge(S["so_done"], 1)
                for k in range(NKV):
                    dve.tensor_copy(HC[:, SC + GQA * k:SC + GQA * k + GQA, SEQ:TOK],
                                    PS[1][:, k, 0:P].rearrange("p (g r) -> p g r", g=GQA)).then_inc(S["so_evac"], 1)
                norm_all(dve, "sn", lambda c: HC[:, c, :], lambda c: HC[:, c, :], C_NSSM, SC)
                dve.drain()
                norm_all(dve, "an", lambda c: HC[:, SC + c, :], lambda c: HC[:, SC + c, :], C_NATT, SC, stat=5)
                def low_half(s, u, hf, hidden_=None):
                    dve.wait_ge(S["wh_ready"], u + hf + 1)
                    tt(WL[:, hf, :], WR[:, s, 8 * hf:8 * hf + 8, :].rearrange("p a b -> p (a b)"), WH[:, hf, :].bitcast(F32), ALU.subtract)
                    if hidden_ is not None:
                        tt(XL[:, 2 * hf:2 * hf + 2, :], HT[:, bass.ds(hidden_ + 2 * hf, 2), :],
                           XH[:, 2 * hf:2 * hf + 2, :].bitcast(F32), ALU.subtract)
                    dve.drain().then_inc(S["wl_ready"], 1)
                    if hf == 1:
                        dve.drain().then_inc(freed[s], 1)

                def low(s, u, hidden_=None):
                    for hf in range(2):
                        low_half(s, u, hf, hidden_)

                def out_add(j, s):
                    dve.wait_ge(S["split_used"], 2 * j + 4)
                    v = XT[:, bass.ds(2 * j, 2), :]
                    tt(v, PS[s][:, :, 0:TOK], v, ALU.add).then_inc(S["out_evac"], 1)

                low(0, 0)
                with dve.Fori(0, 3) as i:
                    low(1, 4 * i + 2)
                    out_add(2 * i, 0)
                    low(0, 4 * i + 4)
                    out_add(2 * i + 1, 1)
                low(1, 14)
                out_add(6, 0)
                out_add(7, 1)
                dve.drain()
                norm_all(dve, "fn", lambda c: XT[:, c, :], lambda c: HC[:, c, :], C_FFN, KC)

                def low_pair(p):
                    for s in range(2):
                        low(s, U_GU + 4 * p + 2 * s)

                def gate(p, m):
                    dve.wait_ge(S["silu_ready"], p + 1)
                    tt(HT[:, bass.ds(2 * p, 2), :], PS[2 * m + 1][:, :, 0:TOK], (NV, NR)[m][:, :, :], ALU.mult)\
                        .then_inc(S["gu_evac"], 1)

                low_pair(0)
                with dve.Fori(0, MF // 2 - 1) as i:
                    for m in range(2):
                        low_pair(2 * i + m + 1)
                        gate(2 * i + m, m)
                low_pair(MF - 1)
                for m in range(2):
                    gate(MF - 2 + m, m)

                def down_add(r):
                    dve.wait_ge(S["down_done"], r + 1)
                    for m in range(4):
                        v = XT[:, 8 * r + 2 * m:8 * r + 2 * m + 2, :]
                        tt(v, PS[m][:, :, 0:TOK], v, ALU.add).then_inc(S["down_evac"], 1)

                for r in range(2):
                    n = DR * r
                    low_half(r, U_DN + 2 * n, 0, 0)
                    if r:
                        down_add(0)
                    low_half(r, U_DN + 2 * n, 1, 0)
                    with dve.Fori(0, DR // 2) as i:
                        for t in range(2):
                            low((r + t + 1) % 2, 4 * i + U_DN + 2 * (n + t + 1), 8 * i + 4 * t + 4)
                down_add(1)

        nc.all_engine_barrier(sems_to_clear=range(handles[0].num, handles[-1].num + 1))

    with nc.Block() as block:
        @block.sync
        def _(sp):
            sp.dma_start(T["y"], XT[:, :, :]).then_inc(S["y_out"], 16)
            sp.wait_ge(S["y_out"], 16)
    stack.close()


def arrays_of(v):
    def blocks(w, k, cols):
        n = w.shape[2] // cols
        return w.reshape(L, k, P, n, cols).transpose(0, 3, 2, 1, 4).reshape(L * n, P, k * cols)

    def feature_major(x):
        return x.reshape(x.shape[0], -1, P).transpose(2, 1, 0)

    def gain(g):
        return g.reshape(L, -1, P).transpose(0, 2, 1)

    pool = v["cache_cmp_kv"].shape[1]
    a = {"consts": constant_table()[0], "ties": tie_table()}
    x = np.concatenate([v["x_prompt"].reshape(SEQ, D_MODEL), v["x_sample"].reshape(SMP, D_MODEL)])
    a["x"] = feature_major(x)
    a["pages"] = v["page_table"].reshape(1, NB * NPG)
    a["w_in"] = blocks(v["w_in"][:, :, :NTILE * P], KC, 256)
    a["w_gates"] = v["w_in"][:, :, NTILE * P:].reshape(L, KC, P, 24).transpose(0, 2, 1, 3).reshape(L, P, KC * 24)
    a["w_glu"] = blocks(v["ssm_w_glu"], SC, 256)
    a["w_out"] = blocks(v["w_out"], KC, 256)
    gate, up = (blocks(v[n], KC, 256).reshape(L, MF, 1, P, KC * 256) for n in ("w_ffn_gate", "w_ffn_up"))
    a["w_gu"] = np.concatenate([gate, up], 2).reshape(L * 2 * MF, P, KC * 256)
    a["w_down"] = v["w_ffn_down"].reshape(L, 11, 4, P, 2, 1024).transpose(0, 4, 1, 3, 2, 5).reshape(L * 22, P, 4 * 1024)
    w1 = np.stack([v["cmp_w1_k"], v["cmp_w1_v"]], 1).reshape(L, 2, 32, HD, HD)
    a["cmp_w1"] = w1.transpose(0, 1, 3, 2, 4).reshape(L * 2, P, 32 * HD)
    a["cmp_w2"] = np.stack([v["cmp_w2_k"], v["cmp_w2_v"]], 2).reshape(L, P, 2 * HD)
    a["params"] = np.concatenate(
        [gain(v[n]) for n in ("norm_mix", "norm_ffn", "norm_ssm_out", "norm_attn_out")]
        + [gain(v["ssm_d"].reshape(L, -1))]
        + [v[n][:, :, None] for n in ("q_norm", "k_norm_slc", "k_norm_win", "k_norm_cmp", "cmp_b1_k", "cmp_b1_v")], 2)
    pair = lambda t: t.reshape(L, NPAIR, P).transpose(0, 2, 1)
    dt = np.broadcast_to(v["ssm_log_dt"][:, :, None], (L, 64, 64))
    a["lam"] = np.concatenate([pair(v["ssm_a_re"]), pair(v["ssm_a_im"]), pair(dt)], 2)
    b = np.zeros((L, 2, 64, 2, NPAIR, 2, 16), np.float32)
    c = np.zeros((L, 2, 64, NPAIR, 2, 2, 16), np.float32)
    for r, (nb, nc_) in enumerate([("ssm_b_re", "ssm_c_re"), ("ssm_b_im", "ssm_c_im")]):
        bb = v[nb].reshape(L, NPAIR, 2, 64, 16)
        cc = v[nc_].reshape(L, NPAIR, 2, 16, 64)
        for m in range(2):
            b[:, m, :, r, :, m, :] = bb[:, :, m].transpose(0, 2, 1, 3)
            c[:, m, :, :, r, m, :] = cc[:, :, m].transpose(0, 3, 1, 2)
    a["ssm_b"] = b.reshape(L, P, 2048)
    a["ssm_c"] = c.reshape(L, P, 2048)
    h0 = v["state_ssm"].reshape(L, NB, NPAIR, 2, 64, 2)
    a["ssm_h0"] = h0.transpose(0, 3, 4, 2, 5, 1).reshape(L, P, NPAIR * 2 * NB)
    cc = v["cache_cmp_kv"].reshape(L * pool, 8, 16, 2, 2, HD)
    a["cache_cmp"] = cc.transpose(0, 5, 3, 4, 2, 1).reshape(L * pool, P, 512)
    cs = v["cache_slc_kv"].reshape(L * pool, PAGE, 2, 2, HD)
    a["cache_slc_k"] = cs[:, :, :, 0].transpose(0, 3, 2, 1).reshape(L * pool, P, 256)
    a["cache_slc_v"] = cs[:, :, :, 1].reshape(L * pool, P, 256)
    w = v["state_win_kv"].reshape(L * NB, WIN, 2, 2, HD)
    a["win_k"] = w[:, :, :, 0].reshape(L * NB, 4, P, 2, HD).transpose(0, 4, 1, 3, 2).reshape(L * NB, P, 1024)
    a["win_v"] = w[:, :, :, 1].reshape(L * NB, 4, P, 2, HD).transpose(0, 2, 1, 3, 4).reshape(L * NB, P, 1024)
    a["win_rows"] = v["state_win_kv"].reshape(L, NB, WIN, 512)
    return {n: np.ascontiguousarray(t) for n, t in a.items()}


OUTS = {"y": (P, KC, TOK), "kv_new": (L, P, 12 * TOK), "win_kept": (L, NB, WIN - NT, 512),
        "win_zeros": (L, P, 1024), "ssm_last": (L, P, NPAIR * 2 * 9)}


def kernel(**inputs):
    import concourse.bacc as _bacc
    from concourse.bass_utils import run_bass_kernel_spmd as _run

    nc = _bacc.Bacc("TRN2", target_bir_lowering=False, num_devices=1)
    arrays = arrays_of({k: np.asarray(x) for k, x in inputs.items()})
    T = {n: nc.dram_tensor(f"in_{n}", a.shape, mybir.dt.from_np(a.dtype), kind="ExternalInput").ap()
         for n, a in arrays.items()}
    T |= {n: nc.dram_tensor(f"out_{n}", s, F32, kind="ExternalOutput").ap() for n, s in OUTS.items()}
    build(nc, T)
    got = _run(nc, [{f"in_{n}": a for n, a in arrays.items()}], core_ids=[0]).results[0]
    y = got["out_y"].transpose(2, 1, 0).reshape(TOK, D_MODEL)
    new = got["out_kv_new"].reshape(L, P, 3, 2, 2, TOK).transpose(2, 0, 5, 4, 3, 1)
    rows_p = new[:, :, :SEQ].reshape(3, L, 1, SEQ, 2, 2, HD)
    rows_s = new[:, :, SEQ:].reshape(3, L, NB, NT, 2, 2, HD)
    zeros = got["out_win_zeros"].reshape(L, 1, WIN - SEQ, 2, 2, HD)
    kept = got["out_win_kept"].reshape(L, NB, WIN - NT, 2, 2, HD)
    last = got["out_ssm_last"].reshape(L, 2, 64, NPAIR, 2, 9).transpose(0, 5, 3, 1, 2, 4).reshape(L, 9, 64, 64, 2)
    out = (y[:SEQ].reshape(1, SEQ, D_MODEL), y[SEQ:].reshape(NB, NT, D_MODEL), rows_p[0], rows_p[1],
           np.concatenate([zeros, rows_p[2]], 2), last[:, :1], rows_s[0], rows_s[1],
           np.concatenate([kept, rows_s[2]], 2), last[:, 1:])
    return tuple(np.ascontiguousarray(o) for o in out)
```

```python
from contextlib import ExitStack

import numpy as np

import concourse.bass as bass
from concourse import mybir

F32 = mybir.dt.float32
F32R = mybir.dt.float32r
I32 = mybir.dt.int32
ALU = mybir.AluOpType
ACT = mybir.ActivationFunctionType
AXX = mybir.AxisListType.X

P = 128
L = 2
D_MODEL, SEQ, NB, NT = 2048, 256, 8, 4
SMP = NB * NT
TOK = SEQ + SMP
PAST, PAGE, NPG, WIN = 2048, 128, 16, 512
KC = D_MODEL // P
D_FF = 5632
MF = D_FF // 256
NQ, NKV, GQA, HD = 8, 2, 4, 128
SC = 8
NCMP, NCMP_P = 127, 15
NBLK, NSEL, SEL = 33, 16, 64
CH = 16
NPAIR, QP = 32, 8
EPS = 1e-6
SCALE = HD ** -0.5
TINY = 1.1754943508222875e-38
MASKED = -1e30
FORCED = 1e4
STEP = 2 * TOK

T_Q, T_KC, T_VC, T_KS, T_VS, T_KW, T_VW, NTILE = 8, 16, 18, 20, 22, 24, 26, 28
C_MIX, C_FFN, C_NSSM, C_NATT, C_D, C_QN, C_KS, C_KW, C_KC, C_B1, NPAR = 0, 16, 32, 40, 48, 56, 57, 58, 59, 60, 62
K_ID, K_ONE, K_DS, K_DW, K_DC, K_DCP, K_D1, K_SLR, K_SLH, K_G, K_FRC = range(11)


def constant_table():
    r = np.arange(P)
    t, s = r[:, None], np.arange(SMP)[None, :]
    b, step, g = (r % 32) // NT, r % NT, r // 32
    big = -MASKED
    fresh = np.where((s // NT == b[:, None]) & (s % NT <= step[:, None]), step[:, None] - s % NT, big)
    past = PAST + step[:, None] - np.arange(PAST)[None, :]
    j = np.arange(WIN)[None, :]
    win = np.where(j > step[:, None], WIN + step[:, None] - j, big)
    c = np.arange(NCMP)[None, :]
    cmp_s = PAST + step[:, None] - 16 * c - 15.5
    cp = np.arange(NCMP_P)[None, :]
    cmp_p = [np.where(16 * cp + 31 <= t + 128 * n, t + 128 * n - 16 * cp - 15.5, big) for n in range(2)]
    causal = np.where(P + t - np.arange(SEQ)[None, :] >= 0, P + t - np.arange(SEQ)[None, :], big)
    slope = -(2.0 ** -np.arange(1, NQ + 1))
    rows = np.stack([slope[g], slope[4 + g]], 1)
    blk = np.arange(NBLK)
    force = np.where((blk == 0) | (blk >= 31), FORCED, 0.0)
    parts = [np.eye(P), np.ones((P, P)), np.concatenate([past, fresh], 1), np.concatenate([win, fresh], 1),
             cmp_s, np.concatenate(cmp_p, 1), causal, rows, np.tile(slope, (P, 1)),
             (r[:, None] % 32 == np.arange(32)[None, :]) * 1.0, np.tile(force, (P, 1))]
    at = np.cumsum([0] + [x.shape[1] for x in parts])
    return np.concatenate(parts, 1).astype(np.float32), [int(a) for a in at]


def tie_table():
    i = np.arange(NBLK)
    return np.tile((i[None, :] < i[:, None]).reshape(1, -1), (64, 1)).astype(np.float32)



SEMS = """consts_in x_in pages_in zero_set zero_out
params_in ssm_in gate_w_in w2_in slot0_full slot1_full slot0_used slot1_used slot0_freed slot1_freed wh_ready wl_ready split_used x_hi x_lo
mix_sq mix_stat mix_var mix_root mix_normed
lam_dt lam_xr lam_mag lam_sin bbar_ready bbar_turned bbar_evac c_slot bu_done bu_evac scan_done pool_scanned
state_kept y_done y_evac z_ready proj_evac gates_done gates_sig states_out
gated_step glu_done glu_sig glu_evac
qk_sq qk_stat qk_var qk_root qk_normed kv_out vt_done vr_ready qgain
cache0_full cache1_full cache0_used cache1_used conv_done conv_evac hid_pre hid_ready w2_done ck_evac
ckn_sq ckn_stat ckn_var ckn_root ck_normed
q_copied ps_done ps_max p_exp p_ready pt_done pt_evac po_done po_evac
qpad_ready cs_done cs_ready c_max c_exp c_prob gsum_done tie_in ranked gates_rows
kring0_more kring1_more kring2_more kring3_more kring0_full kring1_full kring2_full kring3_full kring_free kgroup_done kgroup_evac fresh_done fresh_evac
sw_max sw_exp sw_ready st_done st_evac
vbuf0_more vbuf1_more vbuf0_full vbuf1_full vbuf0_rest vbuf1_rest vwin0_full vwin1_full vring_free o_done o_kept so_done so_evac
sn_sq sn_stat sn_var sn_root sn_normed an_sq an_stat an_var an_root an_normed
out_step out_evac fn_sq fn_stat fn_var fn_root fn_normed
gu_done silu_ready gu_evac down_done down_evac win_copied x_out y_out""".split()


def build(nc, T):
    _, at = constant_table()
    stack = ExitStack()
    handles = [nc.alloc_semaphore(n) for n in SEMS]
    assert [h.num for h in handles] == list(range(handles[0].num, handles[0].num + len(SEMS)))
    S = dict(zip(SEMS, handles))

    def sb(name, shape, dt=F32):
        return stack.enter_context(nc.sbuf_tensor(name, shape, dt))

    CT = sb("consts", [P, at[-1]])

    def const(i):
        return CT[:, at[i]:at[i + 1]]
    ident, ones = const(K_ID), const(K_ONE)
    XT = sb("residual", [P, KC, TOK])
    WR = sb("weight_slots", [P, 2, 16, 256])
    HC = sb("normed", [P, KC, TOK])
    PR = sb("params", [P, NPAR])
    SQ = sb("squares", [P, 2, TOK])
    NV = sb("norm_var", [P, 2, TOK])
    NR = sb("norm_rstd", [P, 2, TOK])
    PG = sb("page_numbers", [1, NB * NPG], I32)
    SM = sb("smalls", [P, 64])
    HT_SIZE, SPLIT = 2 * MF * TOK, 8 * 256
    with ExitStack() as late:
        XH = late.enter_context(nc.sbuf_tensor("normed_hi", [P, KC, TOK], F32R))
        XL = late.enter_context(nc.sbuf_tensor("normed_lo", [P, KC, TOK], F32R))
        WH = late.enter_context(nc.sbuf_tensor("weights_hi", [P, 2, SPLIT], F32R))
        WL = late.enter_context(nc.sbuf_tensor("weights_lo", [P, 2, SPLIT], F32R))
        HT = late.enter_context(nc.sbuf_tensor("ffn_hidden", [P, 2 * MF, TOK], F32))
    PJ = sb("projected", [P, NTILE, TOK])
    ZB = sb("ssm_out", [P, SC, TOK])
    W2 = sb("cmp_w2", [P, 2, HD])
    GT = sb("gates_t", [24, TOK])
    GR = sb("gates_rows", [P, 3, 24])
    GS = sb("gates_sample", [P, NKV, 3])
    VRF = sb("v_rows", [P, 3 * 2 * 2 * HD])
    VR = VRF[:, :].rearrange("p (t b h d) -> p t b h d", t=3, b=2, h=2)
    WG = VRF[:, 0:KC * 24].rearrange("p (k x) -> p k x", k=KC)
    ARENA = 17800
    AR = sb("arena", [P, ARENA])
    PS = [stack.enter_context(nc.psum_tensor(f"banks{i}", [P, 2, 512], F32)) for i in range(4)]

    def bank(i):
        return PS[i // 2][:, i % 2, :]

    def carve(sizes):
        out, o = [], 0
        for n in sizes:
            out.append(AR[:, o:o + n])
            o += n
        assert o <= ARENA, o
        return out

    s_hs, s_bn, s_cb, s_bbn, s_bbs, s_cbs, s_t1, s_t2, s_pwr, s_pwi, s_h0, s_hl, s_ca, s_c1, s_c2, s_lam = carve(
        [QP * 2 * TOK, 2048, 2048, 512, 512, 512, 1920, 1920, 512, 512, 512, 576, 256, 256, 256, 26 * 32])
    HS = s_hs.rearrange("p (j r t) -> p j r t", j=QP, r=2)
    BN = s_bn.rearrange("p (r j x) -> p r j x", r=2, j=NPAIR)
    CB = s_cb.rearrange("p (j r x) -> p j r x", j=NPAIR, r=2)
    BBN = s_bbn.rearrange("p (r j x) -> p r j x", r=2, j=QP)
    BBS = s_bbs.rearrange("p (r t x) -> p r t x", r=2, t=2)
    CBS = s_cbs.rearrange("p (j r x) -> p j r x", j=QP, r=2)
    PWR = s_pwr.rearrange("p (j i) -> p j i", j=NPAIR)
    PWI = s_pwi.rearrange("p (j i) -> p j i", j=NPAIR)
    H0 = s_h0.rearrange("p (j r b) -> p j r b", j=NPAIR, r=2)
    HL = s_hl.rearrange("p (j r b) -> p j r b", j=NPAIR, r=2)
    CA = s_ca.rearrange("p (j r c) -> p j r c", j=QP, r=2)

    def lam(i, n=1):
        return s_lam[:, 32 * i:32 * (i + n)]
    c_t0, c_t1, c_hid, c_hb = carve([8192, 8192, 508, 256])
    CTB = [x.rearrange("p (g h k i c) -> p g h k i c", g=NPG, h=2, k=2, i=16) for x in (c_t0, c_t1)]
    HID = [c_hid[:, 254 * i:254 * i + 254] for i in range(2)]
    ubuf = PJ[:, 0:8, :].rearrange("p a b -> p (a b)")
    zbuf = ZB[:, :, :].rearrange("p a b -> p (a b)")
    CW = 2 * NCMP
    CKP = ubuf[:, 0:CW].rearrange("p (h c) -> p h c", h=2)[:, :, 0:NCMP_P]
    CK = ubuf[:, CW:CW * (NB + 1)].rearrange("p (b h c) -> p b h c", b=NB, h=2)
    CVP = zbuf[:, 0:256].rearrange("p (h d) -> p h d", h=2)
    CV = zbuf[:, 256:2304].rearrange("p (b h d) -> p b h d", b=NB, h=2)
    class Head:
        def __init__(self, j):
            buf = WR[:, 1, :, :].rearrange("p a b -> p (a b)")[:, 1824 * j:1824 * j + 1824]
            self.p1 = buf[:, 0:512].rearrange("p (b s) -> p b s", b=2)
            self.p0 = buf[:, 512:768].rearrange("p (b s) -> p b s", b=2)
            self.pc = buf[:, 768:798].rearrange("p (t s) -> p t s", t=2)
            self.pt = buf[:, 800:1568].rearrange("p (n s) -> p n s", n=6)
            self.ptc = buf[0:NCMP_P, 1568:1824]
            self.q = SQ[:, :, :].rearrange("p a b -> p (a b)")[:, 256 * j:256 * j + 256].rearrange("p (t s) -> p t s", t=2)
            self.s1, self.s0 = bank(4 * j), bank(4 * j + 1)
            self.m, self.d = SM[:, 16 * j:16 * j + 6], SM[:, 16 * j + 8:16 * j + 14]
    HEADS = [Head(0), Head(1)]
    NS, NW = PAST + SMP, WIN + SMP
    a_s, a_w, a_c, a_ring, a_qp, a_qa, a_pt = carve([2 * NS, 2 * NW, 2 * NCMP, 4096, 2048, 256, 2 * 23 * 128])
    SS = a_s.rearrange("p (k s) -> p k s", k=2)
    OW = a_w[:, 0:1024].rearrange("p (k x) -> p k x", k=2)
    SW = a_w.rearrange("p (k s) -> p k s", k=2)
    SCM = a_c.rearrange("p (k s) -> p k s", k=2)
    KR = [a_ring[:, 1024 * n:1024 * n + 1024].rearrange("p (g h s) -> p g h s", g=4, h=2) for n in range(4)]
    vbufs = [(a_ring, a_qp[:, 0:1024]), (a_s, a_qp[:, 1024:2048])]
    VG = [[r[:, 1024 * n:1024 * n + 1024].rearrange("p (g h d) -> p g h d", g=4, h=2) for n in range(4)]
          + [w_.rearrange("p (g h d) -> p g h d", g=4, h=2)] for r, w_ in vbufs]
    QPF = a_qp
    QPD = a_qp.rearrange("p (k b r) -> p k b r", k=2, b=NB)
    QA = a_qa.rearrange("p (k r) -> p k r", k=2)
    PTS = a_pt.rearrange("p (n k r) -> p n k r", n=23, k=2)
    SEL3 = a_pt[0:64, 0:3267].rearrange("p (n a) -> p n a", n=3)
    PPD = a_pt[0:64, 3267:3399]
    SCR = a_pt[0:64, 3400:3433]
    SUM2 = a_pt[0:64, 3440:3504]
    RNK = a_pt[0:64, 3510:3543]
    MB = a_pt[:, 3550:3614].rearrange("p (k j) -> p k j", k=2)

    J_IN, J_GLU, J_W1, J_OUT, J_GU, J_DN = 0, 14, 18, 20, 28, 72
    full = [S["slot0_full"], S["slot1_full"]]
    used = [S["slot0_used"], S["slot1_used"]]
    freed = [S["slot0_freed"], S["slot1_freed"]]
    U_GU, U_DN = 16, 16 + 88
    DR = 11

    with nc.Block() as block:
        @block.sync
        def _(sp):
            sp.dma_start(CT[:, :], T["consts"]).then_inc(S["consts_in"], 16)
            sp.dma_start(XT[:, :, :], T["x"]).then_inc(S["x_in"], 16)
            sp.dma_start(PG[:, :], T["pages"]).then_inc(S["pages_in"], 16)
            sp.wait_ge(S["zero_set"], 1)
            for i in range(L):
                sp.dma_start(T["win_zeros"][i], AR[:, 0:1024]).then_inc(S["zero_out"], 16)
            sp.wait_ge(S["consts_in"], 16)
            sp.wait_ge(S["x_in"], 16)
            sp.wait_ge(S["pages_in"], 16)
            sp.wait_ge(S["zero_out"], 16 * L)

        @block.vector
        def _(dve):
            dve.memset(AR[:, 0:1024], 0.0).then_inc(S["zero_set"], 1)
    nc.all_engine_barrier(sems_to_clear=range(handles[0].num, handles[-1].num + 1))

    with nc.Fori(0, L) as lay:
        with nc.Block() as block:
            def pages(eng, name, ring, n, i, free, count, sem):
                first = 0 if eng is nc.sync else 2
                p = [eng.value_load(PG[0:1, bass.ds(i + first + g, 1)], min_val=0, max_val=159) for g in range(2)]
                eng.wait_ge(free, count)
                for g in range(2):
                    at_ = 1024 * n + (first + g) * 256
                    eng.dma_start(ring[:, at_:at_ + 256],
                                  T[name][bass.ds(lay * 160 + p[g], 1)].rearrange("a p x -> p (a x)")).then_inc(sem, 16)

            def values(eng, i, hb, part):
                b = 2 * i + hb
                mine = range(("full", "more", "rest").index(part), NPG, 3)
                p = [eng.value_load(PG[0:1, bass.ds(b * NPG + x, 1)], min_val=0, max_val=159) for x in mine]
                eng.wait_ge(*((S["st_done"], 12) if hb else (S["kring_free"], 44)))
                for x, page in zip(mine, p):
                    eng.wait_ge(S["vring_free"], b * 5 + x // 4 + 1)
                    eng.dma_start(vbufs[hb][0][:, 256 * x:256 * x + 256],
                                  T["cache_slc_v"][bass.ds(lay * 160 + page, 1)].rearrange("a p x -> p (a x)"))\
                        .then_inc(S[f"vbuf{hb}_{part}"], 16)

            def swapped(v):
                a = [list(x) for x in v.ap]
                step, n = a[2]
                return bass.AP(v.tensor, v.offset + step, [a[0], a[1], [-step, n]] + a[3:])

            ARQ, AIQ = s_lam[:, 0:8], s_lam[:, 8:24].rearrange("p (j r) -> p j r", r=2)
            CHUNK_POWERS = [(PWR[:, :, 15], PWI[:, :, 15])] + [(lam(20 + 2 * i), lam(21 + 2 * i)) for i in range(3)]
            POOL_PAIRS = 2

            def scan(eng, q, j0, j1):
                J = j1 - j0
                js = slice(j0, j1)
                sl = bass.ds(q * QP + j0, J)
                hs, ca, arq, aiq = HS[:, js], CA[:, js], ARQ[:, js], AIQ[:, js]

                def tt(out, a, b, op):
                    return eng.tensor_tensor(out, a, b, op)

                def coef(pr, pi):
                    eng.tensor_copy(arq, pr[:, sl])
                    for r in range(2):
                        eng.tensor_copy(aiq[:, :, r], pi[:, sl])
                    eng.drain()
                    eng.tensor_scalar(aiq[:, :, 0], aiq[:, :, 0], -1.0, None, ALU.mult)
                    eng.drain()

                def advance(prev, cur, n):
                    t1, t2 = (v[:, 32 * j0:32 * j0 + J * 2 * n].rearrange("p (j r c) -> p j r c", j=J, r=2) for v in (s_c1, s_c2))
                    tt(t1, prev, arq.unsqueeze(2).unsqueeze(3).to_broadcast([P, J, 2, n]), ALU.mult)
                    tt(t2, swapped(prev), aiq.unsqueeze(3).to_broadcast([P, J, 2, n]), ALU.mult)
                    eng.drain()
                    tt(cur, cur, t1, ALU.add)
                    eng.drain()
                    tt(cur, cur, t2, ALU.add)
                    eng.drain()

                coef(PWR[:, :, 0], PWI[:, :, 0])
                eng.tensor_copy(ca[:, :, :, 0:NB], H0[:, sl, :, :])
                eng.drain()
                advance(ca[:, :, :, 0:NB], hs[:, :, :, SEQ:TOK:NT], NB)
                for i in range(1, NT):
                    advance(hs[:, :, :, SEQ + i - 1:TOK:NT], hs[:, :, :, SEQ + i:TOK:NT], NB)
                for i in range(1, CH):
                    advance(hs[:, :, :, i - 1:SEQ:CH], hs[:, :, :, i:SEQ:CH], CH)
                eng.tensor_copy(ca, hs[:, :, :, CH - 1:SEQ:CH])
                for i, d in enumerate((1, 2, 4, 8)):
                    coef(*CHUNK_POWERS[i])
                    advance(ca[:, :, :, 0:CH - d], ca[:, :, :, d:CH], CH - d)
                for r in range(2):
                    t1, t2 = (v[:, 240 * j0:240 * j1].rearrange("p (j c i) -> p j c i", j=J, c=CH - 1) for v in (s_t1, s_t2))
                    pr, pi = (v[:, sl, :].unsqueeze(2).to_broadcast([P, J, CH - 1, CH]) for v in (PWR, PWI))
                    own = ca[:, :, r, 0:CH - 1].unsqueeze(3).to_broadcast([P, J, CH - 1, CH])
                    other = ca[:, :, 1 - r, 0:CH - 1].unsqueeze(3).to_broadcast([P, J, CH - 1, CH])
                    tt(t1, pr, own, ALU.mult)
                    tt(t2, pi, other, ALU.mult)
                    eng.drain()
                    tt(t1, t1, t2, ALU.add if r else ALU.subtract)
                    eng.drain()
                    h = hs[:, :, r, CH:SEQ].rearrange("p j (c i) -> p j c i", i=CH)
                    tt(h, h, t1, ALU.add)
                    eng.drain()

            @block.sync
            def _(sp):
                def slot_load(n, later, dst, src):
                    if n >= 2 or not isinstance(later, int):
                        sp.wait_ge(used[n % 2], n // 2 + later)
                    sp.dma_start(dst, src).then_inc(full[n % 2], 16)

                def slot(n, k=16):
                    return WR[:, n % 2, 0:k, :].rearrange("p k x -> p (k x)")

                def row(name, i):
                    return T[name][bass.ds(i, 1)].rearrange("a p x -> p (a x)")

                def stream(name, first, count, k=16, peel=0, skip=0):
                    for i in range(peel):
                        slot_load(first + i, 0, slot(i, k), row(name, lay * count + i))
                    with sp.Fori(peel // 2 + skip, count // 2) as i:
                        for s in range(2):
                            if first < J_OUT:
                                sp.wait_ge(used[s], first // 2 + i)
                            else:
                                sp.wait_ge(freed[s], (first - J_OUT) // 2 + i)
                            sp.dma_start(slot(s, k), row(name, lay * count + 2 * i + s)).then_inc(full[s], 16)

                stream("w_in", J_IN, 14, peel=2)
                sp.dma_start(T["win_kept"][bass.ds(lay, 1)].rearrange("a b r x -> (a b) r x"),
                             T["win_rows"][bass.ds(lay, 1)].rearrange("a b r x -> (a b) r x")[:, NT:WIN, :])\
                    .then_inc(S["win_copied"], 16)
                stream("w_glu", J_GLU, 4, k=8)
                for k in range(2):
                    slot_load(J_W1 + k, 0, slot(k), row("cmp_w1", lay * 2 + k))
                slot_load(J_OUT, 0, slot(0), row("w_out", lay * 8))
                sp.wait_ge(S["cache0_used"], 5)
                sp.wait_ge(S["cache1_used"], 5)
                for b in range(NB):
                    sp.wait_ge(S["kring_free"], b + 1)
                    sp.dma_start(a_ring[:, 1024 * (b % 4):1024 * (b % 4) + 1024],
                                 row("win_k", lay * NB + b)).then_inc(S[f"kring{b % 4}_full"], 16)
                with sp.Fori(0, 4) as g4:
                    for b in range(NB):
                        pages(sp, "cache_slc_k", a_ring, b % 4, g4 * 4 + b * NPG, S["kring_free"], g4 * 8 + b + 9, S[f"kring{b % 4}_full"])
                sp.wait_ge(S["kring_free"], 44)
                with sp.Fori(0, NB // 2) as i:
                    for hb in range(2):
                        values(sp, i, hb, "full")
                        b = 2 * i + hb
                        sp.wait_ge(S["vring_free"], b * 5 + 5)
                        sp.dma_start(vbufs[hb][1], row("win_v", lay * NB + b)).then_inc(S[f"vwin{hb}_full"], 16)
                sp.wait_ge(S["po_done"], NQ)
                sp.wait_ge(used[1], J_OUT // 2)
                sp.dma_start(slot(1), row("w_out", lay * 8 + 1)).then_inc(full[1], 16)
                stream("w_out", J_OUT, 8, skip=1)
                stream("w_gu", J_GU, 44)
                stream("w_down", J_DN, 2 * DR)
                sp.wait_ge(S["win_copied"], 16)

            @block.gpsimd
            def _(pool):
                def row(name, i):
                    return T[name][bass.ds(i, 1)].rearrange("a p x -> p (a x)")
                pool.dma_start(PR[:, :], row("params", lay)).then_inc(S["params_in"], 16)
                pool.dma_start(lam(0, 3), row("lam", lay)).then_inc(S["ssm_in"], 16)
                pool.dma_start(s_bn, row("ssm_b", lay)).then_inc(S["ssm_in"], 16)
                pool.dma_start(s_cb, row("ssm_c", lay)).then_inc(S["ssm_in"], 16)
                pool.dma_start(s_h0, row("ssm_h0", lay)).then_inc(S["ssm_in"], 16)
                pool.dma_start(VRF[:, 0:KC * 24], row("w_gates", lay)).then_inc(S["gate_w_in"], 16)
                pool.dma_start(W2[:, :, :].rearrange("p k d -> p (k d)"), row("cmp_w2", lay)).then_inc(S["w2_in"], 16)
                with pool.Fori(0, 4) as q:
                    pool.wait_ge(S["bu_evac"], 16 * q + 18)
                    scan(pool, q, QP - POOL_PAIRS, QP)
                    pool.drain().then_inc(S["pool_scanned"], 1)
                    pool.wait_ge(S["scan_done"], q + 1)
                    pool.tensor_copy(HL[:, bass.ds(q * QP, QP), :, 0:1], HS[:, :, :, SEQ - 1:SEQ])
                    pool.tensor_copy(HL[:, bass.ds(q * QP, QP), :, 1:9], HS[:, :, :, SEQ + NT - 1:TOK:NT])\
                        .then_inc(S["state_kept"], 2)
                pool.wait_ge(S["state_kept"], 8)
                pool.dma_start(row("ssm_last", lay), s_hl).then_inc(S["states_out"], 16)
                pool.wait_ge(S["qk_normed"], 6)
                pool.wait_ge(S["proj_evac"], 16)
                pool.dma_start(row("kv_new", lay), PJ[:, T_KC:NTILE, :].rearrange("p m t -> p (m t)"))\
                    .then_inc(S["kv_out"], 16)
                pool.wait_ge(S["states_out"], 16)
                pool.wait_ge(S["y_evac"], 5)
                pool.wait_ge(S["scan_done"], 4)
                with pool.Fori(0, NB // 2) as b2:
                    for h in range(2):
                        with pool.Fori(0, NPG) as g:
                            pool.wait_ge(S[f"cache{h}_used"], b2 + 1)
                            page = pool.value_load(PG[0:1, bass.ds(b2 * 2 * NPG + h * NPG + g, 1)], min_val=0, max_val=159)
                            pool.dma_start(AR[:, bass.ds(8192 * h + g * 512, 512)], row("cache_cmp", lay * 160 + page))\
                                .then_inc(S[f"cache{h}_full"], 16)
                pool.wait_ge(S["cache0_used"], 5)
                pool.wait_ge(S["cache1_used"], 5)
                pool.dma_start(SEL3[:, 2, :], T["ties"]).then_inc(S["tie_in"], 16)
                pool.wait_ge(S["ck_normed"], NB + 1)
                with pool.Fori(0, NQ // 2) as i:
                    for j in range(2):
                        pool.wait_ge(S["ps_done"], 2 * i + j + 1)
                        pool.tensor_copy(HEADS[j].q, PJ[:, bass.ds(2 * i + j + T_Q, 1), 0:SEQ]
                                         .rearrange("p a (t s) -> p (a t) s", t=2)).then_inc(S["q_copied"], 1)
                    for b in range(NB):
                        pages(pool, "cache_slc_k", a_ring, b % 4, i * 4 + b * NPG, S["kring_free"], i * 8 + b + 9, S[f"kring{b % 4}_more"])
                with pool.Fori(0, NB // 2) as i:
                    for hb in range(2):
                        values(pool, i, hb, "more")
                for n in range(8):
                    pool.wait_ge(S["x_hi"], n + 1)
                    c = slice(4 * (n % 4), 4 * (n % 4) + 4)
                    pool.tensor_tensor(XL[:, c, :], HC[:, c, :], XH[:, c, :].bitcast(F32), ALU.subtract).then_inc(S["x_lo"], 1)
                for n, v in [("params_in", 16), ("ssm_in", 64), ("gate_w_in", 16), ("w2_in", 16), ("states_out", 16),
                             ("kv_out", 16), ("tie_in", 16), ("cache0_full", 1024), ("cache1_full", 1024)] \
                        + [(f"kring{i}_more", 256) for i in range(4)] + [(f"vbuf{i}_more", 320) for i in range(2)]:
                    pool.wait_ge(S[n], v)
                pool.dma_reset(range(handles[0].num, handles[-1].num + 1))

            def norm_squares(act, n, src, count, before=None):
                for c in range(count):
                    if c >= 2:
                        act.wait_ge(S[n + "_stat"], c - 1)
                    act.activation(SQ[:, c % 2, :], src(c), ACT.Square).then_inc(S[n + "_sq"], 1)

            def norm_sum(pe, n, count, dst):
                for c in range(count):
                    pe.wait_ge(S[n + "_sq"], c + 1)
                    pe.matmul(dst, ones, SQ[:, c % 2, :], start=c == 0, stop=c == count - 1).then_inc(S[n + "_stat"], 1)

            def norm_root(act, n, k, v, r):
                act.wait_ge(S[n + "_var"], k)
                act.activation(r, v, ACT.Sqrt).then_inc(S[n + "_root"], 1)

            def norm_var(dve, n, k, stat, v, width):
                dve.wait_ge(S[n + "_stat"], k)
                dve.tensor_scalar(v, stat, 1.0 / width, EPS, ALU.mult, ALU.add).then_inc(S[n + "_var"], 1)

            def norm_recip(dve, n, k, v, r, t):
                dve.wait_ge(S[n + "_root"], k)
                dve.reciprocal(r, r)
                dve.drain()
                dve.tensor_tensor(t, r, r, ALU.mult)
                dve.drain()
                dve.scalar_tensor_tensor(out=t, in0=t, scalar=-0.5, in1=v, op0=ALU.mult, op1=ALU.mult)
                dve.drain()
                dve.scalar_tensor_tensor(out=r, in0=t, scalar=1.5, in1=r, op0=ALU.add, op1=ALU.mult)
                dve.drain()

            def norm_all(dve, n, src, dst, gain, count, stat=4):
                norm_var(dve, n, count, bank(stat)[:, 0:TOK], NV[:, 0, :], count * P)
                norm_recip(dve, n, 1, NV[:, 0, :], NR[:, 0, :], NV[:, 1, :])
                for c in range(count):
                    dve.scalar_tensor_tensor(out=dst(c), in0=src(c), scalar=PR[:, gain + c:gain + c + 1],
                                             in1=NR[:, 0, :], op0=ALU.mult, op1=ALU.mult).then_inc(S[n + "_normed"], 1)

            def qk_set(n):
                return (SQ, NV, NR) if n % 2 == 0 else tuple(HC[:, SC + 2 * i:SC + 2 * i + 2, :] for i in range(3))

            SIG = [VRF[:, STEP * i:STEP * i + STEP].rearrange("p (m t) -> p m t", m=2) for i in range(2)]
            QK = [T_Q, T_Q + 2, T_Q + 4, T_Q + 6, T_KS, T_KW]
            QKG = [C_QN] * 4 + [C_KS, C_KW]

            @block.tensor
            def _(pe):
                for n, v in (("cache0_used", 1), ("cache1_used", 1), ("ps_done", 2), ("pt_done", 2)):
                    pe.drain().then_inc(S[n], v)
                norm_sum(pe, "mix", KC, bank(4)[:, 0:TOK])

                def products(s, wait, rhs, banks_, k=16, start=True, stop=True, first=0):
                    pe.wait_ge(full[s], wait)
                    for m in range(2):
                        for c in range(k):
                            mm = pe.matmul(banks_[:, m, 0:TOK], WR[:, s, c, 128 * m:128 * m + 128], rhs(first + c),
                                           start=start and c == 0, stop=stop and c == k - 1)
                    mm.then_inc(used[s], 1)

                def hc(c):
                    return HC[:, c, :]

                def project(s, i):
                    pe.wait_ge(S["proj_evac"], 2 * i + s + 1)
                    products(s, 16 * i + 16, hc, PS[s])

                pe.wait_ge(full[0], 16)
                for c in range(KC):
                    if c % 4 == 0:
                        pe.wait_ge(S["mix_normed"], c + 4)
                    for m in range(2):
                        mm = pe.matmul(PS[0][:, m, 0:TOK], WR[:, 0, c, 128 * m:128 * m + 128], HC[:, c, :],
                                       start=c == 0, stop=c == KC - 1)
                mm.then_inc(used[0], 1)

                def turn_b(n):
                    pe.wait_ge(S["bbar_ready"], n)
                    for r in range(2):
                        for t in range(2):
                            mm = pe.transpose(bank(4)[:, 256 * r + 128 * t:256 * r + 128 * t + 128],
                                              BBN[:, r, 4 * t:4 * t + 4, :].rearrange("p j x -> p (j x)"), ident)
                    mm.then_inc(S["bbar_turned"], 1)

                def bu(q, n):
                    pe.wait_ge(S["bbar_evac"], n)
                    for j in range(QP):
                        o = 32 * (j % 4)
                        for r in range(2):
                            k = 2 * j + r
                            pe.wait_ge(S["bu_evac"], q * 16 + k + 1)
                            pe.matmul(bank(6 + k % 2)[:, 0:TOK], BBS[o:o + 32, r, j // 4, :],
                                      NV[o:o + 32, j // 4, :],
                                      start=True, stop=True).then_inc(S["bu_done"], 1)

                def y_out(n, b_read):
                    pe.wait_ge(S["scan_done"], n)
                    pe.wait_ge(S["pool_scanned"], n)
                    pe.wait_ge(S["c_slot"], n)
                    pe.wait_ge(S["bbar_evac"], b_read)
                    for j in range(QP):
                        o = 32 * (j % 4)
                        for r in range(2):
                            mm = pe.matmul(PS[2][o:o + 32, j // 4, 0:TOK], CBS[:, j, r, :], HS[:, j, r, :],
                                           start=r == 0, stop=r == 1, tile_position=(0, o))
                    mm.then_inc(S["y_done"], 1)

                turn_b(1)
                bu(0, 1)
                project(1, 0)
                with pe.Fori(0, 3) as q:
                    pe.wait_ge(S["y_evac"], q + 1)
                    turn_b(q + 2)
                    for s in range(2):
                        project(s, 2 * q + 1)
                    y_out(q + 1, q + 2)
                    bu(q + 1, q + 2)
                    for s in range(2):
                        project(s, 2 * q + 2)
                pe.wait_ge(S["gate_w_in"], 16)
                pe.wait_ge(S["proj_evac"], 16)
                for c in range(KC):
                    mm = pe.matmul(bank(0)[0:24, 0:TOK], WG[:, c, :], HC[:, c, :], start=c == 0, stop=c == KC - 1)
                mm.then_inc(S["gates_done"], 1)
                y_out(4, 4)
                def qk_stat(n):
                    pe.wait_ge(S["qk_sq"], n + 1)
                    if n >= 2:
                        pe.wait_ge(S["qk_var"], n - 1)
                    for m in range(2):
                        mm = pe.matmul(PS[2 + n % 2][:, m, 0:TOK], ones, qk_set(n)[0][:, m, :], start=True, stop=True)
                    mm.then_inc(S["qk_stat"], 1)

                pe.wait_ge(S["bu_evac"], 66)
                pe.wait_ge(S["y_evac"], 5)
                pe.wait_ge(S["gates_sig"], 1)
                for n in range(2):
                    qk_stat(n)
                pe.wait_ge(S["z_ready"], 1)
                for n in range(4):
                    pe.wait_ge(S["glu_evac"], n + 1)
                    products(n % 2, 128 + 16 * (n // 2), lambda c: ZB[:, c, :], PS[n % 2], k=8)
                    if n < 2:
                        qk_stat(2 * n + 2)
                        qk_stat(2 * n + 3)
                pe.wait_ge(S["qk_var"], 6)
                pe.wait_ge(S["glu_evac"], 6)
                for t in range(3):
                    n = P if t < 2 else SMP
                    b_ = bank([1, 6, 7][t])
                    for i, tile in enumerate([T_VS, T_VS + 1, T_VW, T_VW + 1]):
                        pe.transpose(b_[0:n, 128 * i:128 * i + 128], PJ[:, tile, P * t:P * t + n], ident)
                    pe.transpose(bank(0)[0:n, 32 * t:32 * t + 24], GT[0:24, P * t:P * t + n], ident[0:24, 0:24])\
                        .then_inc(S["vt_done"], 1)
                pe.wait_ge(S["vr_ready"], 3)
                pe.wait_ge(S["glu_evac"], 6)
                pe.wait_ge(S["w2_in"], 16)
                for k in range(2):
                    pe.wait_ge(full[k], 16 * (J_W1 // 2 + 1))
                W1 = [WR[:, k, :, :].rearrange("p a b -> p (a b)").rearrange("p (l h) -> p l h", h=HD) for k in range(2)]
                for k in range(2):
                    for l in range(32):
                        mm = pe.matmul(bank(k)[:, 0:2 * NCMP_P], W1[k][:, l, :],
                                       PJ[:, T_KC + 2 * k:T_KC + 2 * k + 2, l:l + 16 * (NCMP_P - 1) + 1:16],
                                       start=l == 0, stop=l == 31)
                    mm.then_inc(S["conv_done"], 1)

                def second(k, item):
                    pe.wait_ge(S["hid_ready"], 2 * item + k + 1)
                    pe.wait_ge(S["ck_evac"], 2 * item + k + 1)
                    if k == 0:
                        mm = pe.matmul(bank(2)[:, 0:CW], W2[:, 0, :], HID[0], start=True, stop=True)
                    else:
                        for h in range(2):
                            mm = pe.matmul(bank(3)[0:NCMP, 128 * h:128 * h + 128], HID[1][:, NCMP * h:NCMP * h + NCMP],
                                           W2[:, 1, :], start=True, stop=True)
                    mm.then_inc(S["w2_done"], 1)

                def ck_sum(item):
                    pe.wait_ge(S["ckn_sq"], item + 1)
                    pe.matmul(bank(4)[:, 0:CW], ones, SQ[:, 0, 0:CW], start=True, stop=True).then_inc(S["ckn_stat"], 1)

                second(0, 0)
                with pe.Fori(0, NB // 2) as b2:
                    for hb in range(2):
                        item = 2 * b2 + hb
                        pe.wait_ge(S[f"cache{hb}_full"], b2 * 256 + 256)
                        for k in range(2):
                            pe.wait_ge(S["conv_evac"], 2 * item + k + 1)
                            for half in range(2):
                                for i in range(16):
                                    mm = pe.matmul(bank(k)[:, 256 * half:256 * half + 256]
                                                   .rearrange("p (h g c) -> p h g c", h=2, g=NPG),
                                                   W1[k][:, 16 * half + i, :],
                                                   CTB[hb][:, :, :, k, i, :].rearrange("p g h c -> p h g c"),
                                                   start=i == 0, stop=i == 15)
                            mm.then_inc(S["conv_done"], 1)
                            if k == 0:
                                second(1, item)
                                ck_sum(item)
                        pe.drain().then_inc(S[f"cache{hb}_used"], 1)
                        second(0, item + 1)
                second(1, NB)
                ck_sum(NB)
                for s in range(2):
                    pe.drain().then_inc(used[s], 1)
                pe.drain().then_inc(S["split_used"], 2)
                pe.drain().then_inc(S["kring_free"], 4)
                pe.drain().then_inc(S["vring_free"], 10)
                pe.wait_ge(S["ck_normed"], NB + 1)
                pe.wait_ge(S["qpad_ready"], 1)
                for k in range(NKV):
                    for b in range(NB):
                        mm = pe.matmul(bank(k)[:, 0:NCMP], QPD[:, k, b, :], CK[:, b, k, :], start=b == 0, stop=b == NB - 1)
                mm.then_inc(S["cs_done"], 1)
                for k in range(NKV):
                    pe.matmul(bank(7)[:, 64 * k:64 * k + 32], QA[:, k, :], PJ[:, T_KS + k, SEQ:TOK], start=True, stop=True)
                    mm = pe.matmul(bank(7)[:, 64 * k + 32:64 * k + 64], QA[:, k, :], PJ[:, T_KW + k, SEQ:TOK],
                                   start=True, stop=True)
                mm.then_inc(S["fresh_done"], 1)

                def keys(b, count, more=None):
                    pe.wait_ge(S[f"kring{b % 4}_full"], count)
                    if more is not None:
                        pe.wait_ge(S[f"kring{b % 4}_more"], more)
                    for k in range(NKV):
                        mm = pe.matmul(PS[1][:, k, :].rearrange("p (g s) -> p g s", g=4), QPD[:, k, b, :],
                                       KR[b % 4][:, :, k, :], start=b == 0, stop=b == NB - 1)
                    mm.then_inc(S["kring_free"], 1)
                    if b == NB - 1:
                        pe.drain().then_inc(S["kgroup_done"], 1)

                pe.wait_ge(S["kgroup_evac"], 1)
                for b in range(NB):
                    keys(b, 16 * (b // 4 + 1))
                pe.wait_ge(S["c_prob"], 1)
                for k in range(NKV):
                    mm = pe.matmul(bank(6)[32 * k:32 * k + 32, 0:NCMP], const(K_G), SCM[:, k, :], start=True, stop=True,
                                   tile_position=(0, 32 * k))
                mm.then_inc(S["gsum_done"], 1)

                def scores(n, h, k):
                    pe.wait_ge(S["q_copied"], n + 1)
                    pe.wait_ge(S["po_evac"], n + 1)
                    for t in range(2):
                        w = P * (t + 1)
                        for br, tile in enumerate((T_KS, T_KW)):
                            pe.matmul((h.s0, h.s1)[t][:, w * br:w * br + w], h.q[:, t, :], PJ[:, tile + k, 0:w],
                                      start=True, stop=True)
                        mm = pe.matmul(h.s0[:, 256 + NCMP_P * t:256 + NCMP_P * t + NCMP_P], h.q[:, t, :], CKP[:, k, :],
                                       start=True, stop=True)
                    mm.then_inc(S["ps_done"], 1)

                def turn_p(n, h):
                    pe.wait_ge(S["p_ready"], n + 1)
                    pe.wait_ge(S["pt_evac"], n + 1)
                    for br in range(2):
                        pe.transpose(bank(6)[:, 256 * br:256 * br + P], h.p0[:, br, :], ident)
                        pe.transpose(bank(6)[:, 256 * br + P:256 * br + 256], h.p1[:, br, 0:P], ident)
                        pe.transpose(bank(7)[:, P * br:P * br + P], h.p1[:, br, P:SEQ], ident)
                    for t in range(2):
                        mm = pe.transpose(bank(7)[0:NCMP_P, 256 + P * t:256 + P * t + P], h.pc[:, t, :], ident)
                    mm.then_inc(S["pt_done"], 1)

                def weigh(n, h, k):
                    pe.wait_ge(S["pt_evac"], n + 2)
                    o = h.s1
                    pe.matmul(o[:, 0:SEQ], VR[:, 0, 0, k, :], h.pt[:, 0:2, :], start=True, stop=False, skip_group_check=True)
                    pe.matmul(o[:, P:SEQ], VR[:, 1, 0, k, :], h.pt[:, 4, :], start=False, stop=False, skip_group_check=True)
                    pe.matmul(o[:, P:SEQ], VR[:, 1, 1, k, :], h.pt[:, 5, :], start=False, stop=False, skip_group_check=True)
                    pe.matmul(o[:, 0:SEQ], VR[:, 0, 1, k, :], h.pt[:, 2:4, :], start=False, stop=False, skip_group_check=True)
                    pe.matmul(o[:, 0:SEQ], CVP[0:NCMP_P, k, :], h.ptc, start=False, stop=True, skip_group_check=True)\
                        .then_inc(S["po_done"], 1)

                for k in range(NKV):
                    with pe.Fori(0, 2) as i:
                        n, g4 = 2 * i + GQA * k, i + 2 * k
                        a, b_ = HEADS
                        scores(n, a, k)
                        scores(n + 1, b_, k)
                        pe.wait_ge(S["kgroup_evac"], g4 + 2)
                        for b in range(NB):
                            if b == 4:
                                turn_p(n, a)
                            if b == 6:
                                weigh(n, a, k)
                                turn_p(n + 1, b_)
                            keys(b, g4 * 64 + 32 * (b // 4) + 64, g4 * 64 + 32 * (b // 4) + 32)
                        weigh(n + 1, b_, k)
                banks_ = [0, 1, 4, 5, 6, 7]
                pe.wait_ge(S["ranked"], 1)
                pe.wait_ge(S["fresh_evac"], 1)
                pe.wait_ge(S["sw_ready"], 3)
                blocks = [(SS, x, P) for x in range(16)] + [(SS, 16, SMP)] + [(SW, x, P) for x in range(4)] \
                    + [(SW, 4, SMP)] + [(SCM, 0, NCMP)]
                for n in range(12):
                    if n >= 6:
                        pe.wait_ge(S["st_evac"], n - 5)
                    for m, (src, x, w) in enumerate(blocks[2 * n:2 * n + 2]):
                        for k in range(NKV):
                            o = bank(banks_[n % 6])[0:w, 256 * m + 128 * k:256 * m + 128 * k + 128]
                            mm = pe.transpose(o.rearrange("p (b g t) -> p g b t", b=NB, g=GQA), src[:, k, P * x:P * x + w], ident)
                    mm.then_inc(S["st_done"], 1)
                pe.wait_ge(S["st_evac"], 12)
                norm_sum(pe, "sn", SC, bank(4)[:, 0:TOK])
                def turn_o(first):
                    pe.wait_ge(S["o_kept"], first // 4 + 1)
                    for k in range(NKV):
                        for b in range(first, first + 4):
                            mm = pe.transpose(bank(6)[:, 16 * (NB * k + b):16 * (NB * k + b) + 16],
                                              OW[0:16, k, P * (b % 4):P * (b % 4) + P], ident[0:16, 0:16])
                    mm.then_inc(S["so_done"], 1)

                for b in range(NB):
                    i, hb = divmod(b, 2)
                    out = [bank(2 * k + b // 4)[0:16, P * (b % 4):P * (b % 4) + P] for k in range(NKV)]

                    def rows(blk, k, n=P):
                        return PTS[0:n, blk, k, 16 * b:16 * b + 16]

                    for k in range(NKV):
                        pe.matmul(out[k], rows(22, k, NCMP), CV[0:NCMP, b, k, :], start=True, stop=False)
                        pe.matmul(out[k], rows(16, k, SMP), VR[0:SMP, 2, 0, k, :], start=False, stop=False)
                        pe.matmul(out[k], rows(21, k, SMP), VR[0:SMP, 2, 1, k, :], start=False, stop=False)
                    for n in range(5):
                        if n == 0:
                            for part, c in (("full", 96), ("more", 80), ("rest", 80)):
                                pe.wait_ge(S[f"vbuf{hb}_{part}"], i * c + c)
                        if n == 4:
                            pe.wait_ge(S[f"vwin{hb}_full"], i * 16 + 16)
                        for g in range(4):
                            for k in range(NKV):
                                mm = pe.matmul(out[k], rows(4 * n + g if n < 4 else 17 + g, k), VG[hb][n][:, g, k, :],
                                               start=False, stop=n == 4 and g == 3)
                        mm.then_inc(S["vring_free"], 1)
                    if b == 3:
                        pe.drain().then_inc(S["o_done"], 1)
                    if b == 5:
                        turn_o(0)
                pe.drain().then_inc(S["o_done"], 1)
                turn_o(4)
                norm_sum(pe, "an", SC, bank(5)[:, 0:TOK])
                def half(u, hf, outs, k, rhs, begin, more=None):
                    pe.wait_ge(S["wl_ready"], u + hf + 1)
                    w = len(outs) * P
                    for m, out in enumerate(outs):
                        if more is not None:
                            more(m)
                        for c in range(k):
                            col = slice(c * w + P * m, c * w + P * m + P)
                            for i, (wt, x) in enumerate(((WH, XH), (WH, XL), (WL, XH))):
                                mm = pe.matmul(out, wt[:, hf, col], x[:, rhs + c, :], start=begin and c == 0 and i == 0,
                                               stop=hf == 1 and c == k - 1 and i == 2, skip_group_check=True)
                    mm.then_inc(S["split_used"], 1)

                with pe.Fori(0, 4) as i:
                    for s in range(2):
                        pe.wait_ge(S["out_evac"], 2 * i + s + 1)
                        for hf in range(2):
                            pe.wait_ge(S["x_lo"], 2 * hf + 2)
                            half(4 * i + 2 * s, hf, [PS[s][:, m, 0:TOK] for m in range(2)], 8, 8 * hf, hf == 0)
                norm_sum(pe, "fn", KC, bank(4)[:, 0:TOK])
                with pe.Fori(0, MF // 2) as i:
                    for m in range(2):
                        pe.wait_ge(S["gu_evac"], 2 * i + m + 1)
                        for s in range(2):
                            for hf in range(2):
                                pe.wait_ge(S["x_lo"], 2 * hf + 6)
                                half(U_GU + 8 * i + 4 * m + 2 * s, hf, [PS[2 * m + s][:, t, 0:TOK] for t in range(2)], 8, 8 * hf, hf == 0)
                        pe.drain().then_inc(S["gu_done"], 1)
                pe.wait_ge(S["gu_evac"], MF + 2)
                for r in range(2):
                    def down(j, begin=False):
                        for hf in range(2):
                            half(U_DN + 2 * DR * r + 2 * j, hf, [bank(m)[:, 0:TOK] for m in range(8)], 2, 2 * hf, begin and hf == 0,
                                 (lambda m: pe.wait_ge(S["down_evac"], 4 * r + m // 2 + 1)) if begin and hf == 0 else None)
                    down(0, True)
                    with pe.Fori(0, DR // 2) as i:
                        for s in range(2):
                            down(2 * i + s + 1)
                    pe.drain().then_inc(S["down_done"], 1)

            @block.scalar
            def _(act):
                def evac(dst, src, sem, by=1):
                    act.activation(dst, src, ACT.Copy).then_inc(S[sem], by)

                act.wait_ge(S["params_in"], 16)
                act.drain().then_inc(S["proj_evac"], 2)
                act.drain().then_inc(S["bu_evac"], 2)
                act.drain().then_inc(S["pt_evac"], 1)
                norm_squares(act, "mix", lambda c: XT[:, c, :], KC)
                norm_root(act, "mix", 1, NV[:, 0, :], NR[:, 0, :])
                act.wait_ge(S["ssm_in"], 64)
                act.activation(lam(3), lam(2), ACT.Exp).then_inc(S["lam_dt"], 1)
                act.wait_ge(S["lam_xr"], 1)
                act.activation(lam(6), lam(4), ACT.Exp).then_inc(S["lam_mag"], 1)
                act.activation(lam(9), lam(7), ACT.Sin)
                act.activation(lam(10), lam(8), ACT.Sin).then_inc(S["lam_sin"], 1)
                def project_out(s, i):
                    act.wait_ge(used[s], i + 1)
                    evac(PJ[:, bass.ds(4 * i + 2 * s, 2), :], PS[s][:, :, 0:TOK], "proj_evac")

                project_out(0, 0)

                def b_slot(q):
                    act.wait_ge(S["proj_evac"], q + 3)
                    act.wait_ge(S["bbar_turned"], q + 1)
                    act.activation(NV[:, :, :], PJ[:, bass.ds(2 * q, 2), :], ACT.Copy)
                    act.activation(s_bbs, bank(4), ACT.Copy)
                    act.drain().then_inc(S["bbar_evac"], 1)

                def c_slot(q):
                    act.activation(CBS[:, :, 0, :], CB[:, bass.ds(q * QP, QP), 0, :], ACT.Copy)
                    act.mul(CBS[:, :, 1, :], CB[:, bass.ds(q * QP, QP), 1, :], -1.0)
                    act.drain().then_inc(S["c_slot"], 1)

                def states(q):
                    for k in range(16):
                        act.wait_ge(S["bu_done"], q * 16 + k + 1)
                        evac(HS[:, k // 2, k % 2, :], bank(6 + k % 2)[:, 0:TOK], "bu_evac")

                b_slot(0)
                c_slot(0)
                states(0)
                project_out(1, 0)
                with act.Fori(0, 3) as q:
                    b_slot(q + 1)
                    for s in range(2):
                        project_out(s, 2 * q + 1)
                    act.wait_ge(S["y_done"], q + 1)
                    c_slot(q + 1)
                    act.wait_ge(S["state_kept"], 2 * q + 2)
                    states(q + 1)
                    for s in range(2):
                        project_out(s, 2 * q + 2)
                act.wait_ge(S["gates_done"], 1)
                act.activation(GT[:, :], bank(0)[0:24, 0:TOK], ACT.Sigmoid).then_inc(S["gates_sig"], 1)
                for n in range(2):
                    act.activation(qk_set(n)[0][:, :, :], PJ[:, QK[n]:QK[n] + 2, :], ACT.Square).then_inc(S["qk_sq"], 1)
                act.wait_ge(S["y_evac"], 5)
                act.activation(ZB[:, :, :], ZB[:, :, :], ACT.Gelu_apprx_tanh).then_inc(S["z_ready"], 1)

                def qk_square(n):
                    act.activation(qk_set(n)[0][:, :, :], PJ[:, QK[n]:QK[n] + 2, :], ACT.Square).then_inc(S["qk_sq"], 1)

                def qk_root(n):
                    norm_root(act, "qk", n + 1, qk_set(n)[1][:, :, :], qk_set(n)[2][:, :, :])

                def glu_gate(n):
                    act.wait_ge(used[n % 2], 8 + n // 2)
                    act.activation(SIG[n % 2], PS[n % 2][:, :, 0:TOK], ACT.Sigmoid).then_inc(S["glu_sig"], 1)

                qk_root(0)
                qk_root(1)
                for n in range(2):
                    qk_square(2 * n + 2)
                    qk_square(2 * n + 3)
                    glu_gate(n)
                    qk_root(2 * n + 2)
                    qk_root(2 * n + 3)
                for n in range(2, 4):
                    act.wait_ge(S["glu_evac"], n + 1)
                    glu_gate(n)

                def hidden(k, n):
                    act.wait_ge(S["hid_pre"], n)
                    act.activation(HID[k], HID[k], ACT.Gelu_apprx_tanh,
                                   bias=PR[:, C_B1 + k:C_B1 + k + 1]).then_inc(S["hid_ready"], 1)

                def squares(item):
                    act.wait_ge(S["ck_evac"], 2 * item + 3)
                    act.activation(SQ[:, 0, 0:CW], ubuf[:, bass.ds(item * CW, CW)], ACT.Square).then_inc(S["ckn_sq"], 1)

                for k in range(2):
                    hidden(k, k + 1)
                squares(0)
                with act.Fori(0, NB) as item:
                    hidden(0, 2 * item + 3)
                    norm_root(act, "ckn", item + 1, NV[:, 0, 0:CW], NR[:, 0, 0:CW])
                    hidden(1, 2 * item + 4)
                    squares(item + 1)
                norm_root(act, "ckn", NB + 1, NV[:, 0, 0:CW], NR[:, 0, 0:CW])
                act.wait_ge(S["c_max"], 1)
                for k in range(NKV):
                    act.activation(SCM[:, k, :], SCM[:, k, :], ACT.Exp, bias=SM[:, 32 + k:33 + k], accum_out=SM[:, 34 + k:35 + k])
                act.drain().then_inc(S["c_exp"], 1)
                with act.Fori(0, NQ // 2) as i:
                    for j, h in enumerate(HEADS):
                        act.wait_ge(S["ps_max"], 2 * i + j + 1)
                        for c, v in enumerate([h.p1[:, 0], h.p1[:, 1], h.p0[:, 0], h.p0[:, 1], h.pc[:, 0], h.pc[:, 1]]):
                            act.activation(v, v, ACT.Exp, bias=h.m[:, c:c + 1], accum_out=h.d[:, c:c + 1])
                        act.drain().then_inc(S["p_exp"], 1)
                    for j, h in enumerate(HEADS):
                        act.wait_ge(S["pt_done"], 2 * i + j + 3)
                        act.activation(h.pt[:, 0:4, :].rearrange("p n s -> p (n s)"), bank(6), ACT.Copy)
                        act.activation(h.pt[:, 4:6, :].rearrange("p n s -> p (n s)"), bank(7)[:, 0:256], ACT.Copy)
                        act.activation(h.ptc, bank(7)[0:NCMP_P, 256:512], ACT.Copy)
                        act.drain().then_inc(S["pt_evac"], 1)
                values(act, 0, 0, "rest")
                act.wait_ge(S["sw_max"], 1)
                for k in range(NKV):
                    for i, v in enumerate((SS, SW)):
                        act.activation(v[:, k, :], v[:, k, :], ACT.Exp, bias=SM[:, 54 + 2 * i + k:55 + 2 * i + k],
                                       accum_out=SM[:, 58 + 2 * i + k:59 + 2 * i + k])
                act.drain().then_inc(S["sw_exp"], 1)
                widths = [P] * 16 + [SMP] + [P] * 4 + [SMP] + [NCMP]
                for n in range(12):
                    act.wait_ge(S["st_done"], n + 1)
                    w = widths[2 * n:2 * n + 2]
                    src = bank([0, 1, 4, 5, 6, 7][n % 6])
                    if len(set(w)) == 1:
                        act.activation(PTS[0:w[0], 2 * n:2 * n + len(w), :, :].rearrange("p n k r -> p (n k r)"),
                                       src[0:w[0], 0:256 * len(w)], ACT.Copy)
                    else:
                        for m in range(2):
                            act.activation(PTS[0:w[m], 2 * n + m, :, :].rearrange("p k r -> p (k r)"),
                                           src[0:w[m], 256 * m:256 * m + 256], ACT.Copy)
                    act.drain().then_inc(S["st_evac"], 1)
                values(act, 0, 1, "rest")
                norm_squares(act, "sn", lambda c: HC[:, c, :], SC)
                norm_root(act, "sn", 1, NV[:, 0, :], NR[:, 0, :])
                act.wait_ge(S["sn_stat"], SC)
                with act.Fori(1, NB // 2) as i:
                    for hb in range(2):
                        values(act, i, hb, "rest")
                act.wait_ge(S["so_evac"], 2)
                norm_squares(act, "an", lambda c: HC[:, SC + c, :], SC)
                norm_root(act, "an", 1, NV[:, 0, :], NR[:, 0, :])
                act.wait_ge(S["an_stat"], SC)

                def high(s, full_, u, hidden_=None, halves=range(2)):
                    for hf in halves:
                        if hf == 0:
                            act.wait_ge(full[s], full_)
                        act.wait_ge(S["split_used"], u + hf + 1)
                        w = act.activation(WH[:, hf, :], WR[:, s, 8 * hf:8 * hf + 8, :].rearrange("p a b -> p (a b)"), ACT.Copy)
                        if hidden_ is not None:
                            w = act.activation(XH[:, 2 * hf:2 * hf + 2, :], HT[:, bass.ds(hidden_ + 2 * hf, 2), :], ACT.Copy)
                        act.drain().then_inc(S["wh_ready"], 1)

                def high_x(n, sem, count):
                    act.wait_ge(S[sem], count)
                    c = slice(4 * (n % 4), 4 * (n % 4) + 4)
                    act.activation(XH[:, c, :], HC[:, c, :], ACT.Copy).then_inc(S["x_hi"], 1)

                F_OUT, F_GU, F_DN = (16 * (j // 2 + 1) for j in (J_OUT, J_GU, J_DN))
                for n in range(4):
                    high_x(n, "an_normed" if n >= 2 else "sn_normed", 4 * (n % 2) + 4)
                with act.Fori(0, 4) as i:
                    for s in range(2):
                        high(s, F_OUT + 16 * i, 4 * i + 2 * s)
                act.wait_ge(S["out_evac"], 10)
                norm_squares(act, "fn", lambda c: XT[:, c, :], KC)
                norm_root(act, "fn", 1, NV[:, 0, :], NR[:, 0, :])
                for n in range(4, 8):
                    high_x(n, "fn_normed", 4 * (n - 4) + 4)

                def high_pair(p):
                    for s in range(2):
                        high(s, F_GU + 16 * p, U_GU + 4 * p + 2 * s)

                def silu(p, m):
                    act.wait_ge(S["gu_done"], p + 1)
                    act.wait_ge(S["gu_evac"], p + 1)
                    act.activation((NV, NR)[m][:, :, :], PS[2 * m][:, :, 0:TOK], ACT.Silu).then_inc(S["silu_ready"], 1)

                high_pair(0)
                with act.Fori(0, MF // 2 - 1) as i:
                    for m in range(2):
                        high_pair(2 * i + m + 1)
                        silu(2 * i + m, m)
                high_pair(MF - 1)
                silu(MF - 2, 0)
                act.wait_ge(S["split_used"], U_DN + 1)
                act.wait_ge(S["gu_evac"], MF)
                high(0, F_DN, U_DN, 0, halves=(0,))
                silu(MF - 1, 1)
                act.wait_ge(S["gu_evac"], MF + 2)
                for r in range(2):
                    def down(j, s):
                        n = DR * r + j
                        high(s, 16 * ((J_DN + n - s) // 2 + 1), U_DN + 2 * n, 4 * j)
                    if r == 0:
                        high(0, F_DN, U_DN, 0, halves=(1,))
                    else:
                        down(0, 1)
                    with act.Fori(0, DR // 2) as i:
                        for t in range(2):
                            s = (r + t + 1) % 2
                            n = DR * r + t + 1
                            high(s, 16 * i + 16 * ((J_DN + n - s) // 2 + 1), 4 * i + U_DN + 2 * n, 8 * i + 4 * t + 4)

            @block.vector
            def _(dve):
                def tt(out, a, b, op):
                    return dve.tensor_tensor(out, a, b, op)

                for n, v in (("glu_evac", 2), ("out_evac", 2), ("gu_evac", 2), ("down_evac", 4),
                             ("y_evac", 1), ("po_evac", 2), ("kgroup_evac", 1), ("ck_evac", 2)):
                    dve.drain().then_inc(S[n], v)
                dve.wait_ge(S["params_in"], 16)
                norm_all(dve, "mix", lambda c: XT[:, c, :], lambda c: HC[:, c, :], C_MIX, KC)
                dve.tensor_scalar(PR[:, C_QN:C_QN + 1], PR[:, C_QN:C_QN + 1], SCALE, None, ALU.mult).then_inc(S["qgain"], 1)
                dve.wait_ge(S["lam_dt"], 1)
                LRE, LIM, DT, XR, XI, MAG, RA, RH, SN, SH, AR_, AI_, T1, T2 = (lam(i) for i in (0, 1, 3, 4, 5, 6, 7, 8, 9, 10, 11, 12, 13, 14))
                CR, CI, NR_, DEN, AIN = lam(15), lam(16), lam(17), lam(18), lam(19)
                tt(XR, LRE, DT, ALU.mult)
                tt(XI, LIM, DT, ALU.mult)
                dve.drain()
                magic = 12582912.0
                dve.tensor_scalar(T1, XI, float(1 / (2 * np.pi)), magic, ALU.mult, ALU.add)
                dve.drain()
                dve.tensor_scalar(T1, T1, -magic, None, ALU.add)
                dve.drain()
                c1 = 6.28125
                c2 = float(np.float32(2 * np.pi - c1))
                c3 = float(2 * np.pi - c1 - c2)
                dve.scalar_tensor_tensor(out=RA, in0=T1, scalar=-c1, in1=XI, op0=ALU.mult, op1=ALU.add)
                dve.drain()
                dve.scalar_tensor_tensor(out=RA, in0=T1, scalar=-c2, in1=RA, op0=ALU.mult, op1=ALU.add)
                dve.drain()
                dve.scalar_tensor_tensor(out=RA, in0=T1, scalar=-c3, in1=RA, op0=ALU.mult, op1=ALU.add)
                dve.drain()
                dve.tensor_scalar(RA, RA, 3.1415925, -3.1415925, ALU.min, ALU.max)
                dve.drain()
                dve.tensor_scalar(RH, RA, 0.5, None, ALU.mult)
                dve.drain().then_inc(S["lam_xr"], 1)
                dve.wait_ge(S["lam_sin"], 1)
                tt(T1, SH, SH, ALU.mult)
                tt(AI_, MAG, SN, ALU.mult)
                dve.drain()
                dve.tensor_scalar(T1, T1, -2.0, 1.0, ALU.mult, ALU.add)
                dve.drain()
                tt(AR_, MAG, T1, ALU.mult)
                dve.drain()
                tt(T1, LRE, LRE, ALU.mult)
                tt(T2, LIM, LIM, ALU.mult)
                dve.drain()
                tt(DEN, T1, T2, ALU.add)
                dve.tensor_scalar(NR_, AR_, -1.0, None, ALU.add)
                dve.tensor_scalar(AIN, AI_, -1.0, None, ALU.mult)
                dve.drain()
                dve.reciprocal(DEN, DEN)
                tt(T1, NR_, LRE, ALU.mult)
                tt(T2, AI_, LIM, ALU.mult)
                dve.drain()
                tt(CR, T1, T2, ALU.add)
                dve.drain()
                tt(CR, CR, DEN, ALU.mult)
                dve.drain()
                tt(T1, AI_, LRE, ALU.mult)
                tt(T2, NR_, LIM, ALU.mult)
                dve.drain()
                tt(CI, T1, T2, ALU.subtract)
                dve.drain()
                tt(CI, CI, DEN, ALU.mult)

                def cmul(outr, outi, ar, ai, br, bi, t1, t2):
                    tt(t1, ar, br, ALU.mult)
                    tt(t2, ai, bi, ALU.mult)
                    dve.drain()
                    tt(outr, t1, t2, ALU.subtract)
                    dve.drain()
                    tt(t1, ar, bi, ALU.mult)
                    tt(t2, ai, br, ALU.mult)
                    dve.drain()
                    tt(outi, t1, t2, ALU.add)
                    dve.drain()

                dve.tensor_copy(PWR[:, :, 0], AR_)
                dve.tensor_copy(PWI[:, :, 0], AI_)
                dve.drain()
                for k in (1, 2, 4, 8):
                    tr = s_t1[:, 0:32 * k].rearrange("p (j i) -> p j i", i=k)
                    ti = s_t2[:, 0:32 * k].rearrange("p (j i) -> p j i", i=k)
                    cmul(PWR[:, :, k:2 * k], PWI[:, :, k:2 * k], PWR[:, :, 0:k], PWI[:, :, 0:k],
                         PWR[:, :, k - 1:k].to_broadcast([P, NPAIR, k]), PWI[:, :, k - 1:k].to_broadcast([P, NPAIR, k]), tr, ti)
                for i in range(3):
                    cmul(*CHUNK_POWERS[i + 1], *CHUNK_POWERS[i], *CHUNK_POWERS[i], T1, T2)

                def bbar(q, n):
                    if n is not None:
                        dve.wait_ge(S["bbar_turned"], n)
                    sl = bass.ds(q * QP, QP)
                    b_ = [BN[:, r, sl, :] for r in range(2)]
                    cr, ci = (v[:, sl].unsqueeze(2).to_broadcast([P, QP, 32]) for v in (CR, CI))
                    t1, t2 = (v[:, 0:256].rearrange("p (j x) -> p j x", j=QP) for v in (s_t1, s_t2))
                    cmul(BBN[:, 0], BBN[:, 1], cr, ci, b_[0], b_[1], t1, t2)
                    dve.drain().then_inc(S["bbar_ready"], 1)

                def y_evac(q, n):
                    dve.wait_ge(S["y_done"], n)
                    for t in range(2):
                        dve.scalar_tensor_tensor(out=ZB[:, bass.ds(2 * q + t, 1), :].rearrange("p a t -> p (a t)"),
                                                 in0=PJ[:, bass.ds(2 * q + t, 1), :].rearrange("p a t -> p (a t)"),
                                                 scalar=PR[:, bass.ds(C_D + 2 * q + t, 1)],
                                                 in1=PS[2][:, t, 0:TOK], op0=ALU.mult, op1=ALU.add)
                    dve.drain().then_inc(S["y_evac"], 1)

                bbar(0, None)
                with dve.Fori(0, 3) as q:
                    bbar(q + 1, q + 1)
                    dve.wait_ge(S["bu_evac"], 16 * q + 18)
                    scan(dve, q, 0, QP - POOL_PAIRS)
                    dve.drain().then_inc(S["scan_done"], 1)
                    y_evac(q, q + 1)
                dve.wait_ge(S["bu_evac"], 66)
                scan(dve, 3, 0, QP - POOL_PAIRS)
                dve.drain().then_inc(S["scan_done"], 1)
                dve.wait_ge(S["proj_evac"], 16)
                y_evac(3, 4)
                def qk_var(n):
                    norm_var(dve, "qk", n + 1, PS[2 + n % 2][:, :, 0:TOK], qk_set(n)[1][:, :, :], HD)

                def qk_norm(n):
                    _, v, r = qk_set(n)
                    tile = QK[n]
                    norm_recip(dve, "qk", n + 1, v[:, :, :], r[:, :, :], HC[:, SC + 6:SC + 8, :])
                    dve.scalar_tensor_tensor(out=PJ[:, tile:tile + 2, :], in0=PJ[:, tile:tile + 2, :],
                                             scalar=PR[:, QKG[n]:QKG[n] + 1], in1=r[:, :, :],
                                             op0=ALU.mult, op1=ALU.mult)
                    dve.drain().then_inc(S["qk_normed"], 1)

                def glu(n):
                    dve.wait_ge(S["glu_sig"], n + 1)
                    tt(HC[:, 2 * n:2 * n + 2, :], ZB[:, 2 * n:2 * n + 2, :], SIG[n % 2], ALU.mult).then_inc(S["glu_evac"], 1)

                qk_var(0)
                qk_var(1)
                for n in range(2):
                    qk_norm(2 * n)
                    qk_norm(2 * n + 1)
                    qk_var(2 * n + 2)
                    qk_var(2 * n + 3)
                    glu(n)
                qk_norm(4)
                glu(2)
                qk_norm(5)
                glu(3)
                for t in range(3):
                    n = P if t < 2 else SMP
                    if t == 0:
                        dve.wait_ge(S["vt_done"], 3)
                    dve.tensor_copy(VRF[0:n, 512 * t:512 * t + 512], bank([1, 6, 7][t])[0:n, :])
                    dve.tensor_copy(GR[0:n, t, :], bank(0)[0:n, 32 * t:32 * t + 24])
                    dve.drain().then_inc(S["vr_ready"], 1)
                for g in range(GQA):
                    for k in range(NKV):
                        at_ = 3 * (GQA * k + g)
                        dve.tensor_copy(GS[32 * g:32 * g + 32, k, :], GR[0:SMP, 2, at_:at_ + 3])
                def pre(k, item):
                    dve.wait_ge(S["conv_done"], 2 * item + k + 1)
                    hid = HID[k].rearrange("p (h c) -> p h c", h=2)
                    if isinstance(item, int):
                        dve.tensor_copy(hid[:, :, 0:NCMP_P], bank(k)[:, 0:2 * NCMP_P].rearrange("p (h c) -> p h c", h=2))
                    else:
                        dve.tensor_copy(c_hb, bank(k)[:, 256:512])
                        dve.drain()
                        tt(hid, bank(k)[:, 0:256].rearrange("p (h c) -> p h c", h=2)[:, :, 0:NCMP],
                           c_hb.rearrange("p (h c) -> p h c", h=2)[:, :, 1:128], ALU.add)
                    dve.drain().then_inc(S["hid_pre"], 1)
                    dve.drain().then_inc(S["conv_evac"], 1)

                def ck_out(item):
                    dve.wait_ge(S["w2_done"], 2 * item + 1)
                    dve.tensor_copy(ubuf[:, bass.ds(item * CW, CW)], bank(2)[:, 0:CW]).then_inc(S["ck_evac"], 1)

                def cv_out(item):
                    dve.wait_ge(S["w2_done"], 2 * item + 2)
                    dve.tensor_copy(zbuf[0:NCMP, bass.ds(item * 256, 256)], bank(3)[0:NCMP, 0:256]).then_inc(S["ck_evac"], 1)

                def ck_norm(item):
                    v, r = NV[:, 0, 0:CW], NR[:, 0, 0:CW]
                    norm_var(dve, "ckn", item + 1, bank(4)[:, 0:CW], v, HD)
                    norm_recip(dve, "ckn", item + 1, v, r, SQ[:, 1, 0:CW])
                    c = ubuf[:, bass.ds(item * CW, CW)]
                    dve.scalar_tensor_tensor(out=c, in0=c, scalar=PR[:, C_KC:C_KC + 1], in1=r, op0=ALU.mult, op1=ALU.mult)
                    dve.drain().then_inc(S["ck_normed"], 1)

                dve.wait_ge(S["glu_evac"], 6)
                for k in range(2):
                    dve.memset(HID[k], 0.0)
                dve.drain()
                for k in range(2):
                    pre(k, 0)
                ck_out(0)
                with dve.Fori(0, NB) as item:
                    pre(0, item + 1)
                    cv_out(item)
                    ck_norm(item)
                    pre(1, item + 1)
                    ck_out(item + 1)
                cv_out(NB)
                ck_norm(NB)
                dve.memset(QPF, 0.0)
                dve.drain()
                for k in range(NKV):
                    for g in range(GQA):
                        base = QPD[:, k, 0, 32 * g:32 * g + NT]
                        dst = bass.AP(base.tensor, base.offset, [list(base.ap[0]), [P + NT, NB], [1, NT]])
                        dve.tensor_copy(dst, PJ[:, T_Q + GQA * k + g, SEQ:TOK].rearrange("p (b t) -> p b t", b=NB))
                    dve.tensor_copy(QA[:, k, :].rearrange("p (g r) -> p g r", g=GQA), PJ[:, T_Q + GQA * k:T_Q + GQA * k + GQA, SEQ:TOK])
                dve.drain().then_inc(S["qpad_ready"], 1)
                ds_, dw, dc, slr = const(K_DS), const(K_DW), const(K_DC), const(K_SLR)

                def biased(out, dist, k, scores):
                    dve.scalar_tensor_tensor(out=out, in0=dist, scalar=slr[:, k:k + 1], in1=scores, op0=ALU.mult, op1=ALU.add)

                dve.wait_ge(S["cs_done"], 1)
                for k in range(NKV):
                    biased(SCM[:, k, :], dc, k, bank(k)[:, 0:NCMP])
                dve.drain()
                dve.tensor_reduce(SM[:, 32:34], SCM, AXX, ALU.max)
                dve.drain()
                dve.tensor_scalar(SM[:, 32:34], SM[:, 32:34], -1.0, None, ALU.mult).then_inc(S["c_max"], 1)
                dve.wait_ge(S["fresh_done"], 1)
                for k in range(NKV):
                    biased(SS[:, k, PAST:NS], ds_[:, PAST:NS], k, bank(7)[:, 64 * k:64 * k + 32])
                    biased(SW[:, k, WIN:NW], dw[:, WIN:NW], k, bank(7)[:, 64 * k + 32:64 * k + 64])
                dve.drain().then_inc(S["fresh_evac"], 1)
                mxs, mxw = (SM[:, o:o + 2 * c].rearrange("p (k g) -> p k g", k=2) for o, c in ((40, 5), (50, 2)))
                dve.tensor_reduce(mxs[:, :, 4], SS[:, :, PAST:NS], AXX, ALU.max)
                dve.tensor_reduce(mxw[:, :, 1], SW[:, :, WIN:NW], AXX, ALU.max)
                dve.wait_ge(S["c_exp"], 1)
                dve.tensor_scalar(SM[:, 34:36], SM[:, 34:36], TINY, None, ALU.max)
                dve.drain()
                dve.reciprocal(SM[:, 34:36], SM[:, 34:36])
                dve.drain()
                for k in range(NKV):
                    dve.tensor_scalar(SCM[:, k, :], SCM[:, k, :], SM[:, 34 + k:35 + k], None, ALU.mult)
                dve.drain()
                dve.scalar_tensor_tensor(out=SCM, in0=SCM, scalar=TINY, in1=SCM, op0=ALU.is_ge, op1=ALU.mult)
                dve.drain().then_inc(S["c_prob"], 1)
                dve.wait_ge(S["kgroup_done"], 1)
                for k in range(NKV):
                    biased(SW[:, k, 0:WIN], dw[:, 0:WIN], k, PS[1][:, k, :])
                dve.drain().then_inc(S["kgroup_evac"], 1)
                dve.tensor_reduce(mxw[:, :, 0], SW[:, :, 0:WIN], AXX, ALU.max)
                dve.memset(PPD, 0.0)
                dve.memset(SCR, 0.0)
                dve.drain()
                dve.wait_ge(S["gsum_done"], 1)
                dve.tensor_copy(PPD[:, 1:128], bank(6)[0:64, 0:NCMP])
                dve.drain()
                dve.tensor_reduce(SUM2[:, 0:32], PPD[:, 1:129].rearrange("p (j c) -> p j c", c=4), AXX, ALU.add)
                dve.tensor_reduce(SUM2[:, 32:64], PPD[:, 0:128].rearrange("p (j c) -> p j c", c=4), AXX, ALU.add)
                dve.drain()
                tt(SCR[:, 0:32], SUM2[:, 0:32], SUM2[:, 32:64], ALU.add)
                dve.drain()
                tt(SCR, SCR, const(K_FRC)[0:64, :], ALU.max)
                dve.drain()
                other = SCR.unsqueeze(1).to_broadcast([64, NBLK, NBLK])
                own = SCR.unsqueeze(2).to_broadcast([64, NBLK, NBLK])
                sel = [SEL3[:, n, :].rearrange("p (j i) -> p j i", j=NBLK) for n in range(3)]
                tt(sel[0], other, own, ALU.is_gt)
                tt(sel[1], other, own, ALU.is_equal)
                dve.drain()
                dve.wait_ge(S["tie_in"], 16)
                tt(sel[1], sel[1], sel[2], ALU.mult)
                dve.drain()
                tt(sel[0], sel[0], sel[1], ALU.add)
                dve.drain()
                dve.tensor_reduce(RNK, sel[0], AXX, ALU.add)
                dve.drain()
                dve.tensor_scalar(RNK, RNK, float(NSEL), MASKED, ALU.is_ge, ALU.mult)
                dve.drain()
                for g in range(GQA):
                    for k in range(NKV):
                        dve.tensor_copy(MB[32 * g:32 * g + 32, k, :], RNK[32 * k:32 * k + 32, 0:32])
                dve.drain().then_inc(S["ranked"], 1)
                d1, dcp, slh = const(K_D1), const(K_DCP), const(K_SLH)

                def prompt_bias(n, h):
                    dve.wait_ge(S["ps_done"], n + 3)
                    dve.wait_ge(S["pt_done"], n + 1)
                    slope = slh[:, bass.ds(n, 1)]
                    for v, ps, w in ((h.p1, h.s1, 256), (h.p0, h.s0, 128)):
                        dve.scalar_tensor_tensor(out=v, in0=d1[:, SEQ - w:SEQ].unsqueeze(1).to_broadcast([P, 2, w]), scalar=slope,
                                                 in1=ps[:, 0:2 * w].rearrange("p (b s) -> p b s", b=2),
                                                 op0=ALU.mult, op1=ALU.add)
                    dve.scalar_tensor_tensor(out=h.pc, in0=dcp, scalar=slope, in1=h.s0[:, 256:256 + 2 * NCMP_P],
                                             op0=ALU.mult, op1=ALU.add)
                    dve.drain()
                    for c, v in enumerate((h.p1, h.p0, h.pc)):
                        dve.tensor_reduce(h.m[:, 2 * c:2 * c + 2], v, AXX, ALU.max)
                    dve.drain()
                    dve.tensor_scalar(h.m, h.m, -1e20, -1.0, ALU.max, ALU.mult).then_inc(S["ps_max"], 1)

                def prompt_scale(n, h):
                    dve.wait_ge(S["p_exp"], n + 1)
                    f = h.d
                    dve.tensor_scalar(f, f, TINY, None, ALU.max)
                    dve.drain()
                    dve.reciprocal(f, f)
                    dve.drain()
                    tt(f[:, 0:2], f[:, 0:2], GR[:, 1, bass.ds(3 * n + 1, 2)], ALU.mult)
                    tt(f[:, 2:4], f[:, 2:4], GR[:, 0, bass.ds(3 * n + 1, 2)], ALU.mult)
                    tt(f[:, 4:6], f[:, 4:6], GR[:, 0:2, bass.ds(3 * n, 1)].rearrange("p t a -> p (t a)"), ALU.mult)
                    dve.drain()
                    for c, (v, w) in enumerate(((h.p1, 256), (h.p0, 128), (h.pc, NCMP_P))):
                        tt(v, v, f[:, 2 * c:2 * c + 2].unsqueeze(2).to_broadcast([P, 2, w]), ALU.mult)
                    dve.drain().then_inc(S["p_ready"], 1)

                def prompt_out(n, h):
                    dve.wait_ge(S["po_done"], n + 1)
                    dve.tensor_copy(HC[:, bass.ds(n + SC, 1), 0:SEQ].rearrange("p a s -> p (a s)"), h.s1[:, 0:SEQ])\
                        .then_inc(S["po_evac"], 1)

                with dve.Fori(0, 4) as i:
                    a, b_ = HEADS
                    n = 2 * i
                    prompt_bias(n, a)
                    prompt_bias(n + 1, b_)
                    prompt_scale(n, a)
                    prompt_scale(n + 1, b_)
                    prompt_out(n, a)
                    dve.wait_ge(S["kgroup_done"], i + 2)
                    for k in range(NKV):
                        biased(SS[:, k, bass.ds(i * 512, 512)], ds_[:, bass.ds(i * 512, 512)], k, PS[1][:, k, :])
                    dve.drain().then_inc(S["kgroup_evac"], 1)
                    prompt_out(n + 1, b_)
                    for k in range(NKV):
                        v = SS[:, k, bass.ds(i * 512, 512)].rearrange("p (j s) -> p j s", s=SEL)
                        tt(v, v, MB[:, k, bass.ds(i * 8, 8)].unsqueeze(2).to_broadcast([P, 8, SEL]), ALU.add)
                    dve.drain()
                    for k in range(NKV):
                        dve.tensor_reduce(mxs[:, k, bass.ds(i, 1)], SS[:, k, bass.ds(i * 512, 512)], AXX, ALU.max)
                dve.drain()
                dve.tensor_reduce(SM[:, 54:56], mxs, AXX, ALU.max)
                dve.tensor_reduce(SM[:, 56:58], mxw, AXX, ALU.max)
                dve.drain()
                dve.tensor_scalar(SM[:, 54:58], SM[:, 54:58], -1.0, None, ALU.mult).then_inc(S["sw_max"], 1)
                dve.wait_ge(S["gsum_done"], 1)
                for k in range(NKV):
                    dve.tensor_scalar(SCM[:, k, :], SCM[:, k, :], GS[:, k, 0:1], None, ALU.mult)
                dve.drain().then_inc(S["sw_ready"], 1)
                dve.wait_ge(S["sw_exp"], 1)
                f = SM[:, 58:62]
                dve.tensor_scalar(f, f, TINY, None, ALU.max)
                dve.drain()
                dve.reciprocal(f, f)
                dve.drain()
                for i in range(2):
                    tt(f[:, 2 * i:2 * i + 2], f[:, 2 * i:2 * i + 2], GS[:, :, 1 + i], ALU.mult)
                dve.drain()
                for i, v in enumerate((SS, SW)):
                    for k in range(NKV):
                        dve.tensor_scalar(v[:, k, :], v[:, k, :], f[:, 2 * i + k:2 * i + k + 1], None, ALU.mult)
                    dve.drain().then_inc(S["sw_ready"], 1)
                norm_all(dve, "sn", lambda c: HC[:, c, :], lambda c: HC[:, c, :], C_NSSM, SC)
                dve.drain()
                for i in range(2):
                    dve.wait_ge(S["o_done"], i + 1)
                    if i:
                        dve.wait_ge(S["so_done"], 1)
                    for k in range(NKV):
                        dve.tensor_copy(OW[0:16, k, :], bank(2 * k + i)[0:16, :])
                    dve.drain().then_inc(S["o_kept"], 1)
                dve.wait_ge(S["so_done"], 2)
                for k in range(NKV):
                    dve.tensor_copy(HC[:, SC + GQA * k:SC + GQA * k + GQA, SEQ:TOK].rearrange("p g (b t) -> p g b t", t=NT),
                                    bank(6)[:, P * k:P * k + P].rearrange("p (b g t) -> p g b t", b=NB, g=GQA))\
                        .then_inc(S["so_evac"], 1)
                norm_all(dve, "an", lambda c: HC[:, SC + c, :], lambda c: HC[:, SC + c, :], C_NATT, SC, stat=5)
                def low_half(s, u, hf, hidden_=None):
                    dve.wait_ge(S["wh_ready"], u + hf + 1)
                    tt(WL[:, hf, :], WR[:, s, 8 * hf:8 * hf + 8, :].rearrange("p a b -> p (a b)"), WH[:, hf, :].bitcast(F32), ALU.subtract)
                    if hidden_ is not None:
                        tt(XL[:, 2 * hf:2 * hf + 2, :], HT[:, bass.ds(hidden_ + 2 * hf, 2), :],
                           XH[:, 2 * hf:2 * hf + 2, :].bitcast(F32), ALU.subtract)
                    dve.drain().then_inc(S["wl_ready"], 1)
                    if hf == 1:
                        dve.drain().then_inc(freed[s], 1)

                def low(s, u, hidden_=None):
                    for hf in range(2):
                        low_half(s, u, hf, hidden_)

                def out_add(j, s):
                    dve.wait_ge(S["split_used"], 2 * j + 4)
                    v = XT[:, bass.ds(2 * j, 2), :]
                    tt(v, PS[s][:, :, 0:TOK], v, ALU.add).then_inc(S["out_evac"], 1)

                low(0, 0)
                with dve.Fori(0, 3) as i:
                    low(1, 4 * i + 2)
                    out_add(2 * i, 0)
                    low(0, 4 * i + 4)
                    out_add(2 * i + 1, 1)
                low(1, 14)
                out_add(6, 0)
                out_add(7, 1)
                dve.drain()
                norm_all(dve, "fn", lambda c: XT[:, c, :], lambda c: HC[:, c, :], C_FFN, KC)

                def low_pair(p):
                    for s in range(2):
                        low(s, U_GU + 4 * p + 2 * s)

                def gate(p, m):
                    dve.wait_ge(S["silu_ready"], p + 1)
                    tt(HT[:, bass.ds(2 * p, 2), :], PS[2 * m + 1][:, :, 0:TOK], (NV, NR)[m][:, :, :], ALU.mult)\
                        .then_inc(S["gu_evac"], 1)

                low_pair(0)
                with dve.Fori(0, MF // 2 - 1) as i:
                    for m in range(2):
                        low_pair(2 * i + m + 1)
                        gate(2 * i + m, m)
                low_pair(MF - 1)
                gate(MF - 2, 0)
                low_half(0, U_DN, 0, 0)
                gate(MF - 1, 1)

                def down_add(r):
                    dve.wait_ge(S["down_done"], r + 1)
                    for m in range(4):
                        v = XT[:, 8 * r + 2 * m:8 * r + 2 * m + 2, :]
                        tt(v, PS[m][:, :, 0:TOK], v, ALU.add).then_inc(S["down_evac"], 1)

                for r in range(2):
                    n = DR * r
                    if r:
                        low_half(r, U_DN + 2 * n, 0, 0)
                        down_add(0)
                    low_half(r, U_DN + 2 * n, 1, 0)
                    with dve.Fori(0, DR // 2) as i:
                        for t in range(2):
                            low((r + t + 1) % 2, 4 * i + U_DN + 2 * (n + t + 1), 8 * i + 4 * t + 4)
                down_add(1)

        nc.all_engine_barrier(sems_to_clear=range(handles[0].num, handles[-1].num + 1))

    with nc.Block() as block:
        @block.sync
        def _(sp):
            sp.dma_start(T["y"], XT[:, :, :]).then_inc(S["y_out"], 16)
            sp.wait_ge(S["y_out"], 16)
    stack.close()


def arrays_of(v):
    def blocks(w, k, cols):
        n = w.shape[2] // cols
        return w.reshape(L, k, P, n, cols).transpose(0, 3, 2, 1, 4).reshape(L * n, P, k * cols)

    def feature_major(x):
        return x.reshape(x.shape[0], -1, P).transpose(2, 1, 0)

    def gain(g):
        return g.reshape(L, -1, P).transpose(0, 2, 1)

    pool = v["cache_cmp_kv"].shape[1]
    a = {"consts": constant_table()[0], "ties": tie_table()}
    x = np.concatenate([v["x_prompt"].reshape(SEQ, D_MODEL), v["x_sample"].reshape(SMP, D_MODEL)])
    a["x"] = feature_major(x)
    a["pages"] = v["page_table"].reshape(1, NB * NPG)
    a["w_in"] = blocks(v["w_in"][:, :, :NTILE * P], KC, 256)
    a["w_gates"] = v["w_in"][:, :, NTILE * P:].reshape(L, KC, P, 24).transpose(0, 2, 1, 3).reshape(L, P, KC * 24)
    a["w_glu"] = blocks(v["ssm_w_glu"], SC, 256)
    a["w_out"] = blocks(v["w_out"], KC, 256)
    gate, up = (blocks(v[n], KC, 256).reshape(L, MF, 1, P, KC * 256) for n in ("w_ffn_gate", "w_ffn_up"))
    a["w_gu"] = np.concatenate([gate, up], 2).reshape(L * 2 * MF, P, KC * 256)
    a["w_down"] = v["w_ffn_down"].reshape(L, 11, 4, P, 2, 1024).transpose(0, 4, 1, 3, 2, 5).reshape(L * 22, P, 4 * 1024)
    w1 = np.stack([v["cmp_w1_k"], v["cmp_w1_v"]], 1).reshape(L, 2, 32, HD, HD)
    a["cmp_w1"] = w1.transpose(0, 1, 3, 2, 4).reshape(L * 2, P, 32 * HD)
    a["cmp_w2"] = np.stack([v["cmp_w2_k"], v["cmp_w2_v"]], 2).reshape(L, P, 2 * HD)
    a["params"] = np.concatenate(
        [gain(v[n]) for n in ("norm_mix", "norm_ffn", "norm_ssm_out", "norm_attn_out")]
        + [gain(v["ssm_d"].reshape(L, -1))]
        + [v[n][:, :, None] for n in ("q_norm", "k_norm_slc", "k_norm_win", "k_norm_cmp", "cmp_b1_k", "cmp_b1_v")], 2)
    pair = lambda t: t.reshape(L, NPAIR, P).transpose(0, 2, 1)
    dt = np.broadcast_to(v["ssm_log_dt"][:, :, None], (L, 64, 64))
    a["lam"] = np.concatenate([pair(v["ssm_a_re"]), pair(v["ssm_a_im"]), pair(dt)], 2)
    b = np.zeros((L, 2, 64, 2, NPAIR, 2, 16), np.float32)
    c = np.zeros((L, 2, 64, NPAIR, 2, 2, 16), np.float32)
    for r, (nb, nc_) in enumerate([("ssm_b_re", "ssm_c_re"), ("ssm_b_im", "ssm_c_im")]):
        bb = v[nb].reshape(L, NPAIR, 2, 64, 16)
        cc = v[nc_].reshape(L, NPAIR, 2, 16, 64)
        for m in range(2):
            b[:, m, :, r, :, m, :] = bb[:, :, m].transpose(0, 2, 1, 3)
            c[:, m, :, :, r, m, :] = cc[:, :, m].transpose(0, 3, 1, 2)
    a["ssm_b"] = b.reshape(L, P, 2048)
    a["ssm_c"] = c.reshape(L, P, 2048)
    h0 = v["state_ssm"].reshape(L, NB, NPAIR, 2, 64, 2)
    a["ssm_h0"] = h0.transpose(0, 3, 4, 2, 5, 1).reshape(L, P, NPAIR * 2 * NB)
    cc = v["cache_cmp_kv"].reshape(L * pool, 8, 16, 2, 2, HD)
    a["cache_cmp"] = cc.transpose(0, 5, 3, 4, 2, 1).reshape(L * pool, P, 512)
    cs = v["cache_slc_kv"].reshape(L * pool, PAGE, 2, 2, HD)
    a["cache_slc_k"] = cs[:, :, :, 0].transpose(0, 3, 2, 1).reshape(L * pool, P, 256)
    a["cache_slc_v"] = cs[:, :, :, 1].reshape(L * pool, P, 256)
    w = v["state_win_kv"].reshape(L * NB, WIN, 2, 2, HD)
    a["win_k"] = w[:, :, :, 0].reshape(L * NB, 4, P, 2, HD).transpose(0, 4, 1, 3, 2).reshape(L * NB, P, 1024)
    a["win_v"] = w[:, :, :, 1].reshape(L * NB, 4, P, 2, HD).transpose(0, 2, 1, 3, 4).reshape(L * NB, P, 1024)
    a["win_rows"] = v["state_win_kv"].reshape(L, NB, WIN, 512)
    return {n: np.ascontiguousarray(t) for n, t in a.items()}


OUTS = {"y": (P, KC, TOK), "kv_new": (L, P, 12 * TOK), "win_kept": (L, NB, WIN - NT, 512),
        "win_zeros": (L, P, 1024), "ssm_last": (L, P, NPAIR * 2 * 9)}


def kernel(**inputs):
    import concourse.bacc as _bacc
    from concourse.bass_utils import run_bass_kernel_spmd as _run

    nc = _bacc.Bacc("TRN2", target_bir_lowering=False, num_devices=1)
    arrays = arrays_of({k: np.asarray(x) for k, x in inputs.items()})
    T = {n: nc.dram_tensor(f"in_{n}", a.shape, mybir.dt.from_np(a.dtype), kind="ExternalInput").ap()
         for n, a in arrays.items()}
    T |= {n: nc.dram_tensor(f"out_{n}", s, F32, kind="ExternalOutput").ap() for n, s in OUTS.items()}
    build(nc, T)
    got = _run(nc, [{f"in_{n}": a for n, a in arrays.items()}], core_ids=[0]).results[0]
    y = got["out_y"].transpose(2, 1, 0).reshape(TOK, D_MODEL)
    new = got["out_kv_new"].reshape(L, P, 3, 2, 2, TOK).transpose(2, 0, 5, 4, 3, 1)
    rows_p = new[:, :, :SEQ].reshape(3, L, 1, SEQ, 2, 2, HD)
    rows_s = new[:, :, SEQ:].reshape(3, L, NB, NT, 2, 2, HD)
    zeros = got["out_win_zeros"].reshape(L, 1, WIN - SEQ, 2, 2, HD)
    kept = got["out_win_kept"].reshape(L, NB, WIN - NT, 2, 2, HD)
    last = got["out_ssm_last"].reshape(L, 2, 64, NPAIR, 2, 9).transpose(0, 5, 3, 1, 2, 4).reshape(L, 9, 64, 64, 2)
    out = (y[:SEQ].reshape(1, SEQ, D_MODEL), y[SEQ:].reshape(NB, NT, D_MODEL), rows_p[0], rows_p[1],
           np.concatenate([zeros, rows_p[2]], 2), last[:, :1], rows_s[0], rows_s[1],
           np.concatenate([kept, rows_s[2]], 2), last[:, 1:])
    return tuple(np.ascontiguousarray(o) for o in out)
```
